# Optimizing a Trainium2 kernel written in Bass

```python
import jax, jax.numpy as jnp
from jax import lax
import numpy as np

D_MODEL = 2048
BATCH = 1
SEQ = 128
DEPTH = 1
DEC_BATCH = 1
DEC_SEQ = 256
PAST_LEN = 128

GRID_W = 64
MIX_W = D_MODEL
ML_HEADS = 4
ML_W = MIX_W // 2
ML_DH = ML_W // ML_HEADS
SSM_W = MIX_W - ML_W
SSM_P = 64
SSM_HEADS = SSM_W // SSM_P
SSM_N = 128
SSM_G = 2
SSM_R = SSM_HEADS // SSM_G
CONV_K = 5
CONV_CH = SSM_W + 2 * SSM_G * SSM_N
D_FF = 256 * ((8 * D_MODEL // 3 + 255) // 256)
CHUNK = 128
N_MOD = 9
EPS = 1e-6
COL_SIZES = (ML_W, ML_W, ML_W, ML_W, 2 * ML_HEADS, 2 * ML_HEADS, SSM_W, CONV_CH, 2 * SSM_HEADS)
COL_SPLITS = tuple(sum(COL_SIZES[:i + 1]) for i in range(len(COL_SIZES) - 1))
IN_W = sum(COL_SIZES)

kernel_name = "hybrid_mlstm_ssd_diffusion_step"

def rmsnorm(x, g):
    x32 = x.astype(jnp.float32)
    y = x32 * lax.rsqrt(jnp.mean(x32 * x32, axis=-1, keepdims=True) + EPS)
    return (y * g.astype(jnp.float32)).astype(x.dtype)

def flip(a):
    return jnp.flip(a, axis=1)

def to_chunks(a):
    b, l = a.shape[:2]
    return jnp.moveaxis(a.reshape((b, l // CHUNK, CHUNK) + a.shape[2:]), 1, 0)

def from_chunks(a):
    a = jnp.moveaxis(a, 0, 1)
    return a.reshape((a.shape[0], a.shape[1] * a.shape[2]) + a.shape[3:])

def mlstm_direction(q, k, v, log_i, log_f, C0, n0, m0):
    tri = jnp.tril(jnp.ones((CHUNK, CHUNK), dtype=bool))

    def body(carry, inp):
        C, n, m = carry
        qc, kc, vc, li, lf = inp
        b = jnp.cumsum(lf, axis=1)
        log_d = b[:, :, None, :] - b[:, None, :, :] + li[:, None, :, :]
        log_d = jnp.where(tri[None, :, :, None], log_d, -jnp.inf)
        m_inter = b + m[:, None, :]
        m_t = jnp.maximum(m_inter, jnp.max(log_d, axis=2))
        scores = jnp.einsum('bthd,bshd->btsh', qc, kc) * jnp.exp(log_d - m_t[:, :, None, :])
        inter = jnp.exp(m_inter - m_t)
        num = (jnp.einsum('btsh,bshv->bthv', scores, vc)
               + inter[..., None] * jnp.einsum('bthk,bhkv->bthv', qc, C))
        den = jnp.sum(scores, axis=2) + inter * jnp.einsum('bthk,bhk->bth', qc, n)
        h = num / jnp.maximum(jnp.abs(den), jnp.exp(-m_t))[..., None]
        log_w = b[:, -1:, :] - b + li
        m_end_inter = b[:, -1, :] + m
        m_new = jnp.maximum(m_end_inter, jnp.max(log_w, axis=1))
        w = jnp.exp(log_w - m_new[:, None, :])
        decay = jnp.exp(m_end_inter - m_new)
        C_new = decay[..., None, None] * C + jnp.einsum('bshk,bshv->bhkv', w[..., None] * kc, vc)
        n_new = decay[..., None] * n + jnp.einsum('bsh,bshk->bhk', w, kc)
        return (C_new, n_new, m_new), h

    xs = (to_chunks(q), to_chunks(k), to_chunks(v), to_chunks(log_i), to_chunks(log_f))
    (C, n, m), h = lax.scan(body, (C0, n0, m0), xs)
    return from_chunks(h), C, n, m

def ssd_direction(x, bm, cm, dt, A, S0):
    tri = jnp.tril(jnp.ones((CHUNK, CHUNK), dtype=bool))

    def body(S, inp):
        xc, bc, cc, dtc = inp
        a = jnp.cumsum(dtc * A, axis=1)
        seg = a[:, :, None] - a[:, None]
        decay = jnp.exp(jnp.where(tri[None, :, :, None, None], seg, -jnp.inf))
        cb = jnp.einsum('btgn,bsgn->btsg', cc, bc)
        wts = cb[..., None] * decay * dtc[:, None]
        y = (jnp.einsum('btsgr,bsgrp->btgrp', wts, xc)
             + jnp.exp(a)[..., None] * jnp.einsum('btgn,bgrpn->btgrp', cc, S))
        to_end = jnp.exp(a[:, -1:] - a) * dtc
        S_new = (jnp.exp(a[:, -1])[..., None, None] * S
                 + jnp.einsum('bsgrp,bsgn->bgrpn', to_end[..., None] * xc, bc))
        return S_new, y

    S, y = lax.scan(body, S0, (to_chunks(x), to_chunks(bm), to_chunks(cm), to_chunks(dt)))
    return from_chunks(y), S

def dwconv(u, w, bias, n_seg):
    b, l, ch = u.shape
    seg = u.reshape(b * n_seg, l // n_seg, ch)
    out = lax.conv_general_dilated(seg, w[:, None, :].astype(u.dtype), window_strides=(1,),
                                   padding=[(CONV_K // 2, CONV_K // 2)],
                                   dimension_numbers=('NWC', 'WIO', 'NWC'), feature_group_count=ch)
    return (out + bias.astype(u.dtype)).reshape(b, l, ch)

def hybrid_mixer(h, p, ml_state, ssm_state, n_seg):
    f32 = jnp.float32
    bsz, l, _ = h.shape
    proj = h @ p['w_in']
    q, k, v, o_pre, ig, fg, z, xbc, dt_raw = jnp.split(proj, COL_SPLITS, axis=-1)
    heads = lambda a: a.reshape(bsz, l, ML_HEADS, ML_DH).astype(f32)
    q, k, v = heads(q), heads(k) * (ML_DH ** -0.5), heads(v)
    gb = p['gate_bias'].astype(f32)
    log_i = ig.reshape(bsz, l, 2, ML_HEADS).astype(f32) + gb[0]
    log_f = jax.nn.log_sigmoid(fg.reshape(bsz, l, 2, ML_HEADS).astype(f32) + gb[1])
    C0, n0, m0 = (s.astype(f32) for s in ml_state)
    h_f, Cf, nf, mf = mlstm_direction(q, k, v, log_i[:, :, 0], log_f[:, :, 0], C0[:, 0], n0[:, 0], m0[:, 0])
    h_b, Cb, nb, mb = mlstm_direction(flip(q), flip(k), flip(v), flip(log_i[:, :, 1]), flip(log_f[:, :, 1]),
                                      C0[:, 1], n0[:, 1], m0[:, 1])
    h_ml = h_f + flip(h_b)
    mu = jnp.mean(h_ml, axis=-1, keepdims=True)
    var = jnp.mean(jnp.square(h_ml - mu), axis=-1, keepdims=True)
    h_ml = (h_ml - mu) * lax.rsqrt(var + EPS) * p['ml_norm_g'].astype(f32).reshape(ML_HEADS, ML_DH)
    h_ml = jax.nn.sigmoid(o_pre.astype(f32)) * h_ml.reshape(bsz, l, ML_W)
    xbc = jax.nn.silu(dwconv(xbc, p['conv_w'], p['conv_b'], n_seg).astype(f32))
    xs, bm, cm = jnp.split(xbc, (SSM_W, SSM_W + SSM_G * SSM_N), axis=-1)
    xs = xs.reshape(bsz, l, SSM_G, SSM_R, SSM_P)
    bm = bm.reshape(bsz, l, SSM_G, SSM_N)
    cm = cm.reshape(bsz, l, SSM_G, SSM_N)
    dt = jax.nn.softplus(dt_raw.reshape(bsz, l, 2, SSM_HEADS).astype(f32) + p['dt_bias'].astype(f32))
    dt = dt.reshape(bsz, l, 2, SSM_G, SSM_R)
    A = (-jnp.exp(p['a_log'].astype(f32))).reshape(2, SSM_G, SSM_R)
    S0 = ssm_state.astype(f32).reshape(bsz, 2, SSM_G, SSM_R, SSM_P, SSM_N)
    y_f, Sf = ssd_direction(xs, bm, cm, dt[:, :, 0], A[0], S0[:, 0])
    y_b, Sb = ssd_direction(flip(xs), flip(bm), flip(cm), flip(dt[:, :, 1]), A[1], S0[:, 1])
    y = y_f + flip(y_b) + p['d_skip'].astype(f32).reshape(SSM_G, SSM_R)[..., None] * xs
    y = rmsnorm(y.reshape(bsz, l, SSM_W) * jax.nn.silu(z.astype(f32)), p['ssm_norm_g'])
    out = jnp.concatenate([h_ml, y], axis=-1).astype(h.dtype) @ p['w_out']
    new_ml = (jnp.stack([Cf, Cb], axis=1), jnp.stack([nf, nb], axis=1), jnp.stack([mf, mb], axis=1))
    new_ssm = jnp.stack([Sf, Sb], axis=1).reshape(bsz, 2, SSM_HEADS, SSM_P, SSM_N)
    return out, new_ml, new_ssm

def swiglu(h, wg, wu, wd):
    return (jax.nn.silu(h @ wg) * (h @ wu)) @ wd

def adaln_in(x, g, shift, scale):
    return rmsnorm(x, g) * (1 + scale) + shift

def trunk_layer(x, mod, p, ml_state, ssm_state, n_seg):
    mod = mod.astype(x.dtype)
    sh = lambda j: mod[:, j, None, :]
    g = p['norm_g']
    h = adaln_in(x, g[0], sh(0), sh(1))
    x = x + 0.5 * sh(2) * rmsnorm(swiglu(h, p['w_gate'][0], p['w_up'][0], p['w_down'][0]), g[1])
    h = adaln_in(x, g[2], sh(3), sh(4))
    mix, new_ml, new_ssm = hybrid_mixer(h, p, ml_state, ssm_state, n_seg)
    x = x + sh(5) * rmsnorm(mix, g[3])
    h = adaln_in(x, g[4], sh(6), sh(7))
    x = x + 0.5 * sh(8) * rmsnorm(swiglu(h, p['w_gate'][1], p['w_up'][1], p['w_down'][1]), g[5])
    return x, new_ml, new_ssm

def setup_inputs(seed: int = 0) -> dict:
    key = jax.random.key(seed)
    ks = jax.random.split(key, 26)
    nrm = lambda k, shape, s: jax.random.normal(k, shape, jnp.float32) * s
    dt0 = jnp.exp(jax.random.uniform(ks[13], (DEPTH, 2, SSM_HEADS), jnp.float32, np.log(1e-3), np.log(1e-1)))
    gate_bias = nrm(ks[12], (DEPTH, 2, 2, ML_HEADS), 0.1)
    gate_bias = gate_bias.at[:, 1].add(jnp.linspace(3.0, 6.0, ML_HEADS, dtype=jnp.float32))
    return {
        'x_prompt': nrm(ks[0], (BATCH, SEQ, D_MODEL), 1.0),
        'x_sample': nrm(ks[1], (DEC_BATCH, DEC_SEQ, D_MODEL), 1.0),
        'state_mlstm_C': nrm(ks[2], (DEC_BATCH, DEPTH, 2, ML_HEADS, ML_DH, ML_DH), 0.5),
        'state_mlstm_n': nrm(ks[3], (DEC_BATCH, DEPTH, 2, ML_HEADS, ML_DH), 0.5),
        'state_mlstm_m': nrm(ks[4], (DEC_BATCH, DEPTH, 2, ML_HEADS), 1.0),
        'state_ssm': nrm(ks[5], (DEC_BATCH, DEPTH, 2, SSM_HEADS, SSM_P, SSM_N), 0.5),
        'c': nrm(ks[6], (DEC_BATCH, D_MODEL), 1.0),
        'c_ctx': nrm(ks[7], (D_MODEL,), 1.0),
        'w_ada': nrm(ks[8], (DEPTH, D_MODEL, N_MOD * D_MODEL), D_MODEL ** -0.5),
        'b_ada': nrm(ks[9], (DEPTH, N_MOD * D_MODEL), 0.02),
        'norm_g': 1.0 + nrm(ks[10], (DEPTH, 6, D_MODEL), 0.05),
        'w_in': nrm(ks[11], (DEPTH, D_MODEL, IN_W), D_MODEL ** -0.5),
        'gate_bias': gate_bias,
        'dt_bias': dt0 + jnp.log(-jnp.expm1(-dt0)),
        'a_log': jnp.log(jax.random.uniform(ks[14], (DEPTH, 2, SSM_HEADS), jnp.float32, 1.0, 16.0)),
        'd_skip': 1.0 + nrm(ks[15], (DEPTH, SSM_HEADS), 0.1),
        'conv_w': nrm(ks[16], (DEPTH, CONV_K, CONV_CH), CONV_K ** -0.5),
        'conv_b': nrm(ks[17], (DEPTH, CONV_CH), 0.02),
        'ml_norm_g': 1.0 + nrm(ks[18], (DEPTH, ML_W), 0.05),
        'ssm_norm_g': 1.0 + nrm(ks[19], (DEPTH, SSM_W), 0.05),
        'w_out': nrm(ks[20], (DEPTH, MIX_W, D_MODEL), MIX_W ** -0.5),
        'ffn_w_gate': nrm(ks[21], (DEPTH, 2, D_MODEL, D_FF), D_MODEL ** -0.5),
        'ffn_w_up': nrm(ks[22], (DEPTH, 2, D_MODEL, D_FF), D_MODEL ** -0.5),
        'ffn_w_down': nrm(ks[23], (DEPTH, 2, D_FF, D_MODEL), D_FF ** -0.5),
    }

def reference(x_prompt, x_sample, state_mlstm_C, state_mlstm_n, state_mlstm_m, state_ssm, c, c_ctx,
              w_ada, b_ada, norm_g, w_in, gate_bias, dt_bias, a_log, d_skip, conv_w, conv_b,
              ml_norm_g, ssm_norm_g, w_out, ffn_w_gate, ffn_w_up, ffn_w_down):
    f32 = jnp.float32
    bp = x_prompt.shape[0]
    bd = x_sample.shape[0]
    rows = x_sample.shape[1] // GRID_W
    y_p, y_s = x_prompt, x_sample
    out_C, out_n, out_m, out_S = [], [], [], []
    for l in range(DEPTH):
        p = {'norm_g': norm_g[l], 'w_in': w_in[l], 'gate_bias': gate_bias[l], 'dt_bias': dt_bias[l],
             'a_log': a_log[l], 'd_skip': d_skip[l], 'conv_w': conv_w[l], 'conv_b': conv_b[l],
             'ml_norm_g': ml_norm_g[l], 'ssm_norm_g': ssm_norm_g[l], 'w_out': w_out[l],
             'w_gate': ffn_w_gate[l], 'w_up': ffn_w_up[l], 'w_down': ffn_w_down[l]}
        mod_ctx = (jax.nn.silu(c_ctx)[None] @ w_ada[l] + b_ada[l]).reshape(1, N_MOD, D_MODEL)
        mod_lat = (jax.nn.silu(c) @ w_ada[l] + b_ada[l]).reshape(bd, N_MOD, D_MODEL)
        zero_ml = (jnp.zeros((bp, 2, ML_HEADS, ML_DH, ML_DH), f32), jnp.zeros((bp, 2, ML_HEADS, ML_DH), f32),
                   jnp.zeros((bp, 2, ML_HEADS), f32))
        zero_ssm = jnp.zeros((bp, 2, SSM_HEADS, SSM_P, SSM_N), f32)
        y_p, (Cn, nn_, mn), Sn = trunk_layer(y_p, mod_ctx, p, zero_ml, zero_ssm, 1)
        lat_ml = (state_mlstm_C[:, l], state_mlstm_n[:, l], state_mlstm_m[:, l])
        y_s, _, _ = trunk_layer(y_s, mod_lat, p, lat_ml, state_ssm[:, l], rows)
        out_C.append(Cn)
        out_n.append(nn_)
        out_m.append(mn)
        out_S.append(Sn)
    new_mlstm_C = jnp.stack(out_C, axis=1)
    new_mlstm_n = jnp.stack(out_n, axis=1)
    new_mlstm_m = jnp.stack(out_m, axis=1)
    new_ssm = jnp.stack(out_S, axis=1)
    return (y_p, y_s, new_mlstm_C, new_mlstm_n, new_mlstm_m, new_ssm)


_drawn_inputs = setup_inputs


def setup_inputs(seed=0):
    import zlib

    import numpy as np

    out = dict(_drawn_inputs(seed))
    spreads = {}
    factors = {}
    for name, (base, spread) in spreads.items():
        noise = np.random.default_rng([zlib.crc32(name.encode()), seed]).standard_normal(out[name].shape)
        drawn = base * np.exp(spread * noise) if base else spread * noise
        out[name] = __import__('jax').numpy.asarray(drawn.astype(out[name].dtype))
    for name, factor in factors.items():
        out[name] = (out[name] * factor).astype(out[name].dtype)
    return out
```

```python
from contextlib import ExitStack

import concourse.bass as bass
from concourse import mybir

ALU = mybir.AluOpType
ACT = mybir.ActivationFunctionType
F32 = mybir.dt.float32
F32R = mybir.dt.float32r

P = 128
D = 2048
KT = D // P
TOK_P, TOK_S = 128, 256
TOK = TOK_P + TOK_S
NCH = TOK // P
GROUPS = ((0, TOK_P), (TOK_P, TOK))
D_FF = 256 * ((8 * D // 3 + 255) // 256)
HEADS = 4
ML_W = D // 2
DH = ML_W // HEADS
SSM_W = D - ML_W
SSM_P = 64
SSM_H = SSM_W // SSM_P
SSM_N = 128
SSM_G = 2
GRP_W = SSM_W // SSM_G
CONV_K = 5
GRID_W = 64
N_MOD = 9
EPS = 1e-6
COL_Q, COL_K, COL_V, COL_O = 0, ML_W, 2 * ML_W, 3 * ML_W
COL_IG = 4 * ML_W
COL_FG = COL_IG + 2 * HEADS
COL_Z = COL_FG + 2 * HEADS
COL_XBC = COL_Z + SSM_W
COL_DT = COL_XBC + SSM_W + 2 * SSM_G * SSM_N
XBC_T = (SSM_W + 2 * SSM_G * SSM_N) // P

PK, PC = 4, 256
PW = PK * PC
NR, NS, AHEAD = 8, 4, 3
U = KT // PK
FFN_IT = D_FF // 512
DOWN = D // PC
FFN_PER = 4 * U + DOWN
FFN_LEN = FFN_IT * FFN_PER
MIX0 = FFN_LEN
P_GATES = MIX0
P_XBC = P_GATES + U
P_HEADS = P_XBC + (XBC_T // 2) * U
PAIR = 2 * 5 * U
P_OUT = P_HEADS + (HEADS // 2) * PAIR
FFN2 = P_OUT + (D // PC) * U
TOTAL = FFN2 + FFN_LEN

ADA_R = 4
ADA_T = N_MOD * KT
ADA_PER = 5
ADA_FIRST = ADA_T // 2 - ADA_PER * FFN_IT

ROW_ML = (0, 64)
ROW_SS = (32, 96)
SCAN = ((0, 64), (64, 128))
MASKED = -1e30

STEPS = ((0, 0), (0, 1), (1, 0), (2, 1), (2, 0), (1, 1))
N_STATE = 4
FIRST_VISIT = (0, 2, 3)

XBC_ORDER = (4, 5, 0, 1, 2, 3)
UNIT_B, UNIT_C = 0, 1
TOK_UNITS = (0, 2, 3, 4, 5)
GATE_AT = {1: 0, 5: 1, 9: 2, 12: 3, 17: 4}

PAIR_ORDER = [(col, hh, q) for col, hh in (
    (COL_Q, 0), (COL_K, 0), (COL_V, 0), (COL_Q, 1), (COL_K, 1), (COL_V, 1), (COL_O, 0), (COL_O, 1), (COL_Z, 0), (COL_Z, 1))
    for q in range(U)]
CORE_AT = {12: ("kv", 0), 13: ("start", 0), 14: ("a", 0, 0), 15: ("b", 0, 0), 16: ("c", 0, 0, "a", 0, 1), 17: ("b", 0, 1),
           18: ("c", 0, 1, "a", 0, 2), 19: ("b", 0, 2), 20: ("c", 0, 2, "a", 0, 3), 21: ("b", 0, 3),
           22: ("c", 0, 3, "a", 0, 4), 23: ("b", 0, 4), 24: ("a", 0, 5), 25: ("b", 0, 5), 26: ("kv", 1), 27: ("end", 0),
           28: ("start", 1), 29: ("a", 1, 0), 30: ("b", 1, 0), 31: ("c", 1, 0, "a", 1, 1), 32: ("b", 1, 1),
           33: ("c", 1, 1, "a", 1, 2), 34: ("b", 1, 2), 35: ("c", 1, 2, "a", 1, 3), 36: ("b", 1, 3),
           37: ("c", 1, 3, "a", 1, 4), 38: ("b", 1, 4), 39: ("a", 1, 5, "b", 1, 5, "end", 1)}


def core_tasks(j):
    out, rest = [], list(CORE_AT.get(j, ()))
    while rest:
        kind, hh = rest[:2]
        n = rest[2] if kind in "abc" else None
        rest = rest[3:] if kind in "abc" else rest[2:]
        out.append((kind, hh, n))
    return out


def ada_upto(j, length):
    return -(-U * ADA_PER * (j + 1) // length)


V_NORM, V_CONVB, V_MLG, V_SSG = 0, 96, 108, 116
V_CONVW, V_BADA, V_CCTX, V_C = 128, 256, 400, 416
VEC_ROWS = ((124, 0), (60, 128), (128, 256), (48, 384))
N_VEC = 9
N_COLS = 11
LINKS_PAIR = 2 * (6 * 4 + 3)


def at(const, i, per):
    return const if i is None else i * per + const


class Tally:

    def __init__(self, eng, sem):
        self.eng, self.sem, self.n, self.i, self.per = eng, sem, 0, None, 0

    def enter(self, i, per):
        self.start, self.i, self.per = self.n, i, per

    def leave(self, times):
        assert self.n - self.start == self.per, (self.n - self.start, self.per)
        self.n, self.i = self.start + times * self.per, None

    def link(self, ins):
        ins.then_inc(self.sem, 1)
        self.n += 1
        self.eng.wait_ge(self.sem, at(self.n, self.i, self.per))


def hybrid_step(nc, A):
    with ExitStack() as ctx:
        def sb(name, shape, dt=F32):
            return ctx.enter_context(nc.sbuf_tensor(name, shape, dt))

        def sem(name):
            return ctx.enter_context(nc.semaphore(name))

        xT = sb("xT", [P, KT, TOK])
        xn_hi = sb("xn_hi", [P, KT, TOK], F32R)
        xn_lo = sb("xn_lo", [P, KT, TOK], F32R)
        y = sb("y", [P, KT, TOK])
        hid_hi = sb("hid_hi", [P, 4, TOK], F32R)
        hid_lo = sb("hid_lo", [P, 4, TOK], F32R)
        w_raw = sb("w_raw", [P, NR, PW])
        w_hi = sb("w_hi", [P, NS, PW], F32R)
        w_lo = sb("w_lo", [P, NS, PW], F32R)
        idn = sb("idn", [P, P])
        ones = sb("ones", [P, P])
        maskneg = sb("maskneg", [P, 2, P])
        vecT = sb("vecT", [P, 432])
        modT = sb("modT", [P, ADA_T, 2])
        cT = sb("cT", [P, KT, 2])
        coefA = sb("coefA", [P, KT, 2])
        coefG = sb("coefG", [P, KT, 2])
        eps = sb("eps", [P, 1])
        gcol = sb("gcol", [P, 16])
        dsk = sb("dsk", [P, SSM_H])
        dbc = sb("dbc", [P, P])
        small = sb("small", [P, 32])
        stats = sb("stats", [P, NCH, 6])
        AM = sb("AM", [P, 43 * 256])
        AX = xT[:, :, :].rearrange("p k t -> p (k t)")
        psum = [ctx.enter_context(nc.psum_tensor(f"bank{b}", [P, 512], F32)) for b in range(8)]

        def am(kb, n):
            return AM[:, int(kb * 256):int(kb * 256) + n]

        def ax(kb, n):
            return AX[:, int(kb * 256):int(kb * 256) + n]

        ada_raw = am(0, ADA_R * PW).rearrange("p (s w) -> p s w", s=ADA_R)
        sq = am(16, 2 * TOK).rearrange("p (s t) -> p s t", s=2)
        std = am(19, TOK)
        xt = am(20.5, 2 * TOK).rearrange("p (s t) -> p s t", s=2)
        hn = am(23.5, 2 * TOK).rearrange("p (s t) -> p s t", s=2)
        sg = am(27, 2 * TOK).rearrange("p (s t) -> p s t", s=2)
        hidf = am(30, 2 * TOK).rearrange("p (s t) -> p s t", s=2)
        x_tok = y[:, :, :].rearrange("p k t -> p (k t)").rearrange("p (c n) -> p c n", c=NCH)
        vec_rows = am(33, 4 * P).rearrange("p (s n) -> p s n", s=4)
        out_tok = am(0, NCH * D).rearrange("p (c n) -> p c n", c=NCH)
        gw_small = am(33, KT * 48).rearrange("p (k n) -> p k n", k=KT)
        gw_pad = am(0, KT * PC).rearrange("p (k n) -> p k n", k=KT)
        rows = [ax(1.5 * r, TOK) for r in range(13)]
        r_u, r_e, r_lw, r_d, r_q, r_sp, r_cs, r_Q, r_E, r_W, r_T4, r_li, r_t = rows
        r_P = ax(22.5, TOK)
        cols = am(15.25, 4 * NCH * P).rearrange("p (q c r) -> p q c r", q=4, c=NCH)
        C_Q, C_E, C_W, C_T = range(4)
        xs_tok = am(0, NCH * SSM_W).rearrange("p (c n) -> p c n", c=NCH)
        bm_tok = am(12, NCH * SSM_G * SSM_N).rearrange("p (c n) -> p c n", c=NCH)
        bcT = am(21.25, 4 * TOK).rearrange("p (s t) -> p s t", s=4)
        cv = am(27.25, 2 * TOK).rearrange("p (s t) -> p s t", s=2)
        cvs = am(30.25, 2 * TOK).rearrange("p (s t) -> p s t", s=2)
        ST = am(33.5, 2 * SSM_W).rearrange("p (d n) -> p d n", d=2)
        seg = ax(0, 8 * P).rearrange("p (h t) -> p h t", h=8)
        xdt = ax(4, GRP_W)
        xte = ax(6, GRP_W)
        cbs = ax(8, P)
        stt_ = ax(8.5, GRP_W)
        s_out = ax(10.5, GRP_W)
        s_raw = ax(12.5, 2 * 8 * P).rearrange("p (d j n) -> p d j n", d=2, j=8)
        ytmp = ax(20.5, GRP_W)
        yacc = y[:, 0:KT // 2, :].rearrange("p k t -> p (k t)").rearrange("p (c n) -> p c n", c=NCH)
        VW = DH + 1
        def head_set(v):
            a = v.rearrange("p n -> p n")
            qT = a[:, 0:2 * TOK].rearrange("p (s t) -> p s t", s=2)
            kT = a[:, 2 * TOK:4 * TOK].rearrange("p (s t) -> p s t", s=2)
            vT = a[:, 4 * TOK:6 * TOK].rearrange("p (s t) -> p s t", s=2)
            ktok = a[:, 6 * TOK:8 * TOK].rearrange("p (c n) -> p c n", c=NCH)
            va = a[:, 8 * TOK:8 * TOK + NCH * VW].rearrange("p (c n) -> p c n", c=NCH)
            return qT, kT, vT, ktok, va
        HS_N = 8 * TOK + NCH * VW
        hset = [head_set(am(0, HS_N)), head_set(ax(0, HS_N))]
        cst = [am(21.25 + 4.25 * s, 2 * 2 * VW).rearrange("p (d k n) -> p d k n", d=2, k=2) for s in range(2)]
        mrow = am(29.75, 2 * TOK).rearrange("p (d t) -> p d t", d=2)
        ex = am(32.75, P)
        sT = am(33.25, P)
        ti = am(33.75, VW)
        num = am(34.85, VW)
        wk = am(35.95, DH)
        hacc = am(37, NCH * DH).rearrange("p (c n) -> p c n", c=NCH)
        c_out = am(40, 2 * VW).rearrange("p (k n) -> p k n", k=2)
        sigo = [ax(15.2 + 3 * s, 2 * TOK).rearrange("p (k t) -> p k t", k=2) for s in range(2)]

        x_wait = nc.dram_tensor("x_wait", (P, KT * TOK), F32).ap()

        raw_loaded = [sem(f"raw_loaded{s}") for s in range(NR)]
        ada_loaded = [sem(f"ada_loaded{s}") for s in range(ADA_R)]
        w_hi_ready, w_lo_dve, w_lo_pool, pe_piece = sem("w_hi_ready"), sem("w_lo_dve"), sem("w_lo_pool"), sem("pe_piece")
        ada_used, ada_evac = sem("ada_used"), sem("ada_evac")
        const_ready, pool_step, dve_step = sem("const_ready"), sem("pool_step"), sem("dve_step")
        x_loaded, vec_loaded, cols_loaded, gw_loaded = sem("x_loaded"), sem("vec_loaded"), sem("cols_loaded"), sem("gw_loaded")
        vec_tr, vec_ready, c_ready = sem("vec_tr"), sem("vec_ready"), sem("c_ready")
        xt_tr, xT_ready = sem("xt_tr"), sem("xT_ready")
        sq_ready, ss_mm, std_ready, xt_done = sem("sq_ready"), sem("ss_mm"), sem("std_ready"), sem("xt_done")
        hn_ready, xn_hi_ready, xn_lo_ready = sem("hn_ready"), sem("xn_hi_ready"), sem("xn_lo_ready")
        silu_ready, hid_ready = sem("silu_ready"), sem("hid_ready")
        hid_hi_ready, hid_lo_ready = sem("hid_hi_ready"), sem("hid_lo_ready")
        y_zeroed, y_done, u_ready, x_updated = sem("y_zeroed"), sem("y_done"), sem("u_ready"), sem("x_updated")
        out_tr, out_ready_dve, out_ready_act, out_stored = sem("out_tr"), sem("out_ready_dve"), sem("out_ready_act"), sem("out_stored")
        x_spilled, x_back = sem("x_spilled"), sem("x_back")
        gw_ready, gate_read, dve_row, act_row, gates_done = sem("gw_ready"), sem("gate_read"), sem("dve_row"), sem("act_row"), sem("gates_done")
        cols_tr, cols_ready, dec_mm, dec_ready, m_stored = sem("cols_tr"), sem("cols_ready"), sem("dec_mm"), sem("dec_ready"), sem("m_stored")
        conv_done, conv_silu, conv_tr, tok_ready = sem("conv_done"), sem("conv_silu"), sem("conv_tr"), sem("tok_ready")
        sr_loaded, st_tr, st_ready = sem("sr_loaded"), sem("st_tr"), sem("st_ready")
        ss_bc, ss_cb, ss_seg, ss_exp, ss_x = sem("ss_bc"), sem("ss_cb"), sem("ss_seg"), sem("ss_exp"), sem("ss_x")
        ss_wd, ss_wp, ss_y, ss_int, ss_yacc = sem("ss_wd"), sem("ss_wp"), sem("ss_y"), sem("ss_int"), sem("ss_yacc")
        ss_tmp, ss_ypool, ss_stm, ss_state, s_stored = sem("ss_tmp"), sem("ss_ypool"), sem("ss_stm"), sem("ss_state"), sem("s_stored")
        yt_tr, yt_ready = sem("yt_tr"), sem("yt_ready")
        qkv_ready, og_ready, z_silu, z_done = sem("qkv_ready"), sem("og_ready"), sem("z_silu"), sem("z_done")
        kv_tr, kv_tok, row_ready, m_bc, v_ones = sem("kv_tr"), sem("kv_tok"), sem("row_ready"), sem("m_bc"), sem("v_ones")
        c_loaded = [sem(f"c_loaded{s}") for s in range(2)]
        m_seg, m_exp, m_qk, m_s, m_num, m_int = sem("m_seg"), sem("m_exp"), sem("m_qk"), sem("m_s"), sem("m_num"), sem("m_int")
        m_ti, m_h, m_wk, m_upd, m_c, m_cstored = sem("m_ti"), sem("m_h"), sem("m_wk"), sem("m_upd"), sem("m_c"), sem("m_cstored")
        h_var, h_std, h_norm, h_tr, mix_ready, ms_scaled = sem("h_var"), sem("h_std"), sem("h_norm"), sem("h_tr"), sem("mix_ready"), sem("ms_scaled")

        def by_tile(w):
            return w.rearrange("(k p) n -> p k n", p=P)

        w_in = by_tile(A["w_in"][0])
        w_out = by_tile(A["w_out"][0])
        w_ada = by_tile(A["w_ada"][0])
        w_gate = [by_tile(A["ffn_w_gate"][0, n]) for n in range(2)]
        w_up = [by_tile(A["ffn_w_up"][0, n]) for n in range(2)]
        w_down = [by_tile(A["ffn_w_down"][0, n]) for n in range(2)]

        SQ, total = {}, 0
        for name, count in (("x0", KT), ("y1", KT), ("x1", KT), ("ssm", KT // 2), ("y2", KT), ("x2", KT), ("y3", KT)):
            SQ[name] = (total, count)
            total += count
        SQ_ORDER = list(SQ)
        SSM_STEPS = [(g, c, d, n) for g in range(SSM_G) for n, (c, d) in enumerate(STEPS)]

        def ssm_before(n):
            return (sum(1 for x in SSM_STEPS[:n] if x[1]), sum(1 for x in SSM_STEPS[:n] if x[3] < N_STATE))

        def ffn_first(n):
            return FFN2 if n else 0

        def ffn_loop(n):
            return ffn_first(n) + 4 * U

        PARTS = (("g", 0, 0, 0), ("d", 0, U, None), ("u", 0, U + DOWN, U), ("g", 1, 2 * U + DOWN, 2 * U), ("u", 1, 3 * U + DOWN, 3 * U))

        with nc.Block() as block:

            @block.sync
            def _(sp):
                def load(p, src, i=None, per=0):
                    if p >= NR:
                        sp.wait_ge(w_lo_pool if p % 2 else w_lo_dve, at((p - NR) // 2 + 1, i, per // 2))
                    dst = w_raw[:, p % NR, :].rearrange("p (k n) -> p k n", k=PK)
                    sp.dma_start(dst, src).then_inc(raw_loaded[p % NR], 16)

                def load_ada(a, unit, q, i=None):
                    if a >= ADA_R:
                        sp.wait_ge(ada_used, at(a - ADA_R + 1, i, U * ADA_PER))
                    dst = ada_raw[:, a % ADA_R, :].rearrange("p (k n) -> p k n", k=PK)
                    src = w_ada[:, PK * q:PK * q + PK, bass.ds(unit * PC, PC)]
                    sp.dma_start(dst, src).then_inc(ada_loaded[a % ADA_R], 16)

                def block_of(w, c0, q):
                    return w[:, PK * q:PK * q + PK, bass.ds(c0, PC)]

                def ffn_step(n, i):
                    first = i is None
                    base, per = (ffn_first(n), 0) if first else (ffn_loop(n), FFN_PER)
                    f0 = 0 if first else i * 512 + 512
                    length = FFN_PER - (DOWN if first else 0)
                    a0 = U * ADA_FIRST + (0 if first else U * ADA_PER)
                    u0 = ADA_FIRST if first else i * ADA_PER + (ADA_FIRST + ADA_PER)
                    done = 0
                    for kind, s, j_loop, j_first in PARTS:
                        j0 = j_first if first else j_loop
                        if j0 is None:
                            continue
                        for q in range(DOWN if kind == "d" else U):
                            if kind == "d":
                                src = w_down[n][:, bass.ds(i * PK, PK), PC * q:PC * q + PC]
                            else:
                                src = block_of(w_gate[n] if kind == "g" else w_up[n], f0 + PC * s, q)
                            load(base + j0 + q, src, i, per)
                            while n == 0 and done < ada_upto(j0 + q, length):
                                load_ada(a0 + done, u0 + done // U, done % U, i)
                                done += 1

                def ffn(n):
                    ffn_step(n, None)
                    with sp.Fori(0, FFN_IT - 1) as i:
                        ffn_step(n, i)
                    for j in range(DOWN):
                        load(ffn_first(n) + FFN_LEN - DOWN + j, w_down[n][:, D_FF // P - PK:, PC * j:PC * j + PC])

                for q in range(U):
                    load_ada(q, 0, q)
                sp.dma_start(x_tok[:, 0, :], A["x_prompt"][0]).then_inc(x_loaded, 16)
                sp.dma_start(x_tok[:, 1:3, :], A["x_sample"][0].rearrange("(c p) n -> p c n", p=P)).then_inc(x_loaded, 16)
                for u in range(1, ADA_FIRST):
                    for q in range(U):
                        load_ada(U * u + q, u, q)
                ffn(0)
                sp.wait_ge(gw_ready, 1)
                for q in range(U):
                    load(P_GATES + q, gw_pad[:, PK * q:PK * q + PK, :])
                for n, t in enumerate(XBC_ORDER):
                    for q in range(U):
                        load(P_XBC + U * n + q, block_of(w_in, COL_XBC + PC * t, q))
                with sp.Fori(0, HEADS // 2) as i:
                    for j, (col, hh, q) in enumerate(PAIR_ORDER):
                        load(P_HEADS + j, block_of(w_in, i * (2 * DH) + (col + DH * hh), q), i, PAIR)
                for t in range(D // PC):
                    for q in range(U):
                        load(P_OUT + U * t + q, block_of(w_out, PC * t, q))
                ffn(1)
                for kk in range(KT // 4):
                    for c in range(NCH):
                        n = NCH * kk + c
                        sp.wait_ge(out_ready_act if n % 2 else out_ready_dve, n // 2 + 1)
                        dst = A["y_prompt"][0] if c == 0 else A["y_sample"][0, P * (c - 1):P * c]
                        sp.dma_start(dst[:, 512 * kk:512 * kk + 512], out_tok[:, c, 512 * kk:512 * kk + 512]).then_inc(out_stored, 16)
                sp.wait_ge(out_stored, 16 * NCH * (KT // 4))
                sp.wait_ge(s_stored, 16 * 2 * SSM_G)
                sp.wait_ge(m_cstored, 32 * 2 * HEADS)
                sp.wait_ge(m_stored, 32)

            @block.tensor
            def _(pe):
                def wait_piece(p, i=None, per=0):
                    pe.wait_ge(w_lo_pool if p % 2 else w_lo_dve, at(p // 2 + 1, i, per // 2))

                def product(out, slot, off, hi, lo, start, stop):
                    wh = w_hi[:, slot, off:off + P]
                    pe.matmul(out, wh, hi, start=start, stop=False)
                    pe.matmul(out, wh, lo, start=False, stop=False)
                    return pe.matmul(out, w_lo[:, slot, off:off + P], hi, start=False, stop=stop)

                def unit_piece(p, q, b0, i=None, per=0):
                    wait_piece(p, i, per)
                    for f in range(2):
                        for k in range(PK):
                            last = product(psum[b0 + f][:, 0:TOK], p % NS, k * PC + f * P, xn_hi[:, PK * q + k, :],
                                           xn_lo[:, PK * q + k, :], q == 0 and k == 0, q == U - 1 and k == PK - 1)
                    last.then_inc(pe_piece, 1)

                def ada_piece(a, q, bank, i=None):
                    pe.wait_ge(ada_loaded[a % ADA_R], at(16 * (a // ADA_R + 1), i, 16 * U * ADA_PER // ADA_R))
                    for f in range(2):
                        for k in range(PK):
                            off = k * PC + f * P
                            last = pe.matmul(psum[bank][:, 2 * f:2 * f + 2], ada_raw[:, a % ADA_R, off:off + P],
                                             cT[:, PK * q + k, :], start=(q == 0 and k == 0 and f == 0),
                                             stop=(q == U - 1 and k == PK - 1), skip_group_check=True)
                    last.then_inc(ada_used, 1)

                def square_sum(name, k):
                    base, count = SQ[name]
                    pe.wait_ge(sq_ready, base + k + 1)
                    if k == 0 and base:
                        pe.wait_ge(std_ready, SQ_ORDER.index(name))
                    pe.matmul(psum[3][:, 0:TOK], ones[:, :], sq[:, (base + k) % 2, :], start=(k == 0),
                              stop=(k == count - 1)).then_inc(ss_mm, 1)

                pe.wait_ge(const_ready, 1)
                pe.wait_ge(vec_loaded, 16 * N_VEC)
                for r, (n, col) in enumerate(VEC_ROWS):
                    last = pe.transpose(psum[4][:, col:col + n], vec_rows[0:n, r, :], idn[0:n, 0:n])
                last.then_inc(vec_tr, 1)
                pe.wait_ge(c_ready, 2)
                for u in range(ADA_FIRST):
                    if u >= 2:
                        pe.wait_ge(ada_evac, u - 1)
                    for q in range(U):
                        ada_piece(U * u + q, q, 6 + u % 2)
                    if u < KT:
                        if u == 0:
                            pe.wait_ge(x_loaded, 32)
                        if u >= 2:
                            pe.wait_ge(xT_ready, u - 1)
                        for c in range(NCH):
                            last = pe.transpose(psum[u % 2][:, P * c:P * c + P], x_tok[:, c, P * u:P * u + P], idn[:, :])
                        last.then_inc(xt_tr, 1)
                    if u >= 1:
                        square_sum("x0", u - 1)

                def ffn(n):
                    def down_piece(p, j, it, i=None):
                        wait_piece(p, i, FFN_PER)
                        hid = 4 * (FFN_IT * n + it + 1)
                        if j == 0:
                            pe.wait_ge(hid_hi_ready, at(hid, i, 4))
                            pe.wait_ge(hid_lo_ready, at(hid, i, 4))
                        for f in range(2):
                            t = 2 * j + f
                            if n or it or i is not None or t >= 2:
                                before = KT * (FFN_IT * n + it) + (KT if n else 0) + t - 1
                                if before > 0:
                                    pe.wait_ge(y_done, at(before, i, KT))
                            for k in range(PK):
                                last = product(psum[4 + f][:, 0:TOK], p % NS, k * PC + f * P, hid_hi[:, k, :],
                                               hid_lo[:, k, :], k == 0, k == PK - 1)
                        last.then_inc(pe_piece, 1)

                    def step(i):
                        first = i is None
                        base, per = (ffn_first(n), 0) if first else (ffn_loop(n), FFN_PER)
                        it = 0 if first else 1
                        length = FFN_PER - (DOWN if first else 0)
                        a0 = U * ADA_FIRST + (0 if first else U * ADA_PER)
                        done = 0
                        for kind, s, j_loop, j_first in PARTS:
                            j0 = j_first if first else j_loop
                            if j0 is None:
                                continue
                            for q in range(DOWN if kind == "d" else U):
                                if kind == "d":
                                    down_piece(base + j0 + q, q, 0, i)
                                else:
                                    read = 4 * (FFN_IT * n + it) + 2 * s
                                    if q == 0 and read:
                                        pe.wait_ge(silu_ready if kind == "g" else hid_ready, at(read, i, 4))
                                    unit_piece(base + j0 + q, q, 0 if kind == "g" else 2, i, per)
                                while n == 0 and done < ada_upto(j0 + q, length):
                                    u = done // U
                                    if done % U == 0:
                                        before = ADA_FIRST + (0 if first else ADA_PER) + u - (1 if u else 0)
                                        pe.wait_ge(ada_evac, at(before, i, ADA_PER))
                                    ada_piece(a0 + done, done % U, 6 + u % 2, i)
                                    done += 1

                    pe.wait_ge(xn_hi_ready, KT * (4 if n else 1))
                    pe.wait_ge(xn_lo_ready, KT * (4 if n else 1))
                    step(None)
                    with pe.Fori(0, FFN_IT - 1) as i:
                        step(i)
                    name = "y3" if n else "y1"
                    for j in range(DOWN):
                        down_piece(ffn_first(n) + FFN_LEN - DOWN + j, j, FFN_IT - 1)
                        if j:
                            square_sum(name, 2 * j - 2)
                            square_sum(name, 2 * j - 1)
                    square_sum(name, KT - 2)
                    square_sum(name, KT - 1)

                ffn(0)
                for k in range(KT):
                    square_sum("x1", k)

                pe.wait_ge(xn_hi_ready, KT * 2)
                pe.wait_ge(xn_lo_ready, KT * 2)
                for q in range(U):
                    unit_piece(P_GATES + q, q, 0)

                def conv_transposes(n):
                    for f in range(2):
                        m = 2 * TOK_UNITS.index(n) + f
                        pe.wait_ge(conv_silu, 2 * n + f + 1)
                        if m >= 2:
                            pe.wait_ge(tok_ready, m - 1)
                        src = bcT[:, f, :] if n == UNIT_B else cvs[:, f, :]
                        for c in range(NCH):
                            last = pe.transpose(psum[4 + f][:, P * c:P * c + P], src[:, P * c:P * c + P], idn[:, :])
                        last.then_inc(conv_tr, 1)

                for n in range(XBC_T // 2):
                    if n == 1:
                        pe.wait_ge(gate_read, 2)
                    elif n >= 2:
                        pe.wait_ge(conv_done, 2 * (n - 1))
                    for q in range(U):
                        unit_piece(P_XBC + U * n + q, q, 0 if n % 2 else 2)
                    if n - 1 in TOK_UNITS:
                        conv_transposes(n - 1)
                conv_transposes(XBC_T // 2 - 1)

                pe.wait_ge(gates_done, 1)
                pe.wait_ge(tok_ready, 2 * len(TOK_UNITS))
                pe.wait_ge(conv_done, XBC_T)
                for kind, src in enumerate((r_Q, r_E, r_W, r_T4)):
                    for c in range(NCH):
                        last = pe.transpose(psum[4 + kind][:, P * c:P * c + P], src[:, P * c:P * c + P], idn[:, :])
                    last.then_inc(cols_tr, 1)
                pe.matmul(psum[2][:, 0:P], ones[:, :], r_t[:, 0:P], start=True, stop=True).then_inc(dec_mm, 1)
                pe.wait_ge(sr_loaded, 32)
                for n in range(4):
                    d, half = divmod(n, 2)
                    if n >= 2:
                        pe.wait_ge(st_ready, n - 1)
                    for j in range(4):
                        last = pe.transpose(psum[half][:, P * j:P * j + P], s_raw[:, d, 4 * half + j, :], idn[:, :])
                    last.then_inc(st_tr, 1)

                pe.wait_ge(cols_ready, 4)
                pe.wait_ge(st_ready, 4)
                for n, (g, c, d, step) in enumerate(SSM_STEPS):
                    tok = slice(P * c, P * c + P)
                    carried, states = ssm_before(n)
                    if n:
                        pe.wait_ge(ss_seg, n)
                        if carried:
                            pe.wait_ge(ss_tmp, carried)
                        if states:
                            pe.wait_ge(ss_state, states)
                    for h in range(8):
                        r = ROW_SS[d] + 8 * g + h
                        pe.matmul(psum[4 + h // 4][:, P * (h % 4):P * (h % 4) + P], idn[:, r:r + 1].broadcast_to((P, P)),
                                  r_P[:, tok], start=True, stop=True)
                    pe.matmul(psum[6][:, 0:P], bcT[:, g, tok], bcT[:, 2 + g, tok], start=True, stop=True).then_inc(ss_bc, 1)
                    pe.wait_ge(ss_wd, n + 1)
                    pe.wait_ge(ss_wp, n + 1)
                    pe.wait_ge(ss_x, n + 1)
                    if n:
                        pe.wait_ge(ss_yacc, n)
                    for h in range(8):
                        last = pe.matmul(psum[7][:, SSM_P * h:SSM_P * h + SSM_P], seg[:, h, :],
                                         xdt[:, SSM_P * h:SSM_P * h + SSM_P], start=True, stop=True)
                    last.then_inc(ss_y, 1)
                    pe.wait_ge(ss_cb, n + 1)
                    if c:
                        pe.matmul(psum[6][:, :], bcT[:, 2 + g, tok], ST[:, d, GRP_W * g:GRP_W * g + GRP_W],
                                  start=True, stop=True).then_inc(ss_int, 1)
                    if step < N_STATE:
                        if c:
                            pe.wait_ge(ss_tmp, carried + 1)
                            last = pe.matmul(psum[6][:, :], bm_tok[:, c, SSM_N * g:SSM_N * g + SSM_N], xte[:, :],
                                             start=True, stop=True)
                        else:
                            for j in range(4):
                                last = pe.matmul(psum[6][:, P * j:P * j + P], xte[:, P * j:P * j + P],
                                                 bm_tok[:, 0, SSM_N * g:SSM_N * g + SSM_N], start=True, stop=True)
                        last.then_inc(ss_stm, 1)

                pe.wait_ge(ss_yacc, len(SSM_STEPS))
                pe.wait_ge(ss_ypool, ssm_before(len(SSM_STEPS))[0])
                for t in range(KT // 2):
                    if t >= 2:
                        pe.wait_ge(yt_ready, t - 1)
                    for c in range(NCH):
                        last = pe.transpose(psum[4 + t % 2][:, P * c:P * c + P], yacc[:, c, P * t:P * t + P], idn[:, :])
                    last.then_inc(yt_tr, 1)
                pe.wait_ge(yt_ready, KT // 2)

                pe.wait_ge(dec_ready, 1)
                pe.wait_ge(v_ones, 1)
                with pe.Fori(0, HEADS // 2) as i:
                    def kv_transposes(hh):
                        qT, kT, vT, ktok, va = hset[hh]
                        if hh:
                            pe.wait_ge(m_seg, at(6, i, 12))
                        for n, src in enumerate((kT, vT)):
                            pe.wait_ge(qkv_ready, at(6 * hh + 4 + 2 * n, i, 12))
                            for f in range(2):
                                if n:
                                    pe.wait_ge(kv_tok, at(4 * hh + f + 1, i, 8))
                                for c in range(NCH):
                                    last = pe.transpose(psum[4 + f][:, P * c:P * c + P], src[:, f, P * c:P * c + P], idn[:, :])
                                last.then_inc(kv_tr, 1)

                    def core_start(hh):
                        pe.wait_ge(row_ready, at(2 * hh + 2, i, 4))
                        pe.wait_ge(kv_tok, at(4 * hh + 4, i, 8))
                        if hh:
                            pe.wait_ge(mix_ready, at(2, i, 4))
                        for d in range(2):
                            last = pe.matmul(psum[4 + d][:, 0:TOK], ones[:, :], mrow[:, d, :], start=True, stop=True)
                        last.then_inc(m_bc, 1)

                    def core_a(hh, n):
                        qT, kT, vT, ktok, va = hset[hh]
                        tok = slice(P * STEPS[n][0], P * STEPS[n][0] + P)
                        if n or hh:
                            pe.wait_ge(m_h, at(6 * hh + n, i, 12))
                            pe.wait_ge(m_c, at(N_STATE * hh + min(n, N_STATE), i, 8))
                        for k in range(2):
                            last = pe.matmul(psum[6][:, 0:P], kT[:, k, tok], qT[:, k, tok], start=(k == 0), stop=(k == 1))
                        last.then_inc(m_qk, 1)

                    def core_b(hh, n):
                        qT, kT, vT, ktok, va = hset[hh]
                        c, d = STEPS[n]
                        pe.wait_ge(m_s, at(6 * hh + n + 1, i, 12))
                        pe.matmul(psum[7][:, 0:VW], sT[:, :], va[:, c, :], start=True, stop=True).then_inc(m_num, 1)
                        if c:
                            if n == 2:
                                pe.wait_ge(c_loaded[hh], at(64, i, 64))
                            for k in range(2):
                                last = pe.matmul(psum[6][:, 0:VW], qT[:, k, P * c:P * c + P], cst[hh][:, d, k, :],
                                                 start=(k == 0), stop=(k == 1))
                            last.then_inc(m_int, 1)

                    def core_c(hh, n):
                        qT, kT, vT, ktok, va = hset[hh]
                        pe.wait_ge(m_wk, at(N_STATE * hh + n + 1, i, 8))
                        pe.wait_ge(m_h, at(6 * hh + n + 1, i, 12))
                        for k in range(2):
                            last = pe.matmul(psum[7 - k][:, 0:VW], wk[:, P * k:P * k + P], va[:, STEPS[n][0], :], start=True, stop=True)
                        last.then_inc(m_upd, 1)

                    def core_end(hh):
                        pe.wait_ge(h_norm, at(NCH * (hh + 1), i, 2 * NCH))
                        pe.wait_ge(kv_tok, at(8, i, 8))
                        for k in range(2):
                            for c in range(NCH):
                                last = pe.transpose(psum[4 + k][:, P * c:P * c + P], hacc[:, c, P * k:P * k + P], idn[:, :])
                        last.then_inc(h_tr, 1)

                    tasks = {"kv": kv_transposes, "start": core_start, "end": core_end, "a": core_a, "b": core_b, "c": core_c}
                    for j, (col, hh, q) in enumerate(PAIR_ORDER):
                        unit = j // U
                        if q == 0 and unit >= 2:
                            if unit < 8:
                                pe.wait_ge(qkv_ready, at(2 * (unit - 1), i, 12))
                            else:
                                pe.wait_ge(og_ready, at(2 * (unit - 7), i, 4))
                        unit_piece(P_HEADS + j, q, 2 * (unit % 2), i, PAIR)
                        for kind, thh, n in core_tasks(j):
                            tasks[kind](thh) if n is None else tasks[kind](thh, n)
                    pe.wait_ge(z_done, at(4, i, 4))
                    pe.wait_ge(mix_ready, at(4, i, 4))

                for k in range(KT // 2):
                    square_sum("ssm", k)
                pe.wait_ge(xn_hi_ready, KT * 3)
                pe.wait_ge(xn_lo_ready, KT * 3)
                for t in range(D // PC):
                    if t >= 2:
                        pe.wait_ge(y_done, KT * FFN_IT + 2 * (t - 1))
                    for q in range(U):
                        unit_piece(P_OUT + U * t + q, q, 4 if t % 2 else 0)
                    if t:
                        square_sum("y2", 2 * t - 2)
                        square_sum("y2", 2 * t - 1)
                square_sum("y2", KT - 2)
                square_sum("y2", KT - 1)
                for k in range(KT):
                    square_sum("x2", k)
                ffn(1)
                for kk in range(KT // 4):
                    pe.wait_ge(x_updated, 2 * KT + 4 * kk + 4)
                    for c in range(NCH):
                        n = NCH * kk + c
                        if n >= 2:
                            pe.wait_ge(out_ready_act if n % 2 else out_ready_dve, n // 2)
                        for j in range(4):
                            last = pe.transpose(psum[4 + n % 2][:, P * j:P * j + P], xT[:, 4 * kk + j, P * c:P * c + P], idn[:, :])
                        last.then_inc(out_tr, 1)

            @block.scalar
            def _(act):
                def split(p, i=None, per=0):
                    if p >= TOTAL:
                        return
                    act.wait_ge(raw_loaded[p % NR], at(16 * (p // NR + 1), i, 16 * per // NR))
                    if p >= NS:
                        act.wait_ge(pe_piece, at(p - NS + 1, i, per))
                    act.activation(w_hi[:, p % NS, :], w_raw[:, p % NR, :], ACT.Copy).then_inc(w_hi_ready, 1)

                def square(name, k, src):
                    n = SQ[name][0] + k
                    if n >= 2:
                        act.wait_ge(ss_mm, n - 1)
                    act.activation(sq[:, n % 2, :], src, ACT.Square).then_inc(sq_ready, 1)

                def root(name, width):
                    base, count = SQ[name]
                    act.wait_ge(ss_mm, base + count)
                    act.activation(std[:, :], psum[3][:, 0:TOK], ACT.Sqrt, bias=eps[:, 0:1], scale=1.0 / width).then_inc(std_ready, 1)

                def hi_of(stage, src, ready, first):
                    for k in range(KT):
                        act.wait_ge(ready, first + k + 1)
                        act.activation(xn_hi[:, k, :], src(k), ACT.Copy).then_inc(xn_hi_ready, 1)

                def ffn(n):
                    def posts(j0, it, s, kind, p_end, i, per):
                        for f in range(2):
                            m = 4 * (FFN_IT * n + it) + 2 * s + f
                            if kind == "g":
                                act.wait_ge(pe_piece, at(p_end + 1, i, per)) if f == 0 else None
                                if m >= 2:
                                    act.wait_ge(hid_ready, at(m - 1, i, 4))
                                act.activation(sg[:, f, :], psum[f][:, 0:TOK], ACT.Silu).then_inc(silu_ready, 1)
                            else:
                                act.wait_ge(hid_ready, at(m + 1, i, 4))
                                act.activation(hid_hi[:, 2 * s + f, :], hidf[:, f, :], ACT.Copy).then_inc(hid_hi_ready, 1)

                    def step(i):
                        first = i is None
                        base, per = (ffn_first(n), 0) if first else (ffn_loop(n), FFN_PER)
                        for kind, s, j_loop, j_first in PARTS:
                            j0 = j_first if first else j_loop
                            if j0 is None:
                                continue
                            for q in range(DOWN if kind == "d" else U):
                                split(base + j0 + q + AHEAD, i, per)
                            if kind != "d":
                                posts(j0, 0 if first else 1, s, kind, base + j0 + U - 1, i, per)

                    step(None)
                    with act.Fori(0, FFN_IT - 1) as i:
                        step(i)
                    name = "y3" if n else "y1"
                    added = KT * (FFN_IT * (n + 1) - 1) + (KT if n else 0)
                    for j in range(DOWN):
                        split(ffn_first(n) + FFN_LEN - DOWN + j + AHEAD)
                        for k in (2 * j, 2 * j + 1):
                            act.wait_ge(y_done, added + k + 1)
                            square(name, k, y[:, k, :])
                    root(name, D)

                for n, (rows, block_, src) in enumerate((
                        ((0, 96), 0, A["norm_g"][0].rearrange("j (k p) -> (j k) p", p=P)),
                        ((96, 108), 0, A["conv_b"][0].rearrange("(k p) -> k p", p=P)),
                        ((108, 116), 0, A["ml_norm_g"][0].rearrange("(k p) -> k p", p=P)),
                        ((116, 124), 0, A["ssm_norm_g"][0].rearrange("(k p) -> k p", p=P)),
                        ((0, 60), 1, A["conv_w"][0].rearrange("j (k p) -> (j k) p", p=P)),
                        ((0, 128), 2, A["b_ada"][0].rearrange("(k p) -> k p", p=P)[0:P]),
                        ((0, 16), 3, A["b_ada"][0].rearrange("(k p) -> k p", p=P)[P:ADA_T]),
                        ((16, 32), 3, A["c_ctx"].rearrange("(k p) -> k p", p=P)),
                        ((32, 48), 3, A["c"][0].rearrange("(k p) -> k p", p=P)))):
                    act.dma_start(vec_rows[rows[0]:rows[1], block_, :], src).then_inc(vec_loaded, 16)
                act.wait_ge(const_ready, 1)
                for row, col, src in (
                        (0, 0, A["gate_bias"][0, 1, 0]), (64, 0, A["gate_bias"][0, 1, 1]),
                        (32, 0, A["dt_bias"][0, 0]), (96, 0, A["dt_bias"][0, 1]),
                        (0, 2, A["gate_bias"][0, 0, 0]), (64, 2, A["gate_bias"][0, 0, 1]),
                        (32, 3, A["a_log"][0, 0]), (96, 3, A["a_log"][0, 1]),
                        (0, 7, A["state_mlstm_m"][0, 0, 0]), (64, 8, A["state_mlstm_m"][0, 0, 1])):
                    act.dma_start(gcol[row:row + src.shape[0], col:col + 1], src.unsqueeze(1)).then_inc(cols_loaded, 16)
                act.dma_start(dsk[:, :], A["d_skip"][0].partition_broadcast(P)).then_inc(cols_loaded, 16)
                act.wait_ge(vec_ready, 1)
                act.activation(cT[:, :, 0], vecT[:, V_CCTX:V_CCTX + KT], ACT.Silu).then_inc(c_ready, 1)
                act.activation(cT[:, :, 1], vecT[:, V_C:V_C + KT], ACT.Silu).then_inc(c_ready, 1)
                act.dma_start(gw_small[:, :, 0:16], w_in[:, :, COL_IG:COL_IG + 16]).then_inc(gw_loaded, 16)
                act.dma_start(gw_small[:, :, 16:48], w_in[:, :, COL_DT:COL_DT + 32]).then_inc(gw_loaded, 16)
                for k in range(KT):
                    act.wait_ge(xT_ready, k + 1)
                    square("x0", k, xT[:, k, :])
                root("x0", D)
                hi_of(0, lambda k: hn[:, k % 2, :], hn_ready, 0)
                for p in range(AHEAD):
                    split(p)
                ffn(0)
                for k in range(KT):
                    act.wait_ge(x_updated, k + 1)
                    square("x1", k, xT[:, k, :])
                root("x1", D)
                hi_of(1, lambda k: hn[:, k % 2, :], hn_ready, KT)
                act.dma_start(x_wait, AX).then_inc(x_spilled, 16)

                def gate_part(m):
                    if m == 0:
                        act.wait_ge(dve_row, 1)
                        act.activation(r_e, r_t, ACT.Exp, scale=-1.0).then_inc(act_row, 1)
                        act.wait_ge(cols_loaded, 16 * N_COLS)
                        act.activation(gcol[:, 4:5], gcol[:, 3:4], ACT.Exp).then_inc(act_row, 1)
                    if m == 1:
                        act.wait_ge(dve_row, 2)
                        act.activation(r_lw, r_d, ACT.Ln).then_inc(act_row, 1)
                    if m == 3:
                        act.wait_ge(dve_row, 3)
                        for c in range(NCH):
                            t = slice(P * c, P * c + P)
                            act.activation(r_E[:, t], r_P[:, t], ACT.Exp, bias=gcol[:, 6 + c:7 + c])
                            act.activation(r_W[:, t], r_Q[:, t], ACT.Exp, bias=gcol[:, 9 + c:10 + c])
                        act.activation(r_T4, r_li, ACT.Exp).then_inc(act_row, 1)

                for p in range(P_GATES, P_HEADS):
                    split(p + AHEAD)
                    j = p - P_XBC
                    if j >= 0 and j % U == U - 1:
                        n = j // U
                        for f in range(2):
                            act.wait_ge(conv_done, 2 * n + f + 1)
                            if n in (UNIT_B, UNIT_C):
                                dst = bcT[:, 2 * n + f, :]
                            else:
                                dst = cvs[:, f, :]
                                if n > 2:
                                    act.wait_ge(conv_tr, 2 * TOK_UNITS.index(n) + f - 1)
                            act.activation(dst, cv[:, f, :], ACT.Silu).then_inc(conv_silu, 1)
                    if j in GATE_AT:
                        gate_part(GATE_AT[j])
                act.wait_ge(gates_done, 1)
                for d in range(2):
                    act.dma_start(A["new_m"][0, 0, d].unsqueeze(1), gcol[ROW_ML[d]:ROW_ML[d] + HEADS, 13:14]).then_inc(m_stored, 16)
                act.wait_ge(cols_tr, 4)
                act.wait_ge(dec_mm, 1)
                for d in range(2):
                    act.dma_start(s_raw[:, d, :, :], A["state_ssm"][0, 0, d].rearrange("(j a) q n -> (a q) j n", a=2)).then_inc(sr_loaded, 16)
                for n, (g, c, d, step) in enumerate(SSM_STEPS):
                    act.wait_ge(ss_bc, n + 1)
                    if n:
                        act.wait_ge(ss_wd, n)
                        act.wait_ge(ss_wp, n)
                    act.activation(cbs, psum[6][:, 0:P], ACT.Copy).then_inc(ss_cb, 1)
                    act.wait_ge(ss_seg, n + 1)
                    act.activation(seg[:, :, :], seg[:, :, :], ACT.Exp).then_inc(ss_exp, 1)
                    if c == 0:
                        act.wait_ge(ss_state, ssm_before(n)[1] + 1)
                        dst = A["new_ssm"][0, 0, d, 8 * g:8 * g + 8].rearrange("(j a) q n -> (a q) j n", a=2)
                        act.dma_start(dst, s_out.rearrange("p (j n) -> p j n", j=4)).then_inc(s_stored, 16)

                act.wait_ge(yt_ready, KT // 2)
                with act.Fori(0, HEADS // 2) as i:
                    def a(hh, n):
                        if n in (1, 2):
                            act.wait_ge(m_cstored, at(64 * hh + 32 * n, i, 128))
                        act.wait_ge(m_seg, at(6 * hh + n + 1, i, 12))
                        act.activation(ex, ex, ACT.Exp).then_inc(m_exp, 1)

                    def b(hh, n):
                        c, d = STEPS[n]
                        if c:
                            act.wait_ge(m_int, at(4 * hh + n - 1, i, 8))
                            act.wait_ge(m_h, at(6 * hh + n, i, 12))
                            row = i * 2 + (ROW_ML[d] + hh)
                            act.activation(ti, psum[6][:, 0:VW], ACT.Copy, scale=cols[:, C_E, c, bass.ds(row, 1)]).then_inc(m_ti, 1)

                    def c_(hh, n):
                        c, d = STEPS[n]
                        if c == 0:
                            act.wait_ge(m_c, at(N_STATE * hh + n + 1, i, 8))
                            h = i * 2 + hh
                            act.dma_start(A["new_C"][0, 0, d, bass.ds(h, 1)].rearrange("a (k p) v -> p (a k) v", p=P),
                                          c_out[:, :, 0:DH]).then_inc(m_cstored, 16)
                            act.dma_start(A["new_n"][0, 0, d, bass.ds(h, 1)].rearrange("a (k p) -> p (a k)", p=P),
                                          c_out[:, :, DH], allow_slow_non_contiguous=True).then_inc(m_cstored, 16)

                    def end(hh):
                        act.wait_ge(h_var, at(hh + 1, i, 2))
                        act.activation(small[:, 24:27], small[:, 20:23], ACT.Sqrt, bias=eps[:, 0:1]).then_inc(h_std, 1)

                    tasks = {"a": a, "b": b, "c": c_}
                    for j, (col, hh, q) in enumerate(PAIR_ORDER):
                        split(P_HEADS + j + AHEAD, i, PAIR)
                        if j == 0:
                            for s in range(2):
                                h = i * 2 + s
                                for d in range(2):
                                    act.dma_start(cst[s][:, d, :, 0:DH], A["state_mlstm_C"][0, 0, d, bass.ds(h, 1)].rearrange(
                                        "a (k p) v -> p (a k) v", p=P)).then_inc(c_loaded[s], 16)
                                    act.dma_start(cst[s][:, d, :, DH], A["state_mlstm_n"][0, 0, d, bass.ds(h, 1)].rearrange(
                                        "a (k p) -> p (a k)", p=P), allow_slow_non_contiguous=True).then_inc(c_loaded[s], 16)
                        if q == U - 1 and col in (COL_O, COL_Z):
                            b0 = 2 * ((j // U) % 2)
                            act.wait_ge(pe_piece, at(P_HEADS + j + 1, i, PAIR))
                            for f in range(2):
                                if col == COL_O:
                                    act.activation(sigo[hh][:, f, :], psum[b0 + f][:, 0:TOK], ACT.Sigmoid).then_inc(og_ready, 1)
                                else:
                                    act.activation(psum[b0 + f][:, 0:TOK], psum[b0 + f][:, 0:TOK], ACT.Silu).then_inc(z_silu, 1)
                        for kind, thh, n in core_tasks(j):
                            if kind in tasks:
                                tasks[kind](thh, n)
                            elif kind == "end":
                                end(thh)

                act.wait_ge(mix_ready, 2 * HEADS)
                act.wait_ge(z_done, 2 * HEADS)
                for k in range(KT // 2):
                    square("ssm", k, y[:, KT // 2 + k, :])
                root("ssm", SSM_W)
                act.dma_start(AX, x_wait).then_inc(x_back, 16)
                for k in range(KT):
                    if k >= KT // 2:
                        act.wait_ge(ms_scaled, k - KT // 2 + 1)
                    act.activation(xn_hi[:, k, :], y[:, k, :], ACT.Copy).then_inc(xn_hi_ready, 1)
                for t in range(D // PC):
                    for q in range(U):
                        split(P_OUT + U * t + q + AHEAD)
                    for k in (2 * t, 2 * t + 1):
                        act.wait_ge(y_done, KT * FFN_IT + k + 1)
                        square("y2", k, y[:, k, :])
                root("y2", D)
                for k in range(KT):
                    act.wait_ge(x_updated, KT + k + 1)
                    square("x2", k, xT[:, k, :])
                root("x2", D)
                hi_of(3, lambda k: hn[:, k % 2, :], hn_ready, 2 * KT)
                ffn(1)
                for n in range(1, NCH * (KT // 4), 2):
                    kk, c = divmod(n, NCH)
                    act.wait_ge(out_tr, n + 1)
                    act.activation(out_tok[:, c, 512 * kk:512 * kk + 512], psum[4 + n % 2][:, :], ACT.Copy).then_inc(out_ready_act, 1)

            @block.vector
            def _(dve):
                own = Tally(dve, dve_step)
                link = own.link

                def split(p, i=None, per=0):
                    if p % 2 or p >= TOTAL:
                        return
                    dve.wait_ge(w_hi_ready, at(p + 1, i, per))
                    dve.tensor_tensor(w_lo[:, p % NS, :], w_raw[:, p % NR, :], w_hi[:, p % NS, :].bitcast(F32),
                                      ALU.subtract).then_inc(w_lo_dve, 1)

                def norm_coefs(stage):
                    scale = modT[:, KT * (3 * stage + 1):KT * (3 * stage + 2), :]
                    g = vecT[:, V_NORM + 2 * stage * KT:V_NORM + (2 * stage + 1) * KT].unsqueeze(2).broadcast_to((P, KT, 2))
                    link(dve.scalar_tensor_tensor(out=coefA[:, :, :], in0=scale, scalar=1.0, in1=g, op0=ALU.add, op1=ALU.mult))

                def gate_coefs(stage):
                    gate = modT[:, KT * (3 * stage + 2):KT * (3 * stage + 3), :]
                    g = vecT[:, V_NORM + (2 * stage + 1) * KT:V_NORM + (2 * stage + 2) * KT].unsqueeze(2).broadcast_to((P, KT, 2))
                    link(dve.scalar_tensor_tensor(out=coefG[:, :, :], in0=gate, scalar=1.0 if stage == 1 else 0.5, in1=g,
                                                  op0=ALU.mult, op1=ALU.mult))

                def inverse_root(name):
                    dve.wait_ge(std_ready, SQ_ORDER.index(name) + 1)
                    link(dve.reciprocal(psum[2][:, 0:TOK], std[:, :]))

                def pre_norm(stage, name):
                    norm_coefs(stage)
                    inverse_root(name)
                    done = KT * stage
                    lo_done = KT * (0, 1, 3)[stage]

                    def scaled(k):
                        if k >= 2:
                            dve.wait_ge(hn_ready, done + k - 1)
                        dve.tensor_tensor(xt[:, k % 2, :], xT[:, k, :], psum[2][:, 0:TOK], ALU.mult).then_inc(xt_done, 1)

                    def modulated(k):
                        dve.wait_ge(xt_done, done + k + 1)
                        if k >= 2:
                            dve.wait_ge(xn_lo_ready, lo_done + k - 1)
                        for grp, (t0, t1) in enumerate(GROUPS):
                            last = dve.tensor_scalar(hn[:, k % 2, t0:t1], xt[:, k % 2, t0:t1], coefA[:, k, grp:grp + 1],
                                                     modT[:, 3 * stage * KT + k, grp:grp + 1], ALU.mult, ALU.add)
                        last.then_inc(hn_ready, 1)

                    scaled(0)
                    for k in range(KT):
                        if k + 1 < KT:
                            scaled(k + 1)
                        modulated(k)

                def post_norm(stage, name):
                    gate_coefs(stage)
                    inverse_root(name)
                    for k in range(KT):
                        for grp, (t0, t1) in enumerate(GROUPS):
                            last = dve.scalar_tensor_tensor(out=y[:, k, t0:t1], in0=y[:, k, t0:t1], scalar=coefG[:, k, grp:grp + 1],
                                                            in1=psum[2][:, t0:t1], op0=ALU.mult, op1=ALU.mult)
                        last.then_inc(u_ready, 1)

                def ffn(n):
                    def add_down(p, j, it, i=None, per=0):
                        dve.wait_ge(pe_piece, at(p + 1, i, per))
                        for f in range(2):
                            t = 2 * j + f
                            before = KT * (FFN_IT * n + it) + (KT if n else 0) + t
                            if n or it or i is not None:
                                if before - KT + 1 > 0:
                                    dve.wait_ge(y_done, at(before - KT + 1, i, KT))
                            dve.tensor_tensor(y[:, t, :], y[:, t, :], psum[4 + f][:, 0:TOK], ALU.add).then_inc(y_done, 1)

                    def hidden(p_end, it, s, i, per):
                        dve.wait_ge(pe_piece, at(p_end + 1, i, per))
                        for f in range(2):
                            m = 4 * (FFN_IT * n + it) + 2 * s + f
                            dve.wait_ge(silu_ready, at(m + 1, i, 4))
                            if m >= 2:
                                dve.wait_ge(hid_lo_ready, at(m - 1, i, 4))
                            dve.tensor_tensor(hidf[:, f, :], sg[:, f, :], psum[2 + f][:, 0:TOK], ALU.mult).then_inc(hid_ready, 1)

                    def step(i):
                        first = i is None
                        base, per = (ffn_first(n), 0) if first else (ffn_loop(n), FFN_PER)
                        for kind, s, j_loop, j_first in PARTS:
                            j0 = j_first if first else j_loop
                            if j0 is None:
                                continue
                            for q in range(DOWN if kind == "d" else U):
                                split(base + j0 + q + AHEAD, i, per)
                                if kind == "d":
                                    add_down(base + j0 + q, q, 0, i, per)
                                if n == 0:
                                    ada_posts(i, first, j0 + q)
                            if kind == "u":
                                hidden(base + j0 + U - 1, 0 if first else 1, s, i, per)

                    def ada_posts(i, first, j):
                        length = FFN_PER - (DOWN if first else 0)
                        before, now = (ada_upto(j - 1, length) if j else 0), ada_upto(j, length)
                        for u in range(before // U, now // U):
                            unit = ADA_FIRST + u + (0 if first else ADA_PER)
                            ada_store(unit, 6 + u % 2, i)

                    dve.wait_ge(y_zeroed, n + 1)
                    step(None)
                    with dve.Fori(0, FFN_IT - 1) as i:
                        step(i)
                    for j in range(DOWN):
                        p = ffn_first(n) + FFN_LEN - DOWN + j
                        split(p + AHEAD)
                        add_down(p, j, FFN_IT - 1)

                def ada_store(unit, bank, i=None):
                    dve.wait_ge(ada_used, at(U * (unit + 1), i, U * ADA_PER))
                    t0 = 2 * unit if i is None else i * (2 * ADA_PER) + 2 * unit
                    bias = vecT[:, bass.ds(t0 + V_BADA, 2)].unsqueeze(2).broadcast_to((P, 2, 2))
                    dve.tensor_tensor(modT[:, bass.ds(t0, 2), :], psum[bank][:, 0:4].rearrange("p (f g) -> p f g", f=2),
                                      bias, ALU.add).then_inc(ada_evac, 1)

                dve.wait_ge(vec_tr, 1)
                for c0, c1 in ((0, 124), (128, 188)):
                    dve.tensor_copy(vecT[:, c0:c1], psum[4][:, c0:c1])
                dve.tensor_copy(vecT[:, 256:432], psum[4][:, 256:432]).then_inc(vec_ready, 1)
                dve.wait_ge(vec_ready, 1)
                for u in range(ADA_FIRST):
                    ada_store(u, 6 + u % 2)
                    if u < KT:
                        dve.wait_ge(xt_tr, u + 1)
                        dve.tensor_copy(xT[:, u, :], psum[u % 2][:, 0:TOK]).then_inc(xT_ready, 1)
                dve.wait_ge(ada_evac, ADA_FIRST)
                dve.wait_ge(xT_ready, KT)
                pre_norm(0, "x0")
                for p in range(AHEAD):
                    split(p)
                ffn(0)
                dve.wait_ge(ada_evac, ADA_T // 2)
                post_norm(0, "y1")
                pre_norm(1, "x1")

                def both(rows_of):
                    for d in range(2):
                        yield d, rows_of[d]

                def gate_part(m):
                    if m == 0:
                        dve.wait_ge(pe_piece, P_GATES + U)
                        dve.wait_ge(cols_loaded, 16 * N_COLS)
                        dve.wait_ge(x_spilled, 16)
                        dve.tensor_scalar(r_u, psum[0][:, 0:TOK], gcol[:, 0:1], gcol[:, 1:2], ALU.add, ALU.mult).then_inc(gate_read, 1)
                        dve.tensor_scalar(r_li, psum[1][:, 0:TOK], gcol[:, 2:3], None, ALU.add).then_inc(gate_read, 1)
                        dve.wait_ge(gate_read, 2)
                        dve.scalar_tensor_tensor(out=r_t, in0=r_u, scalar=-1.0, in1=r_u, op0=ALU.mult, op1=ALU.max).then_inc(dve_row, 1)
                    if m == 1:
                        dve.wait_ge(act_row, 1)
                        dve.tensor_scalar(r_d, r_e, 1.0, None, ALU.add).then_inc(dve_row, 1)
                        dve.wait_ge(dve_row, 2)
                        link(dve.tensor_scalar(r_t, r_d, -1.0, None, ALU.add))
                        link(dve.tensor_scalar(r_q, r_t, 1e-30, None, ALU.max))
                        link(dve.reciprocal(r_cs, r_q))
                        link(dve.tensor_scalar(r_T4, r_t, 0.0, None, ALU.is_equal))
                    if m == 2:
                        dve.wait_ge(act_row, 3)
                        link(dve.tensor_tensor(r_q, r_lw, r_e, ALU.mult))
                        link(dve.tensor_tensor(r_t, r_q, r_cs, ALU.mult))
                        link(dve.tensor_tensor(r_q, r_T4, r_e, ALU.mult))
                        link(dve.tensor_tensor(r_lw, r_t, r_q, ALU.add))
                        link(dve.scalar_tensor_tensor(out=r_sp, in0=r_u, scalar=0.0, in1=r_lw, op0=ALU.max, op1=ALU.add))
                        link(dve.tensor_scalar(gcol[:, 4:5], gcol[:, 4:5], -1.0, None, ALU.mult))
                        link(dve.tensor_scalar(r_d, r_sp, gcol[:, 4:5], None, ALU.mult))
                        for d, (a, b) in both(SCAN):
                            for c in range(NCH):
                                t = run(d, c)
                                last = dve.tensor_tensor_scan(r_cs[a:b, t], ones[a:b, :], r_d[a:b, t], 0.0, ALU.mult, ALU.add)
                        link(last)
                        link(dve.tensor_tensor(r_Q, r_li, r_cs, ALU.subtract))
                        link(dve.tensor_copy(r_P, r_cs))
                    if m == 3:
                        for d in range(2):
                            a, b = (64 * d, 64 * d + 32)
                            for c in ((0, 1, 2), (0, 2, 1))[d]:
                                t = run(d, c)
                                init = 0.0 if c == 0 else gcol[a:b, 6 + c:7 + c]
                                link(dve.tensor_tensor_scan(r_t[a:b, t], r_Q[a:b, t], r_Q[a:b, t], init, ALU.max, ALU.max))
                                if c == (1, 2)[d]:
                                    e = last_of(d, c)
                                    link(dve.tensor_tensor(gcol[a:b, 9 - c:10 - c], r_cs[a:b, e:e + 1], r_t[a:b, e:e + 1], ALU.add))
                            link(dve.tensor_scalar(r_P[a:b, :], r_t[a:b, :], -1.0, None, ALU.mult))
                        for d, (a, b) in both(SCAN):
                            link(dve.tensor_copy(gcol[a:b, 9:12], r_P[a:b, last_of(d, 0):TOK:P]))
                        dve.tensor_tensor(r_li, r_P, r_cs, ALU.subtract).then_inc(dve_row, 1)
                    if m == 4:
                        dve.wait_ge(act_row, 4)
                        dve.wait_ge(dve_row, 3)
                        for d in range(2):
                            a, b = ROW_SS[d], ROW_SS[d] + 32
                            link(dve.tensor_tensor(r_W[a:b, :], r_W[a:b, :], r_sp[a:b, :], ALU.mult))
                            link(dve.tensor_copy(r_T4[a:b, :], r_sp[a:b, :]))
                        for d, (a, b) in both(SCAN):
                            e, e0 = last_of(d, (1, 2)[d]), last_of(d, 0)
                            link(dve.tensor_copy(gcol[a:b, 12:13], r_E[a:b, e:e + 1]))
                            link(dve.tensor_tensor(gcol[a:b, 13:14], r_cs[a:b, e0:e0 + 1], r_P[a:b, e0:e0 + 1], ALU.subtract))
                        dve.tensor_scalar(r_t[:, 0:P], idn[:, :], gcol[:, 12:13], None, ALU.mult).then_inc(gates_done, 1)

                def run(d, c):
                    if d == 0:
                        return slice(P * c, P * c + P)
                    return slice(P * c + P - 1, P * c - 1 if c else None, -1)

                def last_of(d, c):
                    return P * c + (0 if d else P - 1)

                def conv(n, f):
                    t = 2 * XBC_ORDER[n] + f
                    src, dst = psum[(0 if n % 2 else 2) + f], cv[:, f, :]

                    def tap(k):
                        return vecT[:, V_CONVW + k * XBC_T + t:V_CONVW + k * XBC_T + t + 1]

                    if n:
                        dve.wait_ge(conv_silu, 2 * n + f - 1)
                    link(dve.tensor_scalar(dst, src[:, 0:TOK], tap(CONV_K // 2), vecT[:, V_CONVB + t:V_CONVB + t + 1], ALU.mult, ALU.add))
                    for k in (0, 1, 3, 4):
                        s = k - CONV_K // 2
                        for t0, t1, width in ((0, TOK_P, TOK_P), (TOK_P, TOK, GRID_W)):
                            a, b = max(0, -s), width - max(0, s)
                            o = dst[:, t0:t1].rearrange("p (r w) -> p r w", w=width)[:, :, a:b]
                            x = src[:, t0:t1].rearrange("p (r w) -> p r w", w=width)[:, :, a + s:b + s]
                            last = dve.scalar_tensor_tensor(out=o, in0=x, scalar=tap(k), in1=o, op0=ALU.mult, op1=ALU.add)
                            if k == 4 and t0:
                                last.then_inc(conv_done, 1)
                            elif t0:
                                link(last)

                def to_tok(n):
                    for f in range(2):
                        m = 2 * TOK_UNITS.index(n) + f
                        dve.wait_ge(conv_tr, m + 1)
                        c0 = f * P if n == UNIT_B else 2 * P * XBC_ORDER[n] + f * P
                        dst = (bm_tok if n == UNIT_B else xs_tok)[:, :, c0:c0 + P]
                        dve.tensor_copy(dst, psum[4 + f][:, 0:TOK].rearrange("p (c n) -> p c n", c=NCH)).then_inc(tok_ready, 1)

                for p in range(P_GATES, P_HEADS):
                    split(p + AHEAD)
                    j = p - P_XBC
                    if j >= 0 and j % U == U - 1:
                        n = j // U
                        dve.wait_ge(pe_piece, p + 1)
                        for f in range(2):
                            conv(n, f)
                        if n - 1 in TOK_UNITS:
                            to_tok(n - 1)
                    if j in GATE_AT:
                        gate_part(GATE_AT[j])
                to_tok(XBC_T // 2 - 1)
                for kind in range(4):
                    dve.wait_ge(cols_tr, kind + 1)
                    dve.tensor_copy(cols[:, kind, :, :], psum[4 + kind][:, 0:TOK].rearrange("p (c r) -> p c r", c=NCH)).then_inc(cols_ready, 1)
                dve.wait_ge(dec_mm, 1)
                dve.tensor_copy(dbc[:, :], psum[2][:, 0:P]).then_inc(dec_ready, 1)
                for n in range(4):
                    d, half = divmod(n, 2)
                    dve.wait_ge(st_tr, n + 1)
                    dve.tensor_copy(ST[:, d, GRP_W * half:GRP_W * half + GRP_W], psum[half][:, :]).then_inc(st_ready, 1)

                dve.wait_ge(cols_ready, 4)
                dve.wait_ge(dec_ready, 1)
                dve.wait_ge(st_ready, 4)

                def by_head(v, n=8):
                    return v.unsqueeze(2).broadcast_to((P, n, SSM_P))

                def heads_of(v):
                    return v.rearrange("p (h q) -> p h q", q=SSM_P)

                for n, (g, c, d, step) in enumerate(SSM_STEPS):
                    carried, states = ssm_before(n)
                    r0 = ROW_SS[d] + 8 * g
                    mine = slice(GRP_W * g, GRP_W * g + GRP_W)
                    dve.wait_ge(ss_bc, n + 1)
                    if n:
                        dve.wait_ge(ss_y, n)
                    for h in range(8):
                        last = dve.scalar_tensor_tensor(out=seg[:, h, :], in0=psum[4 + h // 4][:, P * (h % 4):P * (h % 4) + P],
                                                        scalar=cols[:, C_Q, c, r0 + h:r0 + h + 1], in1=maskneg[:, d, :],
                                                        op0=ALU.add, op1=ALU.add)
                    last.then_inc(ss_seg, 1)
                    dve.wait_ge(ss_exp, n + 1)
                    dve.wait_ge(ss_cb, n + 1)
                    dve.tensor_tensor(seg[:, 0:4, :], seg[:, 0:4, :], cbs.unsqueeze(1).broadcast_to((P, 4, P)), ALU.mult).then_inc(ss_wd, 1)
                    dve.wait_ge(ss_y, n + 1)
                    dve.wait_ge(ss_x, n + 1)
                    if carried:
                        dve.wait_ge(ss_ypool, carried)
                    if n:
                        dve.wait_ge(ss_yacc, n)
                    dve.tensor_tensor(yacc[:, c, mine], yacc[:, c, mine], psum[7][:, :], ALU.add).then_inc(ss_yacc, 1)
                    if c:
                        dve.wait_ge(ss_int, carried + 1)
                        dve.tensor_tensor(heads_of(ytmp), heads_of(psum[6][:, :]), by_head(cols[:, C_E, c, r0:r0 + 8]),
                                          ALU.mult).then_inc(ss_tmp, 1)
                    if step < N_STATE:
                        if c:
                            link(dve.tensor_tensor(heads_of(stt_), heads_of(ST[:, d, mine]), by_head(dbc[:, r0:r0 + 8]), ALU.mult))
                            dve.wait_ge(ss_stm, states + 1)
                            dve.tensor_tensor(ST[:, d, mine], stt_, psum[6][:, :], ALU.add).then_inc(ss_state, 1)
                        else:
                            dve.wait_ge(ss_stm, states + 1)
                            stored = 2 * g + step
                            if stored:
                                dve.wait_ge(s_stored, 16 * stored)
                            dve.tensor_copy(s_out, psum[6][:, :]).then_inc(ss_state, 1)
                for t in range(KT // 2):
                    dve.wait_ge(yt_tr, t + 1)
                    dve.tensor_copy(y[:, KT // 2 + t, :], psum[4 + t % 2][:, 0:TOK]).then_inc(yt_ready, 1)
                dve.wait_ge(yt_ready, KT // 2)

                with dve.Fori(0, HEADS // 2) as i:
                    own.enter(i, LINKS_PAIR)

                    def kv(hh):
                        ktok, va = hset[hh][3:5]
                        for n, dst in enumerate((ktok, va)):
                            for f in range(2):
                                dve.wait_ge(kv_tr, at(4 * hh + 2 * n + f + 1, i, 8))
                                dve.tensor_copy(dst[:, :, f * P:f * P + P], psum[4 + f][:, 0:TOK].rearrange("p (c n) -> p c n", c=NCH)).then_inc(kv_tok, 1)

                    def start(hh):
                        for d in range(2):
                            row = i * 2 + (ROW_ML[d] + hh)
                            dve.tensor_scalar(mrow[:, d, :], r_P, idn[:, bass.ds(row, 1)], None, ALU.mult).then_inc(row_ready, 1)

                    def a(hh, n):
                        c, d = STEPS[n]
                        row = i * 2 + (ROW_ML[d] + hh)
                        if n == 0:
                            dve.wait_ge(m_bc, at(hh + 1, i, 2))
                        else:
                            dve.wait_ge(m_s, at(6 * hh + n, i, 12))
                        dve.scalar_tensor_tensor(out=ex, in0=psum[4 + d][:, P * c:P * c + P], scalar=cols[:, C_Q, c, bass.ds(row, 1)],
                                                 in1=maskneg[:, d, :], op0=ALU.add, op1=ALU.add).then_inc(m_seg, 1)
                        dve.wait_ge(m_exp, at(6 * hh + n + 1, i, 12))
                        dve.wait_ge(m_qk, at(6 * hh + n + 1, i, 12))
                        dve.tensor_tensor(sT, ex, psum[6][:, 0:P], ALU.mult).then_inc(m_s, 1)

                    def b(hh, n):
                        c, d = STEPS[n]
                        row = i * 2 + (ROW_ML[d] + hh)
                        dve.wait_ge(m_num, at(6 * hh + n + 1, i, 12))
                        if c:
                            dve.wait_ge(m_ti, at(4 * hh + n - 1, i, 8))
                            link(dve.tensor_tensor(num, ti, psum[7][:, 0:VW], ALU.add))
                        else:
                            link(dve.tensor_copy(num, psum[7][:, 0:VW]))
                        link(dve.tensor_scalar(small[:, 2:3], num[:, DH:VW], -1.0, cols[:, C_T, c, bass.ds(row, 1)], ALU.mult, ALU.max))
                        link(dve.tensor_tensor(small[:, 0:1], num[:, DH:VW], small[:, 2:3], ALU.max))
                        link(dve.reciprocal(small[:, 1:2], small[:, 0:1]))
                        if n == 0 and hh:
                            dve.wait_ge(h_tr, at(1, i, 2))
                        if n in FIRST_VISIT:
                            dve.tensor_scalar(hacc[:, c, :], num[:, 0:DH], small[:, 1:2], None, ALU.mult).then_inc(m_h, 1)
                        else:
                            dve.scalar_tensor_tensor(out=hacc[:, c, :], in0=num[:, 0:DH], scalar=small[:, 1:2], in1=hacc[:, c, :],
                                                     op0=ALU.mult, op1=ALU.add).then_inc(m_h, 1)
                        dve.wait_ge(m_h, at(6 * hh + n + 1, i, 12))

                    def c_(hh, n):
                        c, d = STEPS[n]
                        row = i * 2 + (ROW_ML[d] + hh)
                        dve.wait_ge(m_upd, at(N_STATE * hh + n + 1, i, 8))
                        if n == 2:
                            dve.wait_ge(c_loaded[hh], at(64, i, 64))
                        for k in range(2):
                            if c:
                                last = dve.scalar_tensor_tensor(out=cst[hh][:, d, k, :], in0=cst[hh][:, d, k, :], scalar=dbc[:, bass.ds(row, 1)],
                                                                in1=psum[7 - k][:, 0:VW], op0=ALU.mult, op1=ALU.add)
                            else:
                                last = dve.tensor_copy(c_out[:, k, :], psum[7 - k][:, 0:VW])
                        last.then_inc(m_c, 1)

                    def end(hh):
                        for c in range(NCH):
                            last = dve.bn_stats(stats[:, c, :], hacc[:, c, :])
                        link(last)
                        dve.tensor_copy(small[:, 3:4], stats[:, 2, 0:1])
                        for c in range(NCH):
                            last = dve.bn_aggr(small[:, 12 + 2 * c:14 + 2 * c], stats[:, c, :])
                        link(last)
                        dve.tensor_copy(small[:, 20:23], small[:, 13:18:2]).then_inc(h_var, 1)
                        dve.wait_ge(h_std, at(hh + 1, i, 2))
                        link(dve.reciprocal(small[:, 28:31], small[:, 24:27]))
                        for c in range(NCH):
                            dve.tensor_scalar(hacc[:, c, :], hacc[:, c, :], small[:, 12 + 2 * c:13 + 2 * c], small[:, 28 + c:29 + c],
                                              ALU.subtract, ALU.mult).then_inc(h_norm, 1)
                        dve.wait_ge(h_tr, at(hh + 1, i, 2))
                        dve.wait_ge(og_ready, at(2 * hh + 2, i, 4))
                        for k in range(2):
                            t = i * 4 + (2 * hh + k)
                            dve.scalar_tensor_tensor(out=y[:, bass.ds(t, 1), :].rearrange("p a t -> p (a t)"), in0=psum[4 + k][:, 0:TOK],
                                                     scalar=vecT[:, bass.ds(t + V_MLG, 1)], in1=sigo[hh][:, k, :], op0=ALU.mult,
                                                     op1=ALU.mult).then_inc(mix_ready, 1)

                    tasks = {"kv": kv, "start": start, "end": end, "a": a, "b": b, "c": c_}
                    for j, (col, hh, q) in enumerate(PAIR_ORDER):
                        split(P_HEADS + j + AHEAD, i, PAIR)
                        if q == U - 1:
                            b0 = 2 * ((j // U) % 2)
                            if col in (COL_Q, COL_K, COL_V):
                                dst = hset[hh][(COL_Q, COL_K, COL_V).index(col)]
                                dve.wait_ge(pe_piece, at(P_HEADS + j + 1, i, PAIR))
                                for f in range(2):
                                    if col == COL_K:
                                        dve.tensor_scalar(dst[:, f, :], psum[b0 + f][:, 0:TOK], DH ** -0.5, None, ALU.mult).then_inc(qkv_ready, 1)
                                    else:
                                        dve.tensor_copy(dst[:, f, :], psum[b0 + f][:, 0:TOK]).then_inc(qkv_ready, 1)
                            elif col == COL_Z:
                                for f in range(2):
                                    dve.wait_ge(z_silu, at(2 * hh + f + 1, i, 4))
                                    t = i * 4 + (KT // 2 + 2 * hh + f)
                                    tile = y[:, bass.ds(t, 1), :].rearrange("p a t -> p (a t)")
                                    dve.tensor_tensor(tile, tile, psum[b0 + f][:, 0:TOK], ALU.mult).then_inc(z_done, 1)
                        for kind, thh, n in core_tasks(j):
                            tasks[kind](thh) if n is None else tasks[kind](thh, n)
                own.leave(HEADS // 2)

                dve.wait_ge(z_done, 2 * HEADS)
                inverse_root("ssm")
                for k in range(KT // 2, KT):
                    g = vecT[:, V_SSG + k - KT // 2:V_SSG + k - KT // 2 + 1]
                    dve.scalar_tensor_tensor(out=y[:, k, :], in0=y[:, k, :], scalar=g, in1=psum[2][:, 0:TOK],
                                             op0=ALU.mult, op1=ALU.mult).then_inc(ms_scaled, 1)
                for t in range(D // PC):
                    for q in range(U):
                        split(P_OUT + U * t + q + AHEAD)
                    dve.wait_ge(pe_piece, P_OUT + U * t + U)
                    for f in range(2):
                        dve.tensor_copy(y[:, 2 * t + f, :], psum[(4 if t % 2 else 0) + f][:, 0:TOK]).then_inc(y_done, 1)
                dve.wait_ge(y_done, KT * (FFN_IT + 1))
                post_norm(1, "y2")
                pre_norm(2, "x2")
                ffn(1)
                dve.wait_ge(y_done, KT * (2 * FFN_IT + 1))
                post_norm(2, "y3")
                for n in range(0, NCH * (KT // 4), 2):
                    kk, c = divmod(n, NCH)
                    dve.wait_ge(out_tr, n + 1)
                    dve.tensor_copy(out_tok[:, c, 512 * kk:512 * kk + 512], psum[4 + n % 2][:, :]).then_inc(out_ready_dve, 1)

            @block.gpsimd
            def _(pool):
                own = Tally(pool, pool_step)
                link = own.link

                def split(p, i=None, per=0):
                    if p % 2 == 0 or p >= TOTAL:
                        return
                    pool.wait_ge(w_hi_ready, at(p + 1, i, per))
                    pool.tensor_tensor(w_lo[:, p % NS, :], w_raw[:, p % NR, :], w_hi[:, p % NS, :].bitcast(F32),
                                       ALU.subtract).then_inc(w_lo_pool, 1)

                def lo_of(done, src):
                    for k in range(KT):
                        pool.wait_ge(xn_hi_ready, done + k + 1)
                        pool.tensor_tensor(xn_lo[:, k, :], src(k), xn_hi[:, k, :].bitcast(F32), ALU.subtract).then_inc(xn_lo_ready, 1)

                def update(stage):
                    for k in range(KT):
                        pool.wait_ge(u_ready, KT * stage + k + 1)
                        pool.tensor_tensor(xT[:, k, :], xT[:, k, :], y[:, k, :], ALU.add).then_inc(x_updated, 1)

                def ffn(n):
                    def hid_lo_part(it, s, i):
                        for f in range(2):
                            m = 4 * (FFN_IT * n + it) + 2 * s + f
                            pool.wait_ge(hid_hi_ready, at(m + 1, i, 4))
                            pool.tensor_tensor(hid_lo[:, 2 * s + f, :], hidf[:, f, :], hid_hi[:, 2 * s + f, :].bitcast(F32),
                                               ALU.subtract).then_inc(hid_lo_ready, 1)

                    def step(i):
                        first = i is None
                        base, per = (ffn_first(n), 0) if first else (ffn_loop(n), FFN_PER)
                        for kind, s, j_loop, j_first in PARTS:
                            j0 = j_first if first else j_loop
                            if j0 is None:
                                continue
                            for q in range(DOWN if kind == "d" else U):
                                split(base + j0 + q + AHEAD, i, per)
                            if kind == "u":
                                hid_lo_part(0 if first else 1, s, i)

                    step(None)
                    with pool.Fori(0, FFN_IT - 1) as i:
                        step(i)
                    if n == 0:
                        pad_gates()
                    for j in range(DOWN):
                        split(ffn_first(n) + FFN_LEN - DOWN + j + AHEAD)

                def pad_gates():
                    pool.wait_ge(gw_loaded, 32)
                    pool.wait_ge(ada_used, U * ADA_T // 2)
                    link(pool.memset(gw_pad[:, :, :], 0.0))
                    for dst, src, n in ((ROW_ML[0], 2 * HEADS, HEADS), (ROW_ML[1], 3 * HEADS, HEADS),
                                        (ROW_SS[0], 4 * HEADS, SSM_H), (ROW_SS[1], 4 * HEADS + SSM_H, SSM_H),
                                        (P + ROW_ML[0], 0, HEADS), (P + ROW_ML[1], HEADS, HEADS)):
                        last = pool.tensor_copy(gw_pad[:, :, dst:dst + n], gw_small[:, :, src:src + n])
                    last.then_inc(gw_ready, 1)

                link(pool.memset(idn[:, :], 0.0))
                link(pool.affine_select(out=idn[:, :], in_=idn[:, :], compare_op=ALU.not_equal, fill=1.0, base=0,
                                        pattern=[[-1, P]], channel_multiplier=1))
                link(pool.memset(ones[:, :], 1.0))
                link(pool.memset(gcol[:, :], 0.0))
                link(pool.memset(gcol[:, 1:2], 1.0))
                link(pool.memset(gcol[0:32, 1:2], -1.0))
                link(pool.memset(gcol[64:96, 1:2], -1.0))
                link(pool.memset(maskneg[:, :, :], 0.0))
                for d in range(2):
                    sign = -1 if d else 1
                    link(pool.affine_select(out=maskneg[:, d, :], in_=maskneg[:, d, :], compare_op=ALU.is_ge, fill=MASKED, base=0,
                                            pattern=[[sign, P]], channel_multiplier=-sign))
                pool.memset(eps[:, :], EPS).then_inc(const_ready, 1)
                pool.wait_ge(xt_tr, KT)
                pool.memset(y[:, :, :], 0.0).then_inc(y_zeroed, 1)
                lo_of(0, lambda k: hn[:, k % 2, :])
                for p in range(AHEAD):
                    split(p)
                ffn(0)
                update(0)
                lo_of(KT, lambda k: hn[:, k % 2, :])
                for p in range(P_GATES, P_HEADS):
                    split(p + AHEAD)
                pool.wait_ge(cols_ready, 4)
                pool.wait_ge(tok_ready, 2 * len(TOK_UNITS))
                pool.wait_ge(cols_loaded, 16 * N_COLS)

                def by_head(v):
                    return v.unsqueeze(2).broadcast_to((P, 8, SSM_P))

                def heads_of(v):
                    return v.rearrange("p (h q) -> p h q", q=SSM_P)

                for n, (g, c, d, step) in enumerate(SSM_STEPS):
                    carried, states = ssm_before(n)
                    r0 = ROW_SS[d] + 8 * g
                    mine = slice(GRP_W * g, GRP_W * g + GRP_W)
                    x = heads_of(xs_tok[:, c, mine])
                    if n:
                        pool.wait_ge(ss_y, n)
                        if states:
                            pool.wait_ge(ss_stm, states)
                    last = pool.tensor_tensor(heads_of(xdt), x, by_head(cols[:, C_T, c, r0:r0 + 8]), ALU.mult)
                    if step < N_STATE:
                        last = pool.tensor_tensor(heads_of(xte), x, by_head(cols[:, C_W, c, r0:r0 + 8]), ALU.mult)
                    if step in FIRST_VISIT:
                        last = pool.tensor_tensor(heads_of(yacc[:, c, mine]), x, by_head(dsk[:, 8 * g:8 * g + 8]), ALU.mult)
                    last.then_inc(ss_x, 1)
                    pool.wait_ge(ss_exp, n + 1)
                    pool.wait_ge(ss_cb, n + 1)
                    pool.tensor_tensor(seg[:, 4:8, :], seg[:, 4:8, :], cbs.unsqueeze(1).broadcast_to((P, 4, P)), ALU.mult).then_inc(ss_wp, 1)
                    if c:
                        pool.wait_ge(ss_tmp, carried + 1)
                        pool.wait_ge(ss_yacc, n + 1)
                        pool.tensor_tensor(yacc[:, c, mine], yacc[:, c, mine], ytmp, ALU.add).then_inc(ss_ypool, 1)

                pool.wait_ge(ss_stm, ssm_before(len(SSM_STEPS))[1])
                for head in hset:
                    last = pool.memset(head[4][:, :, DH:VW], 1.0)
                last.then_inc(v_ones, 1)

                with pool.Fori(0, HEADS // 2) as i:
                    for j, (col, hh_, q) in enumerate(PAIR_ORDER):
                        split(P_HEADS + j + AHEAD, i, PAIR)
                        for kind, hh, n in core_tasks(j):
                            ktok, va = hset[hh][3:5]
                            if kind == "a" and n < N_STATE:
                                c, d = STEPS[n]
                                row = i * 2 + (ROW_ML[d] + hh)
                                if n == 0:
                                    pool.wait_ge(kv_tok, at(4 * hh + 4, i, 8))
                                if n or hh:
                                    pool.wait_ge(m_upd, at(N_STATE * hh + n, i, 8))
                                pool.tensor_tensor(wk, ktok[:, c, :], cols[:, C_W, c, bass.ds(row, 1)].broadcast_to((P, DH)),
                                                   ALU.mult).then_inc(m_wk, 1)
                lo_of(2 * KT, lambda k: y[:, k, :])
                for t in range(D // PC):
                    for q in range(U):
                        split(P_OUT + U * t + q + AHEAD)
                pool.wait_ge(x_back, 16)
                update(1)
                pool.wait_ge(x_updated, 2 * KT)
                pool.memset(y[:, :, :], 0.0).then_inc(y_zeroed, 1)
                lo_of(3 * KT, lambda k: hn[:, k % 2, :])
                ffn(1)
                update(2)


_INS = ['x_prompt', 'x_sample', 'state_mlstm_C', 'state_mlstm_n', 'state_mlstm_m', 'state_ssm', 'c', 'c_ctx', 'w_ada', 'b_ada',
        'norm_g', 'w_in', 'gate_bias', 'dt_bias', 'a_log', 'd_skip', 'conv_w', 'conv_b', 'ml_norm_g', 'ssm_norm_g', 'w_out',
        'ffn_w_gate', 'ffn_w_up', 'ffn_w_down']
_OUTS = [('y_prompt', (1, TOK_P, D)), ('y_sample', (1, TOK_S, D)), ('new_C', (1, 1, 2, HEADS, DH, DH)), ('new_n', (1, 1, 2, HEADS, DH)),
         ('new_m', (1, 1, 2, HEADS)), ('new_ssm', (1, 1, 2, SSM_H, SSM_P, SSM_N))]


def kernel(**inputs):
    import numpy as _np
    import concourse.bacc as _bacc
    from concourse.bass_utils import run_bass_kernel_spmd as _run

    nc = _bacc.Bacc("TRN2", target_bir_lowering=False, num_devices=1, dynamic_dma_scratch_size=1024)
    arrays, args = {}, {}
    for name in _INS:
        a = _np.ascontiguousarray(inputs[name])
        arrays[f"in_{name}_dram"] = a
        args[name] = nc.dram_tensor(f"in_{name}_dram", a.shape, mybir.dt.from_np(a.dtype), kind="ExternalInput").ap()
    for name, shape in _OUTS:
        args[name] = nc.dram_tensor(f"out_{name}_dram", shape, F32, kind="ExternalOutput").ap()
    hybrid_step(nc, args)
    r = _run(nc, [arrays], core_ids=[0])
    return tuple(r.results[0][f"out_{name}_dram"] for name, _ in _OUTS)
```

```python
from contextlib import ExitStack

import concourse.bass as bass
from concourse import mybir

ALU = mybir.AluOpType
ACT = mybir.ActivationFunctionType
F32 = mybir.dt.float32
F32R = mybir.dt.float32r

P = 128
D = 2048
KT = D // P
TOK_P, TOK_S = 128, 256
TOK = TOK_P + TOK_S
NCH = TOK // P
GROUPS = ((0, TOK_P), (TOK_P, TOK))
D_FF = 256 * ((8 * D // 3 + 255) // 256)
HEADS = 4
ML_W = D // 2
DH = ML_W // HEADS
SSM_W = D - ML_W
SSM_P = 64
SSM_H = SSM_W // SSM_P
SSM_N = 128
SSM_G = 2
GRP_W = SSM_W // SSM_G
CONV_K = 5
GRID_W = 64
N_MOD = 9
EPS = 1e-6
COL_Q, COL_K, COL_V, COL_O = 0, ML_W, 2 * ML_W, 3 * ML_W
COL_IG = 4 * ML_W
COL_FG = COL_IG + 2 * HEADS
COL_Z = COL_FG + 2 * HEADS
COL_XBC = COL_Z + SSM_W
COL_DT = COL_XBC + SSM_W + 2 * SSM_G * SSM_N
XBC_T = (SSM_W + 2 * SSM_G * SSM_N) // P

PK, PC = 4, 256
PW = PK * PC
NR, NS, AHEAD = 8, 4, 3
U = KT // PK
FFN_IT = D_FF // 512
DOWN = D // PC
ADA_T = N_MOD * KT
ADA_STEP = 4
FFN_START = (4 * U + ADA_STEP * U, 4 * U)
FFN_PER = (4 * U + DOWN + ADA_STEP * U, 4 * U + DOWN)
FFN_LEN = [FFN_START[n] + (FFN_IT - 1) * FFN_PER[n] + DOWN for n in range(2)]
ADA_FIRST = KT
ADA_SSM = ADA_T // 2 - ADA_FIRST - ADA_STEP * FFN_IT
FFN1 = ADA_FIRST * U
P_GATES = FFN1 + FFN_LEN[0]
P_XBC = P_GATES + U
P_SSM = P_XBC + (XBC_T // 2) * U
P_HEADS = P_SSM + ADA_SSM * U
PAIR = 2 * 5 * U
P_OUT = P_HEADS + (HEADS // 2) * PAIR
FFN2 = P_OUT + (D // PC) * U
TOTAL = FFN2 + FFN_LEN[1]


def ffn_pieces(n, first):
    main = [(kind, s, q) for kind, s in (("g", 0), ("d", 0), ("u", 0), ("g", 1), ("u", 1)) if kind != "d" or not first
            for q in range(DOWN if kind == "d" else U)]
    ada = [("a", k, q) for k in range(ADA_STEP if n == 0 else 0) for q in range(U)]
    out, done = [], 0
    for m, piece in enumerate(main):
        upto = (m + 1) * len(ada) // len(main)
        out += ada[done:upto] + [piece]
        done = upto
    return out


ROW_ML = (0, 64)
ROW_SS = (32, 96)
SCAN = ((0, 64), (64, 128))
MASKED = -1e30

STEPS = ((0, 0), (0, 1), (1, 0), (2, 1), (2, 0), (1, 1))
N_STATE = 4
FIRST_VISIT = (0, 2, 3)

ADA_START = [ADA_FIRST // 2 * (v % 2) + v // 2 for v in range(ADA_FIRST)]
PAIR_AT = 9

XBC_ORDER = (4, 5, 0, 1, 2, 3)
UNIT_B, UNIT_C = 0, 1
TOK_UNITS = (0, 2, 3, 4, 5)
GATE_AT = {1: 0, 5: 1, 9: 2, 12: 3, 17: 4}

PAIR_ORDER = [(col, hh, q) for col, hh in (
    (COL_Q, 0), (COL_K, 0), (COL_V, 0), (COL_Q, 1), (COL_K, 1), (COL_V, 1), (COL_O, 0), (COL_O, 1), (COL_Z, 0), (COL_Z, 1))
    for q in range(U)]
CORE_AT = {12: ("kv", 0), 13: ("start", 0), 14: ("a", 0, 0), 15: ("b", 0, 0), 16: ("c", 0, 0, "a", 0, 1), 17: ("b", 0, 1),
           18: ("c", 0, 1, "a", 0, 2), 19: ("b", 0, 2), 20: ("c", 0, 2, "a", 0, 3), 21: ("b", 0, 3),
           22: ("c", 0, 3, "a", 0, 4), 23: ("b", 0, 4), 24: ("a", 0, 5), 25: ("b", 0, 5), 26: ("kv", 1), 27: ("end", 0),
           28: ("start", 1), 29: ("a", 1, 0), 30: ("b", 1, 0), 31: ("c", 1, 0, "a", 1, 1), 32: ("b", 1, 1),
           33: ("c", 1, 1, "a", 1, 2), 34: ("b", 1, 2), 35: ("c", 1, 2, "a", 1, 3), 36: ("b", 1, 3),
           37: ("c", 1, 3, "a", 1, 4), 38: ("b", 1, 4), 39: ("a", 1, 5, "b", 1, 5, "end", 1)}


def core_tasks(j):
    out, rest = [], list(CORE_AT.get(j, ()))
    while rest:
        kind, hh = rest[:2]
        n = rest[2] if kind in "abc" else None
        rest = rest[3:] if kind in "abc" else rest[2:]
        out.append((kind, hh, n))
    return out


V_NORM, V_CONVB, V_MLG, V_SSG = 0, 96, 108, 116
V_CONVW, V_BADA, V_CCTX, V_C = 128, 256, 400, 416
VEC_ROWS = ((124, 0), (60, 128), (128, 256), (16, 384), (32, V_CCTX))
N_VEC = 7
N_COLS = 11
LINKS_PAIR = 2 * (6 * 4 + 3)


def at(const, i, per):
    return const if i is None else i * per + const


class Tally:

    def __init__(self, eng, sem):
        self.eng, self.sem, self.n, self.i, self.per = eng, sem, 0, None, 0

    def enter(self, i, per):
        self.start, self.i, self.per = self.n, i, per

    def leave(self, times):
        assert self.n - self.start == self.per, (self.n - self.start, self.per)
        self.n, self.i = self.start + times * self.per, None

    def link(self, ins):
        ins.then_inc(self.sem, 1)
        self.n += 1
        self.eng.wait_ge(self.sem, at(self.n, self.i, self.per))


def hybrid_step(nc, A):
    with ExitStack() as ctx:
        def sb(name, shape, dt=F32):
            return ctx.enter_context(nc.sbuf_tensor(name, shape, dt))

        def sem(name):
            return ctx.enter_context(nc.semaphore(name))

        xT = sb("xT", [P, KT, TOK])
        xn_hi = sb("xn_hi", [P, KT, TOK], F32R)
        xn_lo = sb("xn_lo", [P, KT, TOK], F32R)
        y = sb("y", [P, KT, TOK])
        hid_hi = sb("hid_hi", [P, 4, TOK], F32R)
        hid_lo = sb("hid_lo", [P, 4, TOK], F32R)
        w_raw = sb("w_raw", [P, NR, PW])
        w_hi = sb("w_hi", [P, NS, PW], F32R)
        w_lo = sb("w_lo", [P, NS, PW], F32R)
        idn = sb("idn", [P, P])
        ones = sb("ones", [P, P])
        maskneg = sb("maskneg", [P, 2, P])
        vecT = sb("vecT", [P, 432])
        modT = sb("modT", [P, ADA_T, 2])
        cT = sb("cT", [P, KT, 2])
        c4 = sb("c4", [P, KT, 4], F32R)
        ada_row = sb("ada_row", [P, PC])
        sel = sb("sel", [P, 2])
        coefA = sb("coefA", [P, KT, 2])
        coefG = sb("coefG", [P, KT, 2])
        eps = sb("eps", [P, 1])
        gcol = sb("gcol", [P, 16])
        dsk = sb("dsk", [P, SSM_H])
        dbc = sb("dbc", [P, P])
        small = sb("small", [P, 32])
        stats = sb("stats", [P, NCH, 6])
        AM = sb("AM", [P, 43 * 256])
        AX = xT[:, :, :].rearrange("p k t -> p (k t)")
        psum = [ctx.enter_context(nc.psum_tensor(f"bank{b}", [P, 512], F32)) for b in range(8)]

        def am(kb, n):
            return AM[:, int(kb * 256):int(kb * 256) + n]

        def ax(kb, n):
            return AX[:, int(kb * 256):int(kb * 256) + n]

        sq = am(16, 2 * TOK).rearrange("p (s t) -> p s t", s=2)
        std = am(19, TOK)
        xt = am(20.5, 2 * TOK).rearrange("p (s t) -> p s t", s=2)
        hn = am(23.5, 2 * TOK).rearrange("p (s t) -> p s t", s=2)
        sg = am(27, 2 * TOK).rearrange("p (s t) -> p s t", s=2)
        hidf = am(30, 2 * TOK).rearrange("p (s t) -> p s t", s=2)
        x_tok = y[:, :, :].rearrange("p k t -> p (k t)").rearrange("p (c n) -> p c n", c=NCH)
        vec_rows = am(33, 5 * P).rearrange("p (s n) -> p s n", s=5)
        out_tok = am(0, NCH * D).rearrange("p (c n) -> p c n", c=NCH)
        gw_small = am(36, KT * 48).rearrange("p (k n) -> p k n", k=KT)
        gw_pad = am(0, KT * PC).rearrange("p (k n) -> p k n", k=KT)
        rows = [ax(1.5 * r, TOK) for r in range(13)]
        r_u, r_e, r_lw, r_d, r_q, r_sp, r_cs, r_Q, r_E, r_W, r_T4, r_li, r_t = rows
        r_P = ax(22.5, TOK)
        cols = am(15.25, 4 * NCH * P).rearrange("p (q c r) -> p q c r", q=4, c=NCH)
        C_Q, C_E, C_W, C_T = range(4)
        xs_tok = am(0, NCH * SSM_W).rearrange("p (c n) -> p c n", c=NCH)
        bm_tok = am(12, NCH * SSM_G * SSM_N).rearrange("p (c n) -> p c n", c=NCH)
        bcT = am(21.25, 4 * TOK).rearrange("p (s t) -> p s t", s=4)
        cv = am(27.25, 2 * TOK).rearrange("p (s t) -> p s t", s=2)
        cvs = am(30.25, 2 * TOK).rearrange("p (s t) -> p s t", s=2)
        ST = am(33.5, 2 * SSM_W).rearrange("p (d n) -> p d n", d=2)
        seg = ax(0, 8 * P).rearrange("p (h t) -> p h t", h=8)
        xdt = ax(4, GRP_W)
        xte = ax(6, GRP_W)
        cbs = ax(8, P)
        stt_ = ax(8.5, GRP_W)
        s_out = ax(10.5, GRP_W)
        s_raw = ax(12.5, 2 * 8 * P).rearrange("p (d j n) -> p d j n", d=2, j=8)
        ytmp = ax(20.5, GRP_W)
        yacc = y[:, 0:KT // 2, :].rearrange("p k t -> p (k t)").rearrange("p (c n) -> p c n", c=NCH)
        VW = DH + 1
        def head_set(v):
            a = v.rearrange("p n -> p n")
            qT = a[:, 0:2 * TOK].rearrange("p (s t) -> p s t", s=2)
            kT = a[:, 2 * TOK:4 * TOK].rearrange("p (s t) -> p s t", s=2)
            vT = a[:, 4 * TOK:6 * TOK].rearrange("p (s t) -> p s t", s=2)
            ktok = a[:, 6 * TOK:8 * TOK].rearrange("p (c n) -> p c n", c=NCH)
            va = a[:, 8 * TOK:8 * TOK + NCH * VW].rearrange("p (c n) -> p c n", c=NCH)
            return qT, kT, vT, ktok, va
        HS_N = 8 * TOK + NCH * VW
        hset = [head_set(am(0, HS_N)), head_set(ax(0, HS_N))]
        cst = [am(21.25 + 4.25 * s, 2 * 2 * VW).rearrange("p (d k n) -> p d k n", d=2, k=2) for s in range(2)]
        mrow = am(29.75, 2 * TOK).rearrange("p (d t) -> p d t", d=2)
        ex = am(32.75, P)
        sT = am(33.25, P)
        ti = am(33.75, VW)
        num = am(34.85, VW)
        wk = am(35.95, DH)
        hacc = am(37, NCH * DH).rearrange("p (c n) -> p c n", c=NCH)
        c_out = am(40, 2 * VW).rearrange("p (k n) -> p k n", k=2)
        sigo = [ax(15.2 + 3 * s, 2 * TOK).rearrange("p (k t) -> p k t", k=2) for s in range(2)]

        x_wait = nc.dram_tensor("x_wait", (P, KT * TOK), F32).ap()

        raw_loaded = [sem(f"raw_loaded{s}") for s in range(NR)]
        w_hi_ready, w_lo_dve, w_lo_pool, pe_piece = sem("w_hi_ready"), sem("w_lo_dve"), sem("w_lo_pool"), sem("pe_piece")
        ada_row_ready, ada_cols, ada_done = sem("ada_row_ready"), sem("ada_cols"), sem("ada_done")
        const_ready, pool_step, dve_step = sem("const_ready"), sem("pool_step"), sem("dve_step")
        x_loaded, cond_loaded, vec_loaded, cols_loaded, gw_loaded = sem("x_loaded"), sem("cond_loaded"), sem("vec_loaded"), sem("cols_loaded"), sem("gw_loaded")
        vec_tr, vec_ready, c_ready, c_lo_ready = sem("vec_tr"), sem("vec_ready"), sem("c_ready"), sem("c_lo_ready")
        xt_tr, xT_ready = sem("xt_tr"), sem("xT_ready")
        sq_ready, ss_mm, std_ready, xt_done = sem("sq_ready"), sem("ss_mm"), sem("std_ready"), sem("xt_done")
        hn_ready, xn_hi_ready, xn_lo_ready = sem("hn_ready"), sem("xn_hi_ready"), sem("xn_lo_ready")
        silu_ready, hid_ready = sem("silu_ready"), sem("hid_ready")
        hid_hi_ready, hid_lo_ready = sem("hid_hi_ready"), sem("hid_lo_ready")
        y_zeroed, y_done, u_ready, x_updated = sem("y_zeroed"), sem("y_done"), sem("u_ready"), sem("x_updated")
        out_tr, out_ready_dve, out_ready_act, out_stored = sem("out_tr"), sem("out_ready_dve"), sem("out_ready_act"), sem("out_stored")
        x_spilled, x_back = sem("x_spilled"), sem("x_back")
        gw_ready, gate_read, dve_row, act_row, gates_done = sem("gw_ready"), sem("gate_read"), sem("dve_row"), sem("act_row"), sem("gates_done")
        cols_tr, cols_ready, dec_mm, dec_ready, m_stored = sem("cols_tr"), sem("cols_ready"), sem("dec_mm"), sem("dec_ready"), sem("m_stored")
        conv_done, conv_silu, conv_tr, tok_ready = sem("conv_done"), sem("conv_silu"), sem("conv_tr"), sem("tok_ready")
        sr_loaded, st_tr, st_ready = sem("sr_loaded"), sem("st_tr"), sem("st_ready")
        ss_bc, ss_cb, ss_seg, ss_exp, ss_x = sem("ss_bc"), sem("ss_cb"), sem("ss_seg"), sem("ss_exp"), sem("ss_x")
        ss_wd, ss_wp, ss_y, ss_int, ss_yacc = sem("ss_wd"), sem("ss_wp"), sem("ss_y"), sem("ss_int"), sem("ss_yacc")
        ss_tmp, ss_ypool, ss_stm, ss_state, s_stored = sem("ss_tmp"), sem("ss_ypool"), sem("ss_stm"), sem("ss_state"), sem("s_stored")
        yt_tr, yt_ready = sem("yt_tr"), sem("yt_ready")
        qkv_ready, og_ready, z_silu, z_done = sem("qkv_ready"), sem("og_ready"), sem("z_silu"), sem("z_done")
        kv_tr, kv_tok, row_ready, m_bc, v_ones = sem("kv_tr"), sem("kv_tok"), sem("row_ready"), sem("m_bc"), sem("v_ones")
        c_loaded = [sem(f"c_loaded{s}") for s in range(2)]
        m_seg, m_exp, m_qk, m_s, m_num, m_int = sem("m_seg"), sem("m_exp"), sem("m_qk"), sem("m_s"), sem("m_num"), sem("m_int")
        m_ti, m_h, m_wk, m_upd, m_c, m_cstored = sem("m_ti"), sem("m_h"), sem("m_wk"), sem("m_upd"), sem("m_c"), sem("m_cstored")
        h_var, h_std, h_norm, h_tr, mix_ready, ms_scaled = sem("h_var"), sem("h_std"), sem("h_norm"), sem("h_tr"), sem("mix_ready"), sem("ms_scaled")

        def by_tile(w):
            return w.rearrange("(k p) n -> p k n", p=P)

        w_in = by_tile(A["w_in"][0])
        w_out = by_tile(A["w_out"][0])
        w_ada = by_tile(A["w_ada"][0])
        w_gate = [by_tile(A["ffn_w_gate"][0, n]) for n in range(2)]
        w_up = [by_tile(A["ffn_w_up"][0, n]) for n in range(2)]
        w_down = [by_tile(A["ffn_w_down"][0, n]) for n in range(2)]

        SQ, total = {}, 0
        for name, count in (("x0", KT), ("y1", KT), ("x1", KT), ("ssm", KT // 2), ("y2", KT), ("x2", KT), ("y3", KT)):
            SQ[name] = (total, count)
            total += count
        SQ_ORDER = list(SQ)
        SSM_STEPS = [(g, c, d, n) for g in range(SSM_G) for n, (c, d) in enumerate(STEPS)]

        def ssm_before(n):
            return (sum(1 for x in SSM_STEPS[:n] if x[1]), sum(1 for x in SSM_STEPS[:n] if x[3] < N_STATE))

        def ffn_first(n):
            return FFN2 if n else FFN1

        def ffn_loop(n):
            return ffn_first(n) + FFN_START[n]

        def ffn_tail(n):
            return ffn_first(n) + FFN_LEN[n] - DOWN

        def step_of(n, i):
            first = i is None
            base = ffn_first(n) if first else ffn_loop(n)
            return 0 if first else FFN_PER[n], [(base + j, *piece) for j, piece in enumerate(ffn_pieces(n, first))]

        def ada_unit(k, i):
            return ADA_FIRST + k + (0 if i is None else ADA_STEP)

        SUM_BANK, ROOT_BANK = psum[0], psum[5]
        ADA_BANKS, ADA_BANKS_SSM = (6, 7), (0, 1)

        with nc.Block() as block:

            @block.sync
            def _(sp):
                def load(p, src, i=None, per=0):
                    if p >= NR:
                        sp.wait_ge(w_lo_pool if p % 2 else w_lo_dve, at((p - NR) // 2 + 1, i, per // 2))
                    dst = w_raw[:, p % NR, :].rearrange("p (k n) -> p k n", k=PK)
                    sp.dma_start(dst, src).then_inc(raw_loaded[p % NR], 16)

                def block_of(w, c0, q):
                    return w[:, PK * q:PK * q + PK, bass.ds(c0, PC)]

                def load_ada(p, unit, i=None, per=0):
                    for q in range(U):
                        load(p + q, block_of(w_ada, unit * PC, q), i, per)

                def ffn_step(n, i):
                    per, pieces = step_of(n, i)
                    f0 = 0 if i is None else i * 512 + 512
                    u0 = ada_unit(0, i) if i is None else i * ADA_STEP + ada_unit(0, i)
                    for p, kind, s, q in pieces:
                        if kind == "a":
                            src = block_of(w_ada, (u0 + s) * PC, q)
                        elif kind == "d":
                            src = w_down[n][:, bass.ds(i * PK, PK), PC * q:PC * q + PC]
                        else:
                            src = block_of(w_gate[n] if kind == "g" else w_up[n], f0 + PC * s, q)
                        load(p, src, i, per)

                def ffn(n):
                    ffn_step(n, None)
                    with sp.Fori(0, FFN_IT - 1) as i:
                        ffn_step(n, i)
                    for j in range(DOWN):
                        load(ffn_tail(n) + j, w_down[n][:, D_FF // P - PK:, PC * j:PC * j + PC])

                for v, unit in enumerate(ADA_START):
                    if v == 2:
                        sp.dma_start(x_tok[:, 0, :], A["x_prompt"][0]).then_inc(x_loaded, 16)
                        sp.dma_start(x_tok[:, 1:3, :], A["x_sample"][0].rearrange("(c p) n -> p c n", p=P)).then_inc(x_loaded, 16)
                    load_ada(U * v, unit)
                ffn(0)
                sp.wait_ge(gw_ready, 1)
                for q in range(U):
                    load(P_GATES + q, gw_pad[:, PK * q:PK * q + PK, :])
                for n, t in enumerate(XBC_ORDER):
                    for q in range(U):
                        load(P_XBC + U * n + q, block_of(w_in, COL_XBC + PC * t, q))
                for n in range(ADA_SSM):
                    load_ada(P_SSM + U * n, ADA_T // 2 - ADA_SSM + n)
                with sp.Fori(0, HEADS // 2) as i:
                    for j, (col, hh, q) in enumerate(PAIR_ORDER):
                        load(P_HEADS + j, block_of(w_in, i * (2 * DH) + (col + DH * hh), q), i, PAIR)
                for t in range(D // PC):
                    for q in range(U):
                        load(P_OUT + U * t + q, block_of(w_out, PC * t, q))
                ffn(1)
                for kk in range(KT // 4):
                    for c in range(NCH):
                        n = NCH * kk + c
                        sp.wait_ge(out_ready_act if n % 2 else out_ready_dve, n // 2 + 1)
                        dst = A["y_prompt"][0] if c == 0 else A["y_sample"][0, P * (c - 1):P * c]
                        sp.dma_start(dst[:, 512 * kk:512 * kk + 512], out_tok[:, c, 512 * kk:512 * kk + 512]).then_inc(out_stored, 16)
                sp.wait_ge(out_stored, 16 * NCH * (KT // 4))
                sp.wait_ge(s_stored, 16 * 2 * SSM_G)
                sp.wait_ge(m_cstored, 32 * 2 * HEADS)
                sp.wait_ge(m_stored, 32)

            @block.tensor
            def _(pe):
                def wait_piece(p, i=None, per=0):
                    pe.wait_ge(w_lo_pool if p % 2 else w_lo_dve, at(p // 2 + 1, i, per // 2))

                def product(out, slot, off, hi, lo, start, stop):
                    wh = w_hi[:, slot, off:off + P]
                    pe.matmul(out, wh, hi, start=start, stop=False)
                    pe.matmul(out, wh, lo, start=False, stop=False)
                    return pe.matmul(out, w_lo[:, slot, off:off + P], hi, start=False, stop=stop)

                def unit_piece(p, q, b0, i=None, per=0, fresh=None):
                    wait_piece(p, i, per)
                    if fresh is not None:
                        pe.wait_ge(xn_lo_ready, fresh + PK * (q + 1))
                    for f in range(2):
                        for k in range(PK):
                            last = product(psum[b0 + f][:, 0:TOK], p % NS, k * PC + f * P, xn_hi[:, PK * q + k, :],
                                           xn_lo[:, PK * q + k, :], q == 0 and k == 0, q == U - 1 and k == PK - 1)
                    last.then_inc(pe_piece, 1)

                def ada_piece(p, q, unit, banks, i=None, per=0):
                    wait_piece(p, i, per)
                    if q == 0 and unit:
                        pe.wait_ge(ada_row_ready, at(unit, i, ADA_STEP))
                    rows = psum[banks[0]]
                    for k in range(PK):
                        w = slice(k * PC, k * PC + PC)
                        last_k = q == U - 1 and k == PK - 1
                        if not last_k:
                            pe.matmul(rows[0:4, 0:PC], c4[:, PK * q + k, :], w_hi[:, p % NS, w], start=(q == 0 and k == 0), stop=False)
                        last = pe.matmul(rows[0:2, 0:PC], c4[:, PK * q + k, 0:2], w_lo[:, p % NS, w], start=False, stop=False)
                        if last_k:
                            last = pe.matmul(rows[0:4, 0:PC], c4[:, PK * q + k, :], w_hi[:, p % NS, w], start=False, stop=True)
                    last.then_inc(pe_piece, 1)

                def ada_columns(unit, banks, i=None):
                    pe.wait_ge(ada_row_ready, at(unit + 1, i, ADA_STEP))
                    if unit:
                        pe.wait_ge(ada_done, at(unit, i, ADA_STEP))
                    for f in range(2):
                        last = pe.matmul(psum[banks[1]][:, 2 * f:2 * f + 2], ada_row[:, P * f:P * f + P], sel[:, :], start=True, stop=True)
                    last.then_inc(ada_cols, 1)

                def square_sum(name, k):
                    base, count = SQ[name]
                    pe.wait_ge(sq_ready, base + k + 1)
                    if k == 0 and base:
                        pe.wait_ge(std_ready, SQ_ORDER.index(name))
                    pe.matmul(SUM_BANK[:, 0:TOK], ones[:, :], sq[:, (base + k) % 2, :], start=(k == 0),
                              stop=(k == count - 1)).then_inc(ss_mm, 1)

                pe.wait_ge(const_ready, 1)
                pe.wait_ge(cond_loaded, 32)
                for r in (4, 0, 1, 2, 3):
                    n, col = VEC_ROWS[r]
                    if r == 0:
                        pe.wait_ge(vec_loaded, 16 * N_VEC)
                        pe.wait_ge(vec_ready, 1)
                    last = pe.transpose(psum[4][:, col:col + n], vec_rows[0:n, r, :], idn[0:n, 0:n])
                    if r >= 3:
                        last.then_inc(vec_tr, 1)
                pe.wait_ge(c_lo_ready, 1)
                for v in range(ADA_FIRST):
                    for q in range(U):
                        ada_piece(U * v + q, q, v, ADA_BANKS)
                        if q == 0 and v:
                            ada_columns(v - 1, ADA_BANKS)
                    for t in (2 * v - 2, 2 * v - 1):
                        if not 0 <= t < KT:
                            continue
                        if t == 0:
                            pe.wait_ge(x_loaded, 32)
                        if t >= 2:
                            pe.wait_ge(xT_ready, t - 1)
                        for c in range(NCH):
                            last = pe.transpose(psum[2 + t % 2][:, P * c:P * c + P], x_tok[:, c, P * t:P * t + P], idn[:, :])
                        last.then_inc(xt_tr, 1)
                        if t:
                            square_sum("x0", t - 1)
                    if 2 * v - 1 == KT - 1:
                        square_sum("x0", KT - 1)
                ada_columns(ADA_FIRST - 1, ADA_BANKS)

                def ffn(n):
                    tiles_before = KT * (FFN_IT * n) + (KT if n else 0)

                    def down_piece(p, j, it, i=None):
                        wait_piece(p, i, FFN_PER[n])
                        if j == 0:
                            pe.wait_ge(hid_lo_ready, at(4 * (FFN_IT * n + it + 1), i, 4))
                        if j >= 2:
                            pe.wait_ge(y_done, at(tiles_before + KT * it + 2 * j - 2, i, KT))
                        for f in range(2):
                            bank = (4 if j % 2 else 2) + f
                            for k in range(PK):
                                last = product(psum[bank][:, 0:TOK], p % NS, k * PC + f * P, hid_hi[:, k, :],
                                               hid_lo[:, k, :], k == 0, k == PK - 1)
                        last.then_inc(pe_piece, 1)

                    def step(i):
                        per, pieces = step_of(n, i)
                        first = i is None
                        pending = None
                        for p, kind, s, q in pieces:
                            read = 4 * (FFN_IT * n + (0 if first else 1)) + 2 * s
                            if kind == "g" and q == 0 and read:
                                pe.wait_ge(silu_ready, at(read, i, 4))
                            if kind == "u" and q == 0 and (s or first) and read:
                                pe.wait_ge(hid_ready, at(read, i, 4))
                            if kind == "u" and q == 0 and not first:
                                pe.wait_ge(y_done, at(tiles_before + (KT if s else KT - 2), i, KT))
                            if kind == "d":
                                down_piece(p, q, 0, i)
                            elif kind == "a":
                                ada_piece(p, q, ada_unit(s, i), ADA_BANKS, i, per)
                            else:
                                fresh = KT * (3 if n else 0) if first and (kind, s) == ("g", 0) else None
                                unit_piece(p, q, 0 if kind == "g" else 2, i, per, fresh)
                            if pending is not None:
                                ada_columns(pending, ADA_BANKS, i)
                                pending = None
                            if kind == "a" and q == U - 1:
                                pending = ada_unit(s, i)

                    step(None)
                    with pe.Fori(0, FFN_IT - 1) as i:
                        step(i)
                    name = "y3" if n else "y1"
                    for j in range(DOWN):
                        down_piece(ffn_tail(n) + j, j, FFN_IT - 1)
                        if j:
                            square_sum(name, 2 * j - 2)
                            square_sum(name, 2 * j - 1)
                    square_sum(name, KT - 2)
                    square_sum(name, KT - 1)

                ffn(0)
                for k in range(KT):
                    square_sum("x1", k)

                for q in range(U):
                    unit_piece(P_GATES + q, q, 0, fresh=KT)

                def conv_transposes(n):
                    for f in range(2):
                        m = 2 * TOK_UNITS.index(n) + f
                        pe.wait_ge(conv_silu, 2 * n + f + 1)
                        if m >= 2:
                            pe.wait_ge(tok_ready, m - 1)
                        src = bcT[:, f, :] if n == UNIT_B else cvs[:, f, :]
                        for c in range(NCH):
                            last = pe.transpose(psum[4 + f][:, P * c:P * c + P], src[:, P * c:P * c + P], idn[:, :])
                        last.then_inc(conv_tr, 1)

                for n in range(XBC_T // 2):
                    if n == 1:
                        pe.wait_ge(gate_read, 2)
                    elif n >= 2:
                        pe.wait_ge(conv_done, 2 * (n - 1))
                    for q in range(U):
                        unit_piece(P_XBC + U * n + q, q, 0 if n % 2 else 2)
                    if n - 1 in TOK_UNITS:
                        conv_transposes(n - 1)
                conv_transposes(XBC_T // 2 - 1)

                pe.wait_ge(gates_done, 1)
                pe.wait_ge(tok_ready, 2 * len(TOK_UNITS))
                pe.wait_ge(conv_done, XBC_T)
                for kind, src in enumerate((r_Q, r_E, r_W, r_T4)):
                    for c in range(NCH):
                        last = pe.transpose(psum[4 + kind][:, P * c:P * c + P], src[:, P * c:P * c + P], idn[:, :])
                    last.then_inc(cols_tr, 1)
                pe.matmul(psum[2][:, 0:P], ones[:, :], r_t[:, 0:P], start=True, stop=True).then_inc(dec_mm, 1)
                pe.wait_ge(sr_loaded, 32)
                for n in range(4):
                    d, half = divmod(n, 2)
                    if n >= 2:
                        pe.wait_ge(st_ready, n - 1)
                    for j in range(4):
                        last = pe.transpose(psum[half][:, P * j:P * j + P], s_raw[:, d, 4 * half + j, :], idn[:, :])
                    last.then_inc(st_tr, 1)

                pe.wait_ge(cols_ready, 4)
                pe.wait_ge(st_ready, 4)
                for n, (g, c, d, step) in enumerate(SSM_STEPS):
                    tok = slice(P * c, P * c + P)
                    carried, states = ssm_before(n)
                    if n:
                        pe.wait_ge(ss_seg, n)
                        if carried:
                            pe.wait_ge(ss_tmp, carried)
                        if states:
                            pe.wait_ge(ss_state, states)
                    for h in range(8):
                        r = ROW_SS[d] + 8 * g + h
                        pe.matmul(psum[4 + h // 4][:, P * (h % 4):P * (h % 4) + P], idn[:, r:r + 1].broadcast_to((P, P)),
                                  r_P[:, tok], start=True, stop=True)
                    pe.matmul(psum[6][:, 0:P], bcT[:, g, tok], bcT[:, 2 + g, tok], start=True, stop=True).then_inc(ss_bc, 1)
                    unit = ADA_T // 2 - ADA_SSM + n
                    for q in range(U):
                        ada_piece(P_SSM + U * n + q, q, unit, ADA_BANKS_SSM)
                    pe.wait_ge(ss_wd, n + 1)
                    pe.wait_ge(ss_wp, n + 1)
                    pe.wait_ge(ss_x, n + 1)
                    if n:
                        pe.wait_ge(ss_yacc, n)
                    for h in range(8):
                        last = pe.matmul(psum[7][:, SSM_P * h:SSM_P * h + SSM_P], seg[:, h, :],
                                         xdt[:, SSM_P * h:SSM_P * h + SSM_P], start=True, stop=True)
                    last.then_inc(ss_y, 1)
                    ada_columns(unit, ADA_BANKS_SSM)
                    pe.wait_ge(ss_cb, n + 1)
                    if c:
                        pe.matmul(psum[6][:, :], bcT[:, 2 + g, tok], ST[:, d, GRP_W * g:GRP_W * g + GRP_W],
                                  start=True, stop=True).then_inc(ss_int, 1)
                    if step < N_STATE:
                        if c:
                            pe.wait_ge(ss_tmp, carried + 1)
                            last = pe.matmul(psum[6][:, :], bm_tok[:, c, SSM_N * g:SSM_N * g + SSM_N], xte[:, :],
                                             start=True, stop=True)
                        else:
                            for j in range(4):
                                last = pe.matmul(psum[6][:, P * j:P * j + P], xte[:, P * j:P * j + P],
                                                 bm_tok[:, 0, SSM_N * g:SSM_N * g + SSM_N], start=True, stop=True)
                        last.then_inc(ss_stm, 1)

                pe.wait_ge(ss_yacc, len(SSM_STEPS))
                pe.wait_ge(ss_ypool, ssm_before(len(SSM_STEPS))[0])
                for t in range(KT // 2):
                    if t >= 2:
                        pe.wait_ge(yt_ready, t - 1)
                    for c in range(NCH):
                        last = pe.transpose(psum[4 + t % 2][:, P * c:P * c + P], yacc[:, c, P * t:P * t + P], idn[:, :])
                    last.then_inc(yt_tr, 1)
                pe.wait_ge(yt_ready, KT // 2)

                pe.wait_ge(dec_ready, 1)
                pe.wait_ge(v_ones, 1)
                with pe.Fori(0, HEADS // 2) as i:
                    def kv_transposes(hh):
                        qT, kT, vT, ktok, va = hset[hh]
                        if hh:
                            pe.wait_ge(m_seg, at(6, i, 12))
                        for n, src in enumerate((kT, vT)):
                            pe.wait_ge(qkv_ready, at(6 * hh + 4 + 2 * n, i, 12))
                            for f in range(2):
                                if n:
                                    pe.wait_ge(kv_tok, at(4 * hh + f + 1, i, 8))
                                for c in range(NCH):
                                    last = pe.transpose(psum[4 + f][:, P * c:P * c + P], src[:, f, P * c:P * c + P], idn[:, :])
                                last.then_inc(kv_tr, 1)

                    def core_start(hh):
                        pe.wait_ge(row_ready, at(2 * hh + 2, i, 4))
                        pe.wait_ge(kv_tok, at(4 * hh + 4, i, 8))
                        if hh:
                            pe.wait_ge(mix_ready, at(2, i, 4))
                        for d in range(2):
                            last = pe.matmul(psum[4 + d][:, 0:TOK], ones[:, :], mrow[:, d, :], start=True, stop=True)
                        last.then_inc(m_bc, 1)

                    def core_a(hh, n):
                        qT, kT, vT, ktok, va = hset[hh]
                        tok = slice(P * STEPS[n][0], P * STEPS[n][0] + P)
                        if n or hh:
                            pe.wait_ge(m_h, at(6 * hh + n, i, 12))
                            pe.wait_ge(m_c, at(N_STATE * hh + min(n, N_STATE), i, 8))
                        for k in range(2):
                            last = pe.matmul(psum[6][:, 0:P], kT[:, k, tok], qT[:, k, tok], start=(k == 0), stop=(k == 1))
                        last.then_inc(m_qk, 1)

                    def core_b(hh, n):
                        qT, kT, vT, ktok, va = hset[hh]
                        c, d = STEPS[n]
                        pe.wait_ge(m_s, at(6 * hh + n + 1, i, 12))
                        pe.matmul(psum[7][:, 0:VW], sT[:, :], va[:, c, :], start=True, stop=True).then_inc(m_num, 1)
                        if c:
                            if n == 2:
                                pe.wait_ge(c_loaded[hh], at(64, i, 64))
                            for k in range(2):
                                last = pe.matmul(psum[6][:, 0:VW], qT[:, k, P * c:P * c + P], cst[hh][:, d, k, :],
                                                 start=(k == 0), stop=(k == 1))
                            last.then_inc(m_int, 1)

                    def core_c(hh, n):
                        qT, kT, vT, ktok, va = hset[hh]
                        pe.wait_ge(m_wk, at(N_STATE * hh + n + 1, i, 8))
                        pe.wait_ge(m_h, at(6 * hh + n + 1, i, 12))
                        for k in range(2):
                            last = pe.matmul(psum[7 - k][:, 0:VW], wk[:, P * k:P * k + P], va[:, STEPS[n][0], :], start=True, stop=True)
                        last.then_inc(m_upd, 1)

                    def core_end(hh):
                        pe.wait_ge(h_norm, at(NCH * (hh + 1), i, 2 * NCH))
                        pe.wait_ge(kv_tok, at(8, i, 8))
                        for k in range(2):
                            for c in range(NCH):
                                last = pe.transpose(psum[4 + k][:, P * c:P * c + P], hacc[:, c, P * k:P * k + P], idn[:, :])
                        last.then_inc(h_tr, 1)

                    tasks = {"kv": kv_transposes, "start": core_start, "end": core_end, "a": core_a, "b": core_b, "c": core_c}
                    for j, (col, hh, q) in enumerate(PAIR_ORDER):
                        unit = j // U
                        if q == 0 and unit >= 2:
                            if unit < 8:
                                pe.wait_ge(qkv_ready, at(2 * (unit - 1), i, 12))
                            else:
                                pe.wait_ge(og_ready, at(2 * (unit - 7), i, 4))
                        unit_piece(P_HEADS + j, q, 2 * (unit % 2), i, PAIR)
                        for kind, thh, n in core_tasks(j):
                            tasks[kind](thh) if n is None else tasks[kind](thh, n)
                    pe.wait_ge(z_done, at(4, i, 4))
                    pe.wait_ge(mix_ready, at(4, i, 4))

                for k in range(KT // 2):
                    square_sum("ssm", k)
                for t in range(D // PC):
                    if t >= 2:
                        pe.wait_ge(y_done, KT * FFN_IT + 2 * (t - 1))
                    for q in range(U):
                        unit_piece(P_OUT + U * t + q, q, 4 if t % 2 else 2, fresh=None if t else 2 * KT)
                    if t:
                        square_sum("y2", 2 * t - 2)
                        square_sum("y2", 2 * t - 1)
                square_sum("y2", KT - 2)
                square_sum("y2", KT - 1)
                for k in range(KT):
                    square_sum("x2", k)
                ffn(1)
                for kk in range(KT // 4):
                    pe.wait_ge(x_updated, 2 * KT + 4 * kk + 4)
                    for c in range(NCH):
                        n = NCH * kk + c
                        if n >= 2:
                            pe.wait_ge(out_ready_act if n % 2 else out_ready_dve, n // 2)
                        for j in range(4):
                            last = pe.transpose(psum[2 + n % 2][:, P * j:P * j + P], xT[:, 4 * kk + j, P * c:P * c + P], idn[:, :])
                        last.then_inc(out_tr, 1)

            @block.scalar
            def _(act):
                def split(p, i=None, per=0):
                    if p >= TOTAL:
                        return
                    act.wait_ge(raw_loaded[p % NR], at(16 * (p // NR + 1), i, 16 * per // NR))
                    if p >= NS:
                        act.wait_ge(pe_piece, at(p - NS + 1, i, per))
                    act.activation(w_hi[:, p % NS, :], w_raw[:, p % NR, :], ACT.Copy).then_inc(w_hi_ready, 1)

                def square(name, k, src):
                    n = SQ[name][0] + k
                    if n >= 2:
                        act.wait_ge(ss_mm, n - 1)
                    act.activation(sq[:, n % 2, :], src, ACT.Square).then_inc(sq_ready, 1)

                def root(name, width):
                    base, count = SQ[name]
                    act.wait_ge(ss_mm, base + count)
                    act.activation(std[:, :], SUM_BANK[:, 0:TOK], ACT.Sqrt, bias=eps[:, 0:1], scale=1.0 / width).then_inc(std_ready, 1)

                def hi_of(stage, src, ready, first):
                    for k in range(KT):
                        act.wait_ge(ready, first + k + 1)
                        act.activation(xn_hi[:, k, :], src(k), ACT.Copy).then_inc(xn_hi_ready, 1)

                def ffn(n):
                    def posts(it, s, kind, p_end, i, per):
                        for f in range(2):
                            m = 4 * (FFN_IT * n + it) + 2 * s + f
                            if kind == "g":
                                if f == 0:
                                    act.wait_ge(pe_piece, at(p_end + 1, i, per))
                                if m >= 2:
                                    act.wait_ge(hid_ready, at(m - 1, i, 4))
                                act.activation(sg[:, f, :], psum[f][:, 0:TOK], ACT.Silu).then_inc(silu_ready, 1)
                            else:
                                act.wait_ge(hid_ready, at(m + 1, i, 4))
                                act.activation(hid_hi[:, 2 * s + f, :], hidf[:, f, :], ACT.Copy).then_inc(hid_hi_ready, 1)

                    def step(i):
                        per, pieces = step_of(n, i)
                        for p, kind, s, q in pieces:
                            split(p + AHEAD, i, per)
                            if kind in "gu" and q == U - 1:
                                posts(0 if i is None else 1, s, kind, p, i, per)

                    step(None)
                    with act.Fori(0, FFN_IT - 1) as i:
                        step(i)
                    name = "y3" if n else "y1"
                    added = KT * (FFN_IT * (n + 1) - 1) + (KT if n else 0)
                    for j in range(DOWN):
                        split(ffn_tail(n) + j + AHEAD)
                        for k in (2 * j, 2 * j + 1):
                            act.wait_ge(y_done, added + k + 1)
                            square(name, k, y[:, k, :])
                    root(name, D)

                for n, src in enumerate((A["c_ctx"], A["c"][0])):
                    act.dma_start(vec_rows[KT * n:KT * n + KT, 4, :], src.rearrange("(k p) -> k p", p=P)).then_inc(cond_loaded, 16)
                for n, (rows, block_, src) in enumerate((
                        ((0, 96), 0, A["norm_g"][0].rearrange("j (k p) -> (j k) p", p=P)),
                        ((96, 108), 0, A["conv_b"][0].rearrange("(k p) -> k p", p=P)),
                        ((108, 116), 0, A["ml_norm_g"][0].rearrange("(k p) -> k p", p=P)),
                        ((116, 124), 0, A["ssm_norm_g"][0].rearrange("(k p) -> k p", p=P)),
                        ((0, 60), 1, A["conv_w"][0].rearrange("j (k p) -> (j k) p", p=P)),
                        ((0, 128), 2, A["b_ada"][0].rearrange("(k p) -> k p", p=P)[0:P]),
                        ((0, 16), 3, A["b_ada"][0].rearrange("(k p) -> k p", p=P)[P:ADA_T]))):
                    act.dma_start(vec_rows[rows[0]:rows[1], block_, :], src).then_inc(vec_loaded, 16)
                for p in range(AHEAD):
                    split(p)
                act.wait_ge(vec_ready, 1)
                act.activation(cT[:, :, 0], vecT[:, V_CCTX:V_CCTX + KT], ACT.Silu).then_inc(c_ready, 1)
                act.activation(cT[:, :, 1], vecT[:, V_C:V_C + KT], ACT.Silu).then_inc(c_ready, 1)
                act.wait_ge(c_ready, 2)
                act.activation(c4[:, :, 0:2], cT[:, :, :], ACT.Copy).then_inc(c_ready, 1)
                act.wait_ge(const_ready, 1)
                for row, col, src in (
                        (0, 0, A["gate_bias"][0, 1, 0]), (64, 0, A["gate_bias"][0, 1, 1]),
                        (32, 0, A["dt_bias"][0, 0]), (96, 0, A["dt_bias"][0, 1]),
                        (0, 2, A["gate_bias"][0, 0, 0]), (64, 2, A["gate_bias"][0, 0, 1]),
                        (32, 3, A["a_log"][0, 0]), (96, 3, A["a_log"][0, 1]),
                        (0, 7, A["state_mlstm_m"][0, 0, 0]), (64, 8, A["state_mlstm_m"][0, 0, 1])):
                    act.dma_start(gcol[row:row + src.shape[0], col:col + 1], src.unsqueeze(1)).then_inc(cols_loaded, 16)
                act.dma_start(dsk[:, :], A["d_skip"][0].partition_broadcast(P)).then_inc(cols_loaded, 16)
                act.dma_start(gw_small[:, :, 0:16], w_in[:, :, COL_IG:COL_IG + 16]).then_inc(gw_loaded, 16)
                act.dma_start(gw_small[:, :, 16:48], w_in[:, :, COL_DT:COL_DT + 32]).then_inc(gw_loaded, 16)
                def first_tiles(pair):
                    for k in (2 * pair, 2 * pair + 1):
                        act.wait_ge(hn_ready, k + 1)
                        act.activation(xn_hi[:, k, :], hn[:, k % 2, :], ACT.Copy).then_inc(xn_hi_ready, 1)

                for v in range(ADA_FIRST):
                    for q in range(U):
                        split(U * v + q + AHEAD)
                    for t in (2 * v - 2, 2 * v - 1):
                        if 0 <= t < KT:
                            act.wait_ge(xT_ready, t + 1)
                            square("x0", t, xT[:, t, :])
                    if 2 * v - 1 == KT - 1:
                        root("x0", D)
                    if v >= PAIR_AT:
                        first_tiles(v - PAIR_AT)
                first_tiles(KT // 2 - 1)
                ffn(0)
                for k in range(KT):
                    act.wait_ge(x_updated, k + 1)
                    square("x1", k, xT[:, k, :])
                root("x1", D)
                hi_of(1, lambda k: hn[:, k % 2, :], hn_ready, KT)
                act.dma_start(x_wait, AX).then_inc(x_spilled, 16)

                def gate_part(m):
                    if m == 0:
                        act.wait_ge(dve_row, 1)
                        act.activation(r_e, r_t, ACT.Exp, scale=-1.0).then_inc(act_row, 1)
                        act.wait_ge(cols_loaded, 16 * N_COLS)
                        act.activation(gcol[:, 4:5], gcol[:, 3:4], ACT.Exp).then_inc(act_row, 1)
                    if m == 1:
                        act.wait_ge(dve_row, 2)
                        act.activation(r_lw, r_d, ACT.Ln).then_inc(act_row, 1)
                    if m == 3:
                        act.wait_ge(dve_row, 3)
                        for c in range(NCH):
                            t = slice(P * c, P * c + P)
                            act.activation(r_E[:, t], r_P[:, t], ACT.Exp, bias=gcol[:, 6 + c:7 + c])
                            act.activation(r_W[:, t], r_Q[:, t], ACT.Exp, bias=gcol[:, 9 + c:10 + c])
                        act.activation(r_T4, r_li, ACT.Exp).then_inc(act_row, 1)

                for p in range(P_GATES, P_SSM):
                    split(p + AHEAD)
                    j = p - P_XBC
                    if j >= 0 and j % U == U - 1:
                        n = j // U
                        for f in range(2):
                            act.wait_ge(conv_done, 2 * n + f + 1)
                            if n in (UNIT_B, UNIT_C):
                                dst = bcT[:, 2 * n + f, :]
                            else:
                                dst = cvs[:, f, :]
                                if n > 2:
                                    act.wait_ge(conv_tr, 2 * TOK_UNITS.index(n) + f - 1)
                            act.activation(dst, cv[:, f, :], ACT.Silu).then_inc(conv_silu, 1)
                    if j in GATE_AT:
                        gate_part(GATE_AT[j])
                act.wait_ge(gates_done, 1)
                for d in range(2):
                    act.dma_start(A["new_m"][0, 0, d].unsqueeze(1), gcol[ROW_ML[d]:ROW_ML[d] + HEADS, 13:14]).then_inc(m_stored, 16)
                act.wait_ge(cols_tr, 4)
                act.wait_ge(dec_mm, 1)
                for d in range(2):
                    act.dma_start(s_raw[:, d, :, :], A["state_ssm"][0, 0, d].rearrange("(j a) q n -> (a q) j n", a=2)).then_inc(sr_loaded, 16)
                for n, (g, c, d, step) in enumerate(SSM_STEPS):
                    act.wait_ge(ss_bc, n + 1)
                    if n:
                        act.wait_ge(ss_wd, n)
                        act.wait_ge(ss_wp, n)
                    act.activation(cbs, psum[6][:, 0:P], ACT.Copy).then_inc(ss_cb, 1)
                    for q in range(2):
                        split(P_SSM + U * n + q + AHEAD)
                    act.wait_ge(ss_seg, n + 1)
                    act.activation(seg[:, :, :], seg[:, :, :], ACT.Exp).then_inc(ss_exp, 1)
                    for q in range(2, U):
                        split(P_SSM + U * n + q + AHEAD)
                    if c == 0:
                        act.wait_ge(ss_state, ssm_before(n)[1] + 1)
                        dst = A["new_ssm"][0, 0, d, 8 * g:8 * g + 8].rearrange("(j a) q n -> (a q) j n", a=2)
                        act.dma_start(dst, s_out.rearrange("p (j n) -> p j n", j=4)).then_inc(s_stored, 16)

                act.wait_ge(yt_ready, KT // 2)
                with act.Fori(0, HEADS // 2) as i:
                    def a(hh, n):
                        if n in (1, 2):
                            act.wait_ge(m_cstored, at(64 * hh + 32 * n, i, 128))
                        act.wait_ge(m_seg, at(6 * hh + n + 1, i, 12))
                        act.activation(ex, ex, ACT.Exp).then_inc(m_exp, 1)

                    def b(hh, n):
                        c, d = STEPS[n]
                        if c:
                            act.wait_ge(m_int, at(4 * hh + n - 1, i, 8))
                            act.wait_ge(m_h, at(6 * hh + n, i, 12))
                            row = i * 2 + (ROW_ML[d] + hh)
                            act.activation(ti, psum[6][:, 0:VW], ACT.Copy, scale=cols[:, C_E, c, bass.ds(row, 1)]).then_inc(m_ti, 1)

                    def c_(hh, n):
                        c, d = STEPS[n]
                        if c == 0:
                            act.wait_ge(m_c, at(N_STATE * hh + n + 1, i, 8))
                            h = i * 2 + hh
                            act.dma_start(A["new_C"][0, 0, d, bass.ds(h, 1)].rearrange("a (k p) v -> p (a k) v", p=P),
                                          c_out[:, :, 0:DH]).then_inc(m_cstored, 16)
                            act.dma_start(A["new_n"][0, 0, d, bass.ds(h, 1)].rearrange("a (k p) -> p (a k)", p=P),
                                          c_out[:, :, DH], allow_slow_non_contiguous=True).then_inc(m_cstored, 16)

                    def end(hh):
                        act.wait_ge(h_var, at(hh + 1, i, 2))
                        act.activation(small[:, 24:27], small[:, 20:23], ACT.Sqrt, bias=eps[:, 0:1]).then_inc(h_std, 1)

                    tasks = {"a": a, "b": b, "c": c_}
                    for j, (col, hh, q) in enumerate(PAIR_ORDER):
                        split(P_HEADS + j + AHEAD, i, PAIR)
                        if j == 0:
                            for s in range(2):
                                h = i * 2 + s
                                for d in range(2):
                                    act.dma_start(cst[s][:, d, :, 0:DH], A["state_mlstm_C"][0, 0, d, bass.ds(h, 1)].rearrange(
                                        "a (k p) v -> p (a k) v", p=P)).then_inc(c_loaded[s], 16)
                                    act.dma_start(cst[s][:, d, :, DH], A["state_mlstm_n"][0, 0, d, bass.ds(h, 1)].rearrange(
                                        "a (k p) -> p (a k)", p=P), allow_slow_non_contiguous=True).then_inc(c_loaded[s], 16)
                        if q == U - 1 and col in (COL_O, COL_Z):
                            b0 = 2 * ((j // U) % 2)
                            act.wait_ge(pe_piece, at(P_HEADS + j + 1, i, PAIR))
                            for f in range(2):
                                if col == COL_O:
                                    act.activation(sigo[hh][:, f, :], psum[b0 + f][:, 0:TOK], ACT.Sigmoid).then_inc(og_ready, 1)
                                else:
                                    act.activation(psum[b0 + f][:, 0:TOK], psum[b0 + f][:, 0:TOK], ACT.Silu).then_inc(z_silu, 1)
                        for kind, thh, n in core_tasks(j):
                            if kind in tasks:
                                tasks[kind](thh, n)
                            elif kind == "end":
                                end(thh)

                act.wait_ge(mix_ready, 2 * HEADS)
                act.wait_ge(z_done, 2 * HEADS)
                for k in range(KT // 2):
                    square("ssm", k, y[:, KT // 2 + k, :])
                root("ssm", SSM_W)
                act.dma_start(AX, x_wait).then_inc(x_back, 16)
                for k in range(KT):
                    if k >= KT // 2:
                        act.wait_ge(ms_scaled, k - KT // 2 + 1)
                    act.activation(xn_hi[:, k, :], y[:, k, :], ACT.Copy).then_inc(xn_hi_ready, 1)
                for t in range(D // PC):
                    for q in range(U):
                        split(P_OUT + U * t + q + AHEAD)
                    for k in (2 * t, 2 * t + 1):
                        act.wait_ge(y_done, KT * FFN_IT + k + 1)
                        square("y2", k, y[:, k, :])
                root("y2", D)
                for k in range(KT):
                    act.wait_ge(x_updated, KT + k + 1)
                    square("x2", k, xT[:, k, :])
                root("x2", D)
                hi_of(3, lambda k: hn[:, k % 2, :], hn_ready, 2 * KT)
                ffn(1)
                for n in range(1, NCH * (KT // 4), 2):
                    kk, c = divmod(n, NCH)
                    act.wait_ge(out_tr, n + 1)
                    act.activation(out_tok[:, c, 512 * kk:512 * kk + 512], psum[2 + n % 2][:, :], ACT.Copy).then_inc(out_ready_act, 1)

            @block.vector
            def _(dve):
                own = Tally(dve, dve_step)
                link = own.link

                def split(p, i=None, per=0):
                    if p % 2 or p >= TOTAL:
                        return
                    dve.wait_ge(w_hi_ready, at(p + 1, i, per))
                    dve.tensor_tensor(w_lo[:, p % NS, :], w_raw[:, p % NR, :], w_hi[:, p % NS, :].bitcast(F32),
                                      ALU.subtract).then_inc(w_lo_dve, 1)

                def norm_coefs(stage, k0=0, n=KT):
                    t = KT * (3 * stage + 1) + k0
                    g = vecT[:, V_NORM + 2 * stage * KT + k0:V_NORM + 2 * stage * KT + k0 + n].unsqueeze(2).broadcast_to((P, n, 2))
                    link(dve.scalar_tensor_tensor(out=coefA[:, k0:k0 + n, :], in0=modT[:, t:t + n, :], scalar=1.0, in1=g,
                                                  op0=ALU.add, op1=ALU.mult))

                def gate_coefs(stage):
                    gate = modT[:, KT * (3 * stage + 2):KT * (3 * stage + 3), :]
                    g = vecT[:, V_NORM + (2 * stage + 1) * KT:V_NORM + (2 * stage + 2) * KT].unsqueeze(2).broadcast_to((P, KT, 2))
                    link(dve.scalar_tensor_tensor(out=coefG[:, :, :], in0=gate, scalar=1.0 if stage == 1 else 0.5, in1=g,
                                                  op0=ALU.mult, op1=ALU.mult))

                def inverse_root(name):
                    dve.wait_ge(std_ready, SQ_ORDER.index(name) + 1)
                    link(dve.reciprocal(ROOT_BANK[:, 0:TOK], std[:, :]))

                def scaled(stage, k):
                    if k >= 2:
                        dve.wait_ge(hn_ready, KT * stage + k - 1)
                    dve.tensor_tensor(xt[:, k % 2, :], xT[:, k, :], ROOT_BANK[:, 0:TOK], ALU.mult).then_inc(xt_done, 1)

                def modulated(stage, k):
                    dve.wait_ge(xt_done, KT * stage + k + 1)
                    if k >= 2:
                        dve.wait_ge(xn_lo_ready, KT * (0, 1, 3)[stage] + k - 1)
                    for grp, (t0, t1) in enumerate(GROUPS):
                        last = dve.tensor_scalar(hn[:, k % 2, t0:t1], xt[:, k % 2, t0:t1], coefA[:, k, grp:grp + 1],
                                                 modT[:, 3 * stage * KT + k, grp:grp + 1], ALU.mult, ALU.add)
                    last.then_inc(hn_ready, 1)

                def pre_norm(stage, name):
                    norm_coefs(stage)
                    inverse_root(name)
                    scaled(stage, 0)
                    for k in range(KT):
                        if k + 1 < KT:
                            scaled(stage, k + 1)
                        modulated(stage, k)

                def post_norm(stage, name):
                    gate_coefs(stage)
                    inverse_root(name)
                    for k in range(KT):
                        for grp, (t0, t1) in enumerate(GROUPS):
                            last = dve.scalar_tensor_tensor(out=y[:, k, t0:t1], in0=y[:, k, t0:t1], scalar=coefG[:, k, grp:grp + 1],
                                                            in1=ROOT_BANK[:, t0:t1], op0=ALU.mult, op1=ALU.mult)
                        last.then_inc(u_ready, 1)

                def ada_rows_out(p_end, unit, banks, i=None, per=0):
                    dve.wait_ge(pe_piece, at(p_end + 1, i, per))
                    dve.tensor_copy(ada_row[0:4, :], psum[banks[0]][0:4, 0:PC]).then_inc(ada_row_ready, 1)

                def ada_store(unit, banks, i=None, t0=None):
                    dve.wait_ge(ada_cols, at(unit + 1, i, ADA_STEP))
                    if t0 is None:
                        t0 = 2 * unit if i is None else i * (2 * ADA_STEP) + 2 * unit
                    bias = vecT[:, bass.ds(t0 + V_BADA, 2)].unsqueeze(2).broadcast_to((P, 2, 2))
                    dve.tensor_tensor(modT[:, bass.ds(t0, 2), :], psum[banks[1]][:, 0:4].rearrange("p (f g) -> p f g", f=2),
                                      bias, ALU.add).then_inc(ada_done, 1)

                def ffn(n):
                    tiles_before = KT * (FFN_IT * n) + (KT if n else 0)

                    def add_down(p, j, it, i=None, per=0):
                        dve.wait_ge(pe_piece, at(p + 1, i, per))
                        for f in range(2):
                            t = 2 * j + f
                            if it or i is not None:
                                before = tiles_before + KT * it + t + 1 - KT
                                if before > 0:
                                    dve.wait_ge(y_done, at(before, i, KT))
                            dve.tensor_tensor(y[:, t, :], y[:, t, :], psum[(4 if j % 2 else 2) + f][:, 0:TOK], ALU.add).then_inc(y_done, 1)

                    def hidden(p_end, it, s, i, per):
                        dve.wait_ge(pe_piece, at(p_end + 1, i, per))
                        for f in range(2):
                            m = 4 * (FFN_IT * n + it) + 2 * s + f
                            dve.wait_ge(silu_ready, at(m + 1, i, 4))
                            if m >= 2:
                                dve.wait_ge(hid_lo_ready, at(m - 1, i, 4))
                            dve.tensor_tensor(hidf[:, f, :], sg[:, f, :], psum[2 + f][:, 0:TOK], ALU.mult).then_inc(hid_ready, 1)

                    def step(i):
                        per, pieces = step_of(n, i)
                        pending = None
                        for p, kind, s, q in pieces:
                            split(p + AHEAD, i, per)
                            if kind == "d":
                                add_down(p, q, 0, i, per)
                            if kind == "u" and q == U - 1:
                                hidden(p, 0 if i is None else 1, s, i, per)
                            if pending is not None:
                                ada_store(pending, ADA_BANKS, i)
                                pending = None
                            if kind == "a" and q == U - 1:
                                pending = ada_unit(s, i)
                                ada_rows_out(p, pending, ADA_BANKS, i, per)

                    dve.wait_ge(y_zeroed, n + 1)
                    step(None)
                    with dve.Fori(0, FFN_IT - 1) as i:
                        step(i)
                    for j in range(DOWN):
                        split(ffn_tail(n) + j + AHEAD)
                        add_down(ffn_tail(n) + j, j, FFN_IT - 1)

                for p in range(AHEAD):
                    split(p)
                dve.wait_ge(vec_tr, 1)
                dve.tensor_copy(vecT[:, V_CCTX:V_CCTX + 32], psum[4][:, V_CCTX:V_CCTX + 32]).then_inc(vec_ready, 1)
                dve.wait_ge(vec_tr, 2)
                for c0, c1 in ((0, 124), (128, 188)):
                    dve.tensor_copy(vecT[:, c0:c1], psum[4][:, c0:c1])
                dve.tensor_copy(vecT[:, V_BADA:V_CCTX], psum[4][:, V_BADA:V_CCTX]).then_inc(vec_ready, 1)
                dve.wait_ge(c_ready, 3)
                dve.tensor_tensor(c4[:, :, 2:4], cT[:, :, :], c4[:, :, 0:2].bitcast(F32), ALU.subtract).then_inc(c_lo_ready, 1)
                dve.wait_ge(vec_ready, 2)

                def first_tiles(pair):
                    dve.wait_ge(ada_done, 2 * pair + 2)
                    norm_coefs(0, 2 * pair, 2)
                    for k in (2 * pair, 2 * pair + 1):
                        scaled(0, k)
                    for k in (2 * pair, 2 * pair + 1):
                        modulated(0, k)

                for v in range(ADA_FIRST):
                    for q in range(U):
                        split(U * v + q + AHEAD)
                        if q == 0 and v:
                            ada_store(v - 1, ADA_BANKS, t0=2 * ADA_START[v - 1])
                    ada_rows_out(U * v + U - 1, v, ADA_BANKS)
                    for t in (2 * v - 2, 2 * v - 1):
                        if 0 <= t < KT:
                            dve.wait_ge(xt_tr, t + 1)
                            dve.tensor_copy(xT[:, t, :], psum[2 + t % 2][:, 0:TOK]).then_inc(xT_ready, 1)
                    if v == PAIR_AT:
                        dve.wait_ge(xT_ready, KT)
                        inverse_root("x0")
                    if v >= PAIR_AT:
                        first_tiles(v - PAIR_AT)
                ada_store(ADA_FIRST - 1, ADA_BANKS, t0=2 * ADA_START[-1])
                first_tiles(KT // 2 - 1)
                ffn(0)
                dve.wait_ge(ada_done, ADA_T // 2 - ADA_SSM)
                post_norm(0, "y1")
                pre_norm(1, "x1")

                def both(rows_of):
                    for d in range(2):
                        yield d, rows_of[d]

                def gate_part(m):
                    if m == 0:
                        dve.wait_ge(pe_piece, P_GATES + U)
                        dve.wait_ge(cols_loaded, 16 * N_COLS)
                        dve.wait_ge(x_spilled, 16)
                        dve.tensor_scalar(r_u, psum[0][:, 0:TOK], gcol[:, 0:1], gcol[:, 1:2], ALU.add, ALU.mult).then_inc(gate_read, 1)
                        dve.tensor_scalar(r_li, psum[1][:, 0:TOK], gcol[:, 2:3], None, ALU.add).then_inc(gate_read, 1)
                        dve.wait_ge(gate_read, 2)
                        dve.scalar_tensor_tensor(out=r_t, in0=r_u, scalar=-1.0, in1=r_u, op0=ALU.mult, op1=ALU.max).then_inc(dve_row, 1)
                    if m == 1:
                        dve.wait_ge(act_row, 1)
                        dve.tensor_scalar(r_d, r_e, 1.0, None, ALU.add).then_inc(dve_row, 1)
                        dve.wait_ge(dve_row, 2)
                        link(dve.tensor_scalar(r_t, r_d, -1.0, None, ALU.add))
                        link(dve.tensor_scalar(r_q, r_t, 1e-30, None, ALU.max))
                        link(dve.reciprocal(r_cs, r_q))
                        link(dve.tensor_scalar(r_T4, r_t, 0.0, None, ALU.is_equal))
                    if m == 2:
                        dve.wait_ge(act_row, 3)
                        link(dve.tensor_tensor(r_q, r_lw, r_e, ALU.mult))
                        link(dve.tensor_tensor(r_t, r_q, r_cs, ALU.mult))
                        link(dve.tensor_tensor(r_q, r_T4, r_e, ALU.mult))
                        link(dve.tensor_tensor(r_lw, r_t, r_q, ALU.add))
                        link(dve.scalar_tensor_tensor(out=r_sp, in0=r_u, scalar=0.0, in1=r_lw, op0=ALU.max, op1=ALU.add))
                        link(dve.tensor_scalar(gcol[:, 4:5], gcol[:, 4:5], -1.0, None, ALU.mult))
                        link(dve.tensor_scalar(r_d, r_sp, gcol[:, 4:5], None, ALU.mult))
                        for d, (a, b) in both(SCAN):
                            for c in range(NCH):
                                t = run(d, c)
                                last = dve.tensor_tensor_scan(r_cs[a:b, t], ones[a:b, :], r_d[a:b, t], 0.0, ALU.mult, ALU.add)
                        link(last)
                        link(dve.tensor_tensor(r_Q, r_li, r_cs, ALU.subtract))
                        link(dve.tensor_copy(r_P, r_cs))
                    if m == 3:
                        for d in range(2):
                            a, b = (64 * d, 64 * d + 32)
                            for c in ((0, 1, 2), (0, 2, 1))[d]:
                                t = run(d, c)
                                init = 0.0 if c == 0 else gcol[a:b, 6 + c:7 + c]
                                link(dve.tensor_tensor_scan(r_t[a:b, t], r_Q[a:b, t], r_Q[a:b, t], init, ALU.max, ALU.max))
                                if c == (1, 2)[d]:
                                    e = last_of(d, c)
                                    link(dve.tensor_tensor(gcol[a:b, 9 - c:10 - c], r_cs[a:b, e:e + 1], r_t[a:b, e:e + 1], ALU.add))
                            link(dve.tensor_scalar(r_P[a:b, :], r_t[a:b, :], -1.0, None, ALU.mult))
                        for d, (a, b) in both(SCAN):
                            link(dve.tensor_copy(gcol[a:b, 9:12], r_P[a:b, last_of(d, 0):TOK:P]))
                        dve.tensor_tensor(r_li, r_P, r_cs, ALU.subtract).then_inc(dve_row, 1)
                    if m == 4:
                        dve.wait_ge(act_row, 4)
                        dve.wait_ge(dve_row, 3)
                        for d in range(2):
                            a, b = ROW_SS[d], ROW_SS[d] + 32
                            link(dve.tensor_tensor(r_W[a:b, :], r_W[a:b, :], r_sp[a:b, :], ALU.mult))
                            link(dve.tensor_copy(r_T4[a:b, :], r_sp[a:b, :]))
                        for d, (a, b) in both(SCAN):
                            e, e0 = last_of(d, (1, 2)[d]), last_of(d, 0)
                            link(dve.tensor_copy(gcol[a:b, 12:13], r_E[a:b, e:e + 1]))
                            link(dve.tensor_tensor(gcol[a:b, 13:14], r_cs[a:b, e0:e0 + 1], r_P[a:b, e0:e0 + 1], ALU.subtract))
                        dve.tensor_scalar(r_t[:, 0:P], idn[:, :], gcol[:, 12:13], None, ALU.mult).then_inc(gates_done, 1)

                def run(d, c):
                    if d == 0:
                        return slice(P * c, P * c + P)
                    return slice(P * c + P - 1, P * c - 1 if c else None, -1)

                def last_of(d, c):
                    return P * c + (0 if d else P - 1)

                def conv(n, f):
                    t = 2 * XBC_ORDER[n] + f
                    src, dst = psum[(0 if n % 2 else 2) + f], cv[:, f, :]

                    def tap(k):
                        return vecT[:, V_CONVW + k * XBC_T + t:V_CONVW + k * XBC_T + t + 1]

                    if n:
                        dve.wait_ge(conv_silu, 2 * n + f - 1)
                    link(dve.tensor_scalar(dst, src[:, 0:TOK], tap(CONV_K // 2), vecT[:, V_CONVB + t:V_CONVB + t + 1], ALU.mult, ALU.add))
                    for k in (0, 1, 3, 4):
                        s = k - CONV_K // 2
                        for t0, t1, width in ((0, TOK_P, TOK_P), (TOK_P, TOK, GRID_W)):
                            a, b = max(0, -s), width - max(0, s)
                            o = dst[:, t0:t1].rearrange("p (r w) -> p r w", w=width)[:, :, a:b]
                            x = src[:, t0:t1].rearrange("p (r w) -> p r w", w=width)[:, :, a + s:b + s]
                            last = dve.scalar_tensor_tensor(out=o, in0=x, scalar=tap(k), in1=o, op0=ALU.mult, op1=ALU.add)
                            if k == 4 and t0:
                                last.then_inc(conv_done, 1)
                            elif t0:
                                link(last)

                def to_tok(n):
                    for f in range(2):
                        m = 2 * TOK_UNITS.index(n) + f
                        dve.wait_ge(conv_tr, m + 1)
                        c0 = f * P if n == UNIT_B else 2 * P * XBC_ORDER[n] + f * P
                        dst = (bm_tok if n == UNIT_B else xs_tok)[:, :, c0:c0 + P]
                        dve.tensor_copy(dst, psum[4 + f][:, 0:TOK].rearrange("p (c n) -> p c n", c=NCH)).then_inc(tok_ready, 1)

                for p in range(P_GATES, P_SSM):
                    split(p + AHEAD)
                    j = p - P_XBC
                    if j >= 0 and j % U == U - 1:
                        n = j // U
                        dve.wait_ge(pe_piece, p + 1)
                        for f in range(2):
                            conv(n, f)
                        if n - 1 in TOK_UNITS:
                            to_tok(n - 1)
                    if j in GATE_AT:
                        gate_part(GATE_AT[j])
                to_tok(XBC_T // 2 - 1)
                for kind in range(4):
                    dve.wait_ge(cols_tr, kind + 1)
                    dve.tensor_copy(cols[:, kind, :, :], psum[4 + kind][:, 0:TOK].rearrange("p (c r) -> p c r", c=NCH)).then_inc(cols_ready, 1)
                dve.wait_ge(dec_mm, 1)
                dve.tensor_copy(dbc[:, :], psum[2][:, 0:P]).then_inc(dec_ready, 1)
                for n in range(4):
                    d, half = divmod(n, 2)
                    dve.wait_ge(st_tr, n + 1)
                    dve.tensor_copy(ST[:, d, GRP_W * half:GRP_W * half + GRP_W], psum[half][:, :]).then_inc(st_ready, 1)

                dve.wait_ge(cols_ready, 4)
                dve.wait_ge(dec_ready, 1)
                dve.wait_ge(st_ready, 4)

                def by_head(v, n=8):
                    return v.unsqueeze(2).broadcast_to((P, n, SSM_P))

                def heads_of(v):
                    return v.rearrange("p (h q) -> p h q", q=SSM_P)

                for n, (g, c, d, step) in enumerate(SSM_STEPS):
                    carried, states = ssm_before(n)
                    r0 = ROW_SS[d] + 8 * g
                    mine = slice(GRP_W * g, GRP_W * g + GRP_W)
                    dve.wait_ge(ss_bc, n + 1)
                    if n:
                        dve.wait_ge(ss_y, n)
                    for h in range(8):
                        last = dve.scalar_tensor_tensor(out=seg[:, h, :], in0=psum[4 + h // 4][:, P * (h % 4):P * (h % 4) + P],
                                                        scalar=cols[:, C_Q, c, r0 + h:r0 + h + 1], in1=maskneg[:, d, :],
                                                        op0=ALU.add, op1=ALU.add)
                    last.then_inc(ss_seg, 1)
                    for q in range(2):
                        split(P_SSM + U * n + q + AHEAD)
                    dve.wait_ge(ss_exp, n + 1)
                    dve.wait_ge(ss_cb, n + 1)
                    dve.tensor_tensor(seg[:, 0:4, :], seg[:, 0:4, :], cbs.unsqueeze(1).broadcast_to((P, 4, P)), ALU.mult).then_inc(ss_wd, 1)
                    unit = ADA_T // 2 - ADA_SSM + n
                    ada_rows_out(P_SSM + U * n + U - 1, unit, ADA_BANKS_SSM)
                    for q in range(2, U):
                        split(P_SSM + U * n + q + AHEAD)
                    dve.wait_ge(ss_y, n + 1)
                    dve.wait_ge(ss_x, n + 1)
                    if carried:
                        dve.wait_ge(ss_ypool, carried)
                    if n:
                        dve.wait_ge(ss_yacc, n)
                    dve.tensor_tensor(yacc[:, c, mine], yacc[:, c, mine], psum[7][:, :], ALU.add).then_inc(ss_yacc, 1)
                    ada_store(unit, ADA_BANKS_SSM)
                    if c:
                        dve.wait_ge(ss_int, carried + 1)
                        dve.tensor_tensor(heads_of(ytmp), heads_of(psum[6][:, :]), by_head(cols[:, C_E, c, r0:r0 + 8]),
                                          ALU.mult).then_inc(ss_tmp, 1)
                    if step < N_STATE:
                        if c:
                            link(dve.tensor_tensor(heads_of(stt_), heads_of(ST[:, d, mine]), by_head(dbc[:, r0:r0 + 8]), ALU.mult))
                            dve.wait_ge(ss_stm, states + 1)
                            dve.tensor_tensor(ST[:, d, mine], stt_, psum[6][:, :], ALU.add).then_inc(ss_state, 1)
                        else:
                            dve.wait_ge(ss_stm, states + 1)
                            stored = 2 * g + step
                            if stored:
                                dve.wait_ge(s_stored, 16 * stored)
                            dve.tensor_copy(s_out, psum[6][:, :]).then_inc(ss_state, 1)
                for t in range(KT // 2):
                    dve.wait_ge(yt_tr, t + 1)
                    dve.tensor_copy(y[:, KT // 2 + t, :], psum[4 + t % 2][:, 0:TOK]).then_inc(yt_ready, 1)
                dve.wait_ge(yt_ready, KT // 2)

                with dve.Fori(0, HEADS // 2) as i:
                    own.enter(i, LINKS_PAIR)

                    def kv(hh):
                        ktok, va = hset[hh][3:5]
                        for n, dst in enumerate((ktok, va)):
                            for f in range(2):
                                dve.wait_ge(kv_tr, at(4 * hh + 2 * n + f + 1, i, 8))
                                dve.tensor_copy(dst[:, :, f * P:f * P + P], psum[4 + f][:, 0:TOK].rearrange("p (c n) -> p c n", c=NCH)).then_inc(kv_tok, 1)

                    def start(hh):
                        for d in range(2):
                            row = i * 2 + (ROW_ML[d] + hh)
                            dve.tensor_scalar(mrow[:, d, :], r_P, idn[:, bass.ds(row, 1)], None, ALU.mult).then_inc(row_ready, 1)

                    def a(hh, n):
                        c, d = STEPS[n]
                        row = i * 2 + (ROW_ML[d] + hh)
                        if n == 0:
                            dve.wait_ge(m_bc, at(hh + 1, i, 2))
                        else:
                            dve.wait_ge(m_s, at(6 * hh + n, i, 12))
                        dve.scalar_tensor_tensor(out=ex, in0=psum[4 + d][:, P * c:P * c + P], scalar=cols[:, C_Q, c, bass.ds(row, 1)],
                                                 in1=maskneg[:, d, :], op0=ALU.add, op1=ALU.add).then_inc(m_seg, 1)
                        dve.wait_ge(m_exp, at(6 * hh + n + 1, i, 12))
                        dve.wait_ge(m_qk, at(6 * hh + n + 1, i, 12))
                        dve.tensor_tensor(sT, ex, psum[6][:, 0:P], ALU.mult).then_inc(m_s, 1)

                    def b(hh, n):
                        c, d = STEPS[n]
                        row = i * 2 + (ROW_ML[d] + hh)
                        dve.wait_ge(m_num, at(6 * hh + n + 1, i, 12))
                        if c:
                            dve.wait_ge(m_ti, at(4 * hh + n - 1, i, 8))
                            link(dve.tensor_tensor(num, ti, psum[7][:, 0:VW], ALU.add))
                        else:
                            link(dve.tensor_copy(num, psum[7][:, 0:VW]))
                        link(dve.tensor_scalar(small[:, 2:3], num[:, DH:VW], -1.0, cols[:, C_T, c, bass.ds(row, 1)], ALU.mult, ALU.max))
                        link(dve.tensor_tensor(small[:, 0:1], num[:, DH:VW], small[:, 2:3], ALU.max))
                        link(dve.reciprocal(small[:, 1:2], small[:, 0:1]))
                        if n == 0 and hh:
                            dve.wait_ge(h_tr, at(1, i, 2))
                        if n in FIRST_VISIT:
                            dve.tensor_scalar(hacc[:, c, :], num[:, 0:DH], small[:, 1:2], None, ALU.mult).then_inc(m_h, 1)
                        else:
                            dve.scalar_tensor_tensor(out=hacc[:, c, :], in0=num[:, 0:DH], scalar=small[:, 1:2], in1=hacc[:, c, :],
                                                     op0=ALU.mult, op1=ALU.add).then_inc(m_h, 1)
                        dve.wait_ge(m_h, at(6 * hh + n + 1, i, 12))

                    def c_(hh, n):
                        c, d = STEPS[n]
                        row = i * 2 + (ROW_ML[d] + hh)
                        dve.wait_ge(m_upd, at(N_STATE * hh + n + 1, i, 8))
                        if n == 2:
                            dve.wait_ge(c_loaded[hh], at(64, i, 64))
                        for k in range(2):
                            if c:
                                last = dve.scalar_tensor_tensor(out=cst[hh][:, d, k, :], in0=cst[hh][:, d, k, :], scalar=dbc[:, bass.ds(row, 1)],
                                                                in1=psum[7 - k][:, 0:VW], op0=ALU.mult, op1=ALU.add)
                            else:
                                last = dve.tensor_copy(c_out[:, k, :], psum[7 - k][:, 0:VW])
                        last.then_inc(m_c, 1)

                    def end(hh):
                        for c in range(NCH):
                            last = dve.bn_stats(stats[:, c, :], hacc[:, c, :])
                        link(last)
                        dve.tensor_copy(small[:, 3:4], stats[:, 2, 0:1])
                        for c in range(NCH):
                            last = dve.bn_aggr(small[:, 12 + 2 * c:14 + 2 * c], stats[:, c, :])
                        link(last)
                        dve.tensor_copy(small[:, 20:23], small[:, 13:18:2]).then_inc(h_var, 1)
                        dve.wait_ge(h_std, at(hh + 1, i, 2))
                        link(dve.reciprocal(small[:, 28:31], small[:, 24:27]))
                        for c in range(NCH):
                            dve.tensor_scalar(hacc[:, c, :], hacc[:, c, :], small[:, 12 + 2 * c:13 + 2 * c], small[:, 28 + c:29 + c],
                                              ALU.subtract, ALU.mult).then_inc(h_norm, 1)
                        dve.wait_ge(h_tr, at(hh + 1, i, 2))
                        dve.wait_ge(og_ready, at(2 * hh + 2, i, 4))
                        for k in range(2):
                            t = i * 4 + (2 * hh + k)
                            dve.scalar_tensor_tensor(out=y[:, bass.ds(t, 1), :].rearrange("p a t -> p (a t)"), in0=psum[4 + k][:, 0:TOK],
                                                     scalar=vecT[:, bass.ds(t + V_MLG, 1)], in1=sigo[hh][:, k, :], op0=ALU.mult,
                                                     op1=ALU.mult).then_inc(mix_ready, 1)

                    tasks = {"kv": kv, "start": start, "end": end, "a": a, "b": b, "c": c_}
                    for j, (col, hh, q) in enumerate(PAIR_ORDER):
                        split(P_HEADS + j + AHEAD, i, PAIR)
                        if q == U - 1:
                            b0 = 2 * ((j // U) % 2)
                            if col in (COL_Q, COL_K, COL_V):
                                dst = hset[hh][(COL_Q, COL_K, COL_V).index(col)]
                                dve.wait_ge(pe_piece, at(P_HEADS + j + 1, i, PAIR))
                                for f in range(2):
                                    if col == COL_K:
                                        dve.tensor_scalar(dst[:, f, :], psum[b0 + f][:, 0:TOK], DH ** -0.5, None, ALU.mult).then_inc(qkv_ready, 1)
                                    else:
                                        dve.tensor_copy(dst[:, f, :], psum[b0 + f][:, 0:TOK]).then_inc(qkv_ready, 1)
                            elif col == COL_Z:
                                for f in range(2):
                                    dve.wait_ge(z_silu, at(2 * hh + f + 1, i, 4))
                                    t = i * 4 + (KT // 2 + 2 * hh + f)
                                    tile = y[:, bass.ds(t, 1), :].rearrange("p a t -> p (a t)")
                                    dve.tensor_tensor(tile, tile, psum[b0 + f][:, 0:TOK], ALU.mult).then_inc(z_done, 1)
                        for kind, thh, n in core_tasks(j):
                            tasks[kind](thh) if n is None else tasks[kind](thh, n)
                own.leave(HEADS // 2)

                dve.wait_ge(z_done, 2 * HEADS)
                inverse_root("ssm")
                for k in range(KT // 2, KT):
                    g = vecT[:, V_SSG + k - KT // 2:V_SSG + k - KT // 2 + 1]
                    dve.scalar_tensor_tensor(out=y[:, k, :], in0=y[:, k, :], scalar=g, in1=ROOT_BANK[:, 0:TOK],
                                             op0=ALU.mult, op1=ALU.mult).then_inc(ms_scaled, 1)
                dve.wait_ge(ada_done, ADA_T // 2)
                for t in range(D // PC):
                    for q in range(U):
                        split(P_OUT + U * t + q + AHEAD)
                    dve.wait_ge(pe_piece, P_OUT + U * t + U)
                    for f in range(2):
                        dve.tensor_copy(y[:, 2 * t + f, :], psum[(4 if t % 2 else 2) + f][:, 0:TOK]).then_inc(y_done, 1)
                dve.wait_ge(y_done, KT * (FFN_IT + 1))
                post_norm(1, "y2")
                pre_norm(2, "x2")
                ffn(1)
                dve.wait_ge(y_done, KT * (2 * FFN_IT + 1))
                post_norm(2, "y3")
                for n in range(0, NCH * (KT // 4), 2):
                    kk, c = divmod(n, NCH)
                    dve.wait_ge(out_tr, n + 1)
                    dve.tensor_copy(out_tok[:, c, 512 * kk:512 * kk + 512], psum[2 + n % 2][:, :]).then_inc(out_ready_dve, 1)

            @block.gpsimd
            def _(pool):
                own = Tally(pool, pool_step)
                link = own.link

                def split(p, i=None, per=0):
                    if p % 2 == 0 or p >= TOTAL:
                        return
                    pool.wait_ge(w_hi_ready, at(p + 1, i, per))
                    pool.tensor_tensor(w_lo[:, p % NS, :], w_raw[:, p % NR, :], w_hi[:, p % NS, :].bitcast(F32),
                                       ALU.subtract).then_inc(w_lo_pool, 1)

                def lo_of(done, src, tiles=range(KT)):
                    for k in tiles:
                        pool.wait_ge(xn_hi_ready, done + k + 1)
                        pool.tensor_tensor(xn_lo[:, k, :], src(k), xn_hi[:, k, :].bitcast(F32), ALU.subtract).then_inc(xn_lo_ready, 1)

                def update(stage):
                    for k in range(KT):
                        pool.wait_ge(u_ready, KT * stage + k + 1)
                        pool.tensor_tensor(xT[:, k, :], xT[:, k, :], y[:, k, :], ALU.add).then_inc(x_updated, 1)

                def ffn(n):
                    def hid_lo_part(it, s, i):
                        for f in range(2):
                            m = 4 * (FFN_IT * n + it) + 2 * s + f
                            pool.wait_ge(hid_hi_ready, at(m + 1, i, 4))
                            pool.tensor_tensor(hid_lo[:, 2 * s + f, :], hidf[:, f, :], hid_hi[:, 2 * s + f, :].bitcast(F32),
                                               ALU.subtract).then_inc(hid_lo_ready, 1)

                    def step(i):
                        per, pieces = step_of(n, i)
                        for p, kind, s, q in pieces:
                            split(p + AHEAD, i, per)
                            if kind == "u" and q == U - 1:
                                hid_lo_part(0 if i is None else 1, s, i)

                    step(None)
                    with pool.Fori(0, FFN_IT - 1) as i:
                        step(i)
                    for j in range(DOWN):
                        split(ffn_tail(n) + j + AHEAD)

                def pad_gates():
                    pool.wait_ge(gw_loaded, 32)
                    link(pool.memset(gw_pad[:, :, :], 0.0))
                    for dst, src, n in ((ROW_ML[0], 2 * HEADS, HEADS), (ROW_ML[1], 3 * HEADS, HEADS),
                                        (ROW_SS[0], 4 * HEADS, SSM_H), (ROW_SS[1], 4 * HEADS + SSM_H, SSM_H),
                                        (P + ROW_ML[0], 0, HEADS), (P + ROW_ML[1], HEADS, HEADS)):
                        last = pool.tensor_copy(gw_pad[:, :, dst:dst + n], gw_small[:, :, src:src + n])
                    last.then_inc(gw_ready, 1)

                link(pool.memset(idn[:, :], 0.0))
                link(pool.affine_select(out=idn[:, :], in_=idn[:, :], compare_op=ALU.not_equal, fill=1.0, base=0,
                                        pattern=[[-1, P]], channel_multiplier=1))
                link(pool.tensor_tensor(sel[:, :], idn[:, 0:2], idn[:, 2:4], ALU.add))
                link(pool.memset(ada_row[:, :], 0.0))
                link(pool.memset(ones[:, :], 1.0))
                link(pool.memset(gcol[:, :], 0.0))
                link(pool.memset(gcol[:, 1:2], 1.0))
                link(pool.memset(gcol[0:32, 1:2], -1.0))
                link(pool.memset(gcol[64:96, 1:2], -1.0))
                link(pool.memset(maskneg[:, :, :], 0.0))
                for d in range(2):
                    sign = -1 if d else 1
                    link(pool.affine_select(out=maskneg[:, d, :], in_=maskneg[:, d, :], compare_op=ALU.is_ge, fill=MASKED, base=0,
                                            pattern=[[sign, P]], channel_multiplier=-sign))
                pool.memset(eps[:, :], EPS).then_inc(const_ready, 1)
                for p in range(AHEAD):
                    split(p)
                for v in range(ADA_FIRST):
                    for q in range(U):
                        split(U * v + q + AHEAD)
                    if v == 2:
                        pad_gates()
                    if v >= PAIR_AT:
                        lo_of(0, lambda k: hn[:, k % 2, :], (2 * (v - PAIR_AT), 2 * (v - PAIR_AT) + 1))
                lo_of(0, lambda k: hn[:, k % 2, :], (KT - 2, KT - 1))
                pool.wait_ge(xt_tr, KT)
                pool.memset(y[:, :, :], 0.0).then_inc(y_zeroed, 1)
                ffn(0)
                update(0)
                lo_of(KT, lambda k: hn[:, k % 2, :])
                for p in range(P_GATES, P_SSM):
                    split(p + AHEAD)
                pool.wait_ge(cols_ready, 4)
                pool.wait_ge(tok_ready, 2 * len(TOK_UNITS))
                pool.wait_ge(cols_loaded, 16 * N_COLS)

                def by_head(v):
                    return v.unsqueeze(2).broadcast_to((P, 8, SSM_P))

                def heads_of(v):
                    return v.rearrange("p (h q) -> p h q", q=SSM_P)

                for n, (g, c, d, step) in enumerate(SSM_STEPS):
                    carried, states = ssm_before(n)
                    r0 = ROW_SS[d] + 8 * g
                    mine = slice(GRP_W * g, GRP_W * g + GRP_W)
                    x = heads_of(xs_tok[:, c, mine])
                    if n:
                        pool.wait_ge(ss_y, n)
                        if states:
                            pool.wait_ge(ss_stm, states)
                    last = pool.tensor_tensor(heads_of(xdt), x, by_head(cols[:, C_T, c, r0:r0 + 8]), ALU.mult)
                    if step < N_STATE:
                        last = pool.tensor_tensor(heads_of(xte), x, by_head(cols[:, C_W, c, r0:r0 + 8]), ALU.mult)
                    if step in FIRST_VISIT:
                        last = pool.tensor_tensor(heads_of(yacc[:, c, mine]), x, by_head(dsk[:, 8 * g:8 * g + 8]), ALU.mult)
                    last.then_inc(ss_x, 1)
                    for q in range(2):
                        split(P_SSM + U * n + q + AHEAD)
                    pool.wait_ge(ss_exp, n + 1)
                    pool.wait_ge(ss_cb, n + 1)
                    pool.tensor_tensor(seg[:, 4:8, :], seg[:, 4:8, :], cbs.unsqueeze(1).broadcast_to((P, 4, P)), ALU.mult).then_inc(ss_wp, 1)
                    for q in range(2, U):
                        split(P_SSM + U * n + q + AHEAD)
                    if c:
                        pool.wait_ge(ss_tmp, carried + 1)
                        pool.wait_ge(ss_yacc, n + 1)
                        pool.tensor_tensor(yacc[:, c, mine], yacc[:, c, mine], ytmp, ALU.add).then_inc(ss_ypool, 1)

                pool.wait_ge(ss_stm, ssm_before(len(SSM_STEPS))[1])
                for head in hset:
                    last = pool.memset(head[4][:, :, DH:VW], 1.0)
                last.then_inc(v_ones, 1)

                with pool.Fori(0, HEADS // 2) as i:
                    for j, (col, hh_, q) in enumerate(PAIR_ORDER):
                        split(P_HEADS + j + AHEAD, i, PAIR)
                        for kind, hh, n in core_tasks(j):
                            ktok, va = hset[hh][3:5]
                            if kind == "a" and n < N_STATE:
                                c, d = STEPS[n]
                                row = i * 2 + (ROW_ML[d] + hh)
                                if n == 0:
                                    pool.wait_ge(kv_tok, at(4 * hh + 4, i, 8))
                                if n or hh:
                                    pool.wait_ge(m_upd, at(N_STATE * hh + n, i, 8))
                                pool.tensor_tensor(wk, ktok[:, c, :], cols[:, C_W, c, bass.ds(row, 1)].broadcast_to((P, DH)),
                                                   ALU.mult).then_inc(m_wk, 1)
                lo_of(2 * KT, lambda k: y[:, k, :])
                for t in range(D // PC):
                    for q in range(U):
                        split(P_OUT + U * t + q + AHEAD)
                pool.wait_ge(x_back, 16)
                update(1)
                pool.wait_ge(x_updated, 2 * KT)
                pool.memset(y[:, :, :], 0.0).then_inc(y_zeroed, 1)
                lo_of(3 * KT, lambda k: hn[:, k % 2, :])
                ffn(1)
                update(2)


_INS = ['x_prompt', 'x_sample', 'state_mlstm_C', 'state_mlstm_n', 'state_mlstm_m', 'state_ssm', 'c', 'c_ctx', 'w_ada', 'b_ada',
        'norm_g', 'w_in', 'gate_bias', 'dt_bias', 'a_log', 'd_skip', 'conv_w', 'conv_b', 'ml_norm_g', 'ssm_norm_g', 'w_out',
        'ffn_w_gate', 'ffn_w_up', 'ffn_w_down']
_OUTS = [('y_prompt', (1, TOK_P, D)), ('y_sample', (1, TOK_S, D)), ('new_C', (1, 1, 2, HEADS, DH, DH)), ('new_n', (1, 1, 2, HEADS, DH)),
         ('new_m', (1, 1, 2, HEADS)), ('new_ssm', (1, 1, 2, SSM_H, SSM_P, SSM_N))]


def kernel(**inputs):
    import numpy as _np
    import concourse.bacc as _bacc
    from concourse.bass_utils import run_bass_kernel_spmd as _run

    nc = _bacc.Bacc("TRN2", target_bir_lowering=False, num_devices=1, dynamic_dma_scratch_size=1024)
    arrays, args = {}, {}
    for name in _INS:
        a = _np.ascontiguousarray(inputs[name])
        arrays[f"in_{name}_dram"] = a
        args[name] = nc.dram_tensor(f"in_{name}_dram", a.shape, mybir.dt.from_np(a.dtype), kind="ExternalInput").ap()
    for name, shape in _OUTS:
        args[name] = nc.dram_tensor(f"out_{name}_dram", shape, F32, kind="ExternalOutput").ap()
    hybrid_step(nc, args)
    r = _run(nc, [arrays], core_ids=[0])
    return tuple(r.results[0][f"out_{name}_dram"] for name, _ in _OUTS)
```

```python
from contextlib import ExitStack

import concourse.bass as bass
from concourse import mybir

ALU = mybir.AluOpType
ACT = mybir.ActivationFunctionType
F32 = mybir.dt.float32
F32R = mybir.dt.float32r

P = 128
D = 2048
KT = D // P
TOK_P, TOK_S = 128, 256
TOK = TOK_P + TOK_S
NCH = TOK // P
GROUPS = ((0, TOK_P), (TOK_P, TOK))
D_FF = 256 * ((8 * D // 3 + 255) // 256)
HEADS = 4
ML_W = D // 2
DH = ML_W // HEADS
SSM_W = D - ML_W
SSM_P = 64
SSM_H = SSM_W // SSM_P
SSM_N = 128
SSM_G = 2
GRP_W = SSM_W // SSM_G
CONV_K = 5
GRID_W = 64
N_MOD = 9
EPS = 1e-6
COL_Q, COL_K, COL_V, COL_O = 0, ML_W, 2 * ML_W, 3 * ML_W
COL_IG = 4 * ML_W
COL_FG = COL_IG + 2 * HEADS
COL_Z = COL_FG + 2 * HEADS
COL_XBC = COL_Z + SSM_W
COL_DT = COL_XBC + SSM_W + 2 * SSM_G * SSM_N
XBC_T = (SSM_W + 2 * SSM_G * SSM_N) // P

PK, PC = 4, 256
PW = PK * PC
NR, NS, AHEAD = 8, 4, 3
U = KT // PK
FFN_IT = D_FF // 512
DOWN = D // PC
ADA_T = N_MOD * KT
ADA_FIRST = KT
ADA_STEP = 4
ADA_SSM = ADA_T // 2 - ADA_FIRST - ADA_STEP * FFN_IT
PAIR_AT = 9


def spread(main, ada, m0, m1):
    out, done = [], 0
    for m, piece in enumerate(main):
        upto = min(max(m + 1 - m0, 0), m1 - m0) * len(ada) // (m1 - m0)
        out += ada[done:upto] + [piece]
        done = upto
    return out


def ada_units(n):
    return [("a", k, q) for k in range(n) for q in range(U)]


def ffn_pieces(n, part):
    if part == "tail":
        return [("d", 0, q) for q in range(DOWN)]
    main = [(kind, s, q) for kind, s in (("g", 0), ("d", 0), ("u", 0), ("g", 1), ("u", 1)) if kind != "d" or part == "loop"
            for q in range(DOWN if kind == "d" else U)]
    if n == 0:
        return spread(main, ada_units(ADA_STEP), len(main) - ADA_STEP * U, len(main))
    return main


def start_on_dve(v, q):
    return q >= (U // 2 if v < PAIR_AT else U - 1)


SSM_PIECES = [("p" if q < U - 1 else "a", n, q) for n in range(ADA_SSM) for q in range(U)]
START_PIECES = [("a" if start_on_dve(v, q) else "p", v, q) for v in range(ADA_FIRST) for q in range(U)]
PAIR = 2 * 5 * U
FFN_PER = [len(ffn_pieces(n, "loop")) for n in range(2)]
_PHASES = [[k for k, _, _ in part] for part in (
    START_PIECES, ffn_pieces(0, "first"), (FFN_IT - 1) * ffn_pieces(0, "loop"), ffn_pieces(0, "tail"),
    (U + (XBC_T // 2) * U) * [("w", 0, 0)], SSM_PIECES, (HEADS // 2) * PAIR * [("w", 0, 0)], (D // PC) * U * [("w", 0, 0)],
    ffn_pieces(1, "first"), (FFN_IT - 1) * ffn_pieces(1, "loop"), ffn_pieces(1, "tail"))]
FFN1, LOOP1, TAIL1, P_GATES, P_SSM, P_HEADS, P_OUT, FFN2, LOOP2, TAIL2, TOTAL = [
    sum(len(x) for x in _PHASES[:n + 1]) for n in range(len(_PHASES))]
P_XBC = P_GATES + U
KINDS = [k for part in _PHASES for k in part]
MAIN = [p for p, k in enumerate(KINDS) if k not in "ap"]
M_OF = {p: m for m, p in enumerate(MAIN)}


def pool_splits(p):
    return p < P_GATES or M_OF[p] % 4 == 3


def counts(test):
    out, n = [], 0
    for p in range(TOTAL):
        n += bool(test(p))
        out.append(n)
    return out


N_HI = counts(lambda p: p in M_OF)
N_PE = counts(lambda p: KINDS[p] != "a")
N_DVE = counts(lambda p: p in M_OF and not pool_splits(p))
N_POOL = counts(lambda p: p in M_OF and pool_splits(p))
N_ADA = counts(lambda p: KINDS[p] == "a")


ROW_ML = (0, 64)
ROW_SS = (32, 96)
SCAN = ((0, 64), (64, 128))
MASKED = -1e30

STEPS = ((0, 0), (0, 1), (1, 0), (2, 1), (2, 0), (1, 1))
N_STATE = 4
FIRST_VISIT = (0, 2, 3)

ADA_START = [ADA_FIRST // 2 * (v % 2) + v // 2 for v in range(ADA_FIRST)]


def first_tile(v, q, late=0):
    g = U * v + q - late - U - 1
    return g // 2 if g >= 0 and g % 2 == 0 and g // 2 < KT else None


XBC_ORDER = (4, 5, 0, 1, 2, 3)
UNIT_B, UNIT_C = 0, 1
TOK_UNITS = (0, 2, 3, 4, 5)
GATE_AT = {1: 0, 5: 1, 9: 2, 12: 3, 17: 4}

PAIR_ORDER = [(col, hh, q) for col, hh in (
    (COL_Q, 0), (COL_K, 0), (COL_V, 0), (COL_Q, 1), (COL_K, 1), (COL_V, 1), (COL_O, 0), (COL_O, 1), (COL_Z, 0), (COL_Z, 1))
    for q in range(U)]
CORE_AT = {12: ("kv", 0), 13: ("start", 0), 14: ("a", 0, 0), 15: ("b", 0, 0), 16: ("c", 0, 0, "a", 0, 1), 17: ("b", 0, 1),
           18: ("c", 0, 1, "a", 0, 2), 19: ("b", 0, 2), 20: ("c", 0, 2, "a", 0, 3), 21: ("b", 0, 3),
           22: ("c", 0, 3, "a", 0, 4), 23: ("b", 0, 4), 24: ("a", 0, 5), 25: ("b", 0, 5), 26: ("kv", 1), 27: ("end", 0),
           28: ("start", 1), 29: ("a", 1, 0), 30: ("b", 1, 0), 31: ("c", 1, 0, "a", 1, 1), 32: ("b", 1, 1),
           33: ("c", 1, 1, "a", 1, 2), 34: ("b", 1, 2), 35: ("c", 1, 2, "a", 1, 3), 36: ("b", 1, 3),
           37: ("c", 1, 3, "a", 1, 4), 38: ("b", 1, 4), 39: ("a", 1, 5, "b", 1, 5, "end", 1)}


def core_tasks(j):
    out, rest = [], list(CORE_AT.get(j, ()))
    while rest:
        kind, hh = rest[:2]
        n = rest[2] if kind in "abc" else None
        rest = rest[3:] if kind in "abc" else rest[2:]
        out.append((kind, hh, n))
    return out


V_NORM, V_CONVB, V_MLG, V_SSG = 0, 96, 108, 116
V_CONVW, V_BADA, V_CCTX, V_C = 128, 256, 400, 416
VEC_ROWS = ((124, 0), (60, 128), (128, 256), (16, 384), (32, V_CCTX))
N_VEC = 7
N_COLS = 11
LINKS_PAIR = 2 * (6 * 4 + 3)


def at(const, i, per):
    return const if i is None else i * per + const


def of_piece(table, p, i, per, each=1):
    if i is None:
        return each * table[p]
    step = table[p + per] - table[p]
    assert per == PAIR or table[p + 2 * per] - table[p + per] == step
    return at(each * table[p], i, each * step)


class Tally:

    def __init__(self, eng, sem):
        self.eng, self.sem, self.n, self.i, self.per = eng, sem, 0, None, 0

    def enter(self, i, per):
        self.start, self.i, self.per = self.n, i, per

    def leave(self, times):
        assert self.n - self.start == self.per, (self.n - self.start, self.per)
        self.n, self.i = self.start + times * self.per, None

    def link(self, ins):
        ins.then_inc(self.sem, 1)
        self.n += 1
        self.eng.wait_ge(self.sem, at(self.n, self.i, self.per))


def hybrid_step(nc, A):
    with ExitStack() as ctx:
        def sb(name, shape, dt=F32):
            return ctx.enter_context(nc.sbuf_tensor(name, shape, dt))

        def sem(name):
            return ctx.enter_context(nc.semaphore(name))

        xT = sb("xT", [P, KT, TOK])
        xn_hi = sb("xn_hi", [P, KT, TOK], F32R)
        xn_lo = sb("xn_lo", [P, KT, TOK], F32R)
        y = sb("y", [P, KT, TOK])
        hid_hi = sb("hid_hi", [P, 4, TOK], F32R)
        hid_lo = sb("hid_lo", [P, 4, TOK], F32R)
        w_raw = sb("w_raw", [P, NR, PW])
        w_hi = sb("w_hi", [P, NS, PW], F32R)
        w_lo = sb("w_lo", [P, NS, PW], F32R)
        idn = sb("idn", [P, P])
        ones = sb("ones", [P, P])
        maskneg = sb("maskneg", [P, 2, P])
        vecT = sb("vecT", [P, 432])
        modT = sb("modT", [P, ADA_T, 2])
        cT = sb("cT", [P, KT, 2])
        ada_row = sb("ada_row", [P, PC])
        coefA = sb("coefA", [P, KT, 2])
        coefG = sb("coefG", [P, KT, 2])
        eps = sb("eps", [P, 1])
        gcol = sb("gcol", [P, 16])
        dsk = sb("dsk", [P, SSM_H])
        dbc = sb("dbc", [P, P])
        small = sb("small", [P, 32])
        stats = sb("stats", [P, NCH, 6])
        AM = sb("AM", [P, 43 * 256])
        AX = xT[:, :, :].rearrange("p k t -> p (k t)")
        psum = [ctx.enter_context(nc.psum_tensor(f"bank{b}", [P, 512], F32)) for b in range(8)]

        def am(kb, n):
            return AM[:, int(kb * 256):int(kb * 256) + n]

        def ax(kb, n):
            return AX[:, int(kb * 256):int(kb * 256) + n]

        sq = am(16, 2 * TOK).rearrange("p (s t) -> p s t", s=2)
        std = am(19, TOK)
        xt = am(20.5, 2 * TOK).rearrange("p (s t) -> p s t", s=2)
        hn = am(23.5, 2 * TOK).rearrange("p (s t) -> p s t", s=2)
        sg = am(27, 2 * TOK).rearrange("p (s t) -> p s t", s=2)
        hidf = am(30, 2 * TOK).rearrange("p (s t) -> p s t", s=2)
        x_tok = y[:, :, :].rearrange("p k t -> p (k t)").rearrange("p (c n) -> p c n", c=NCH)
        vec_rows = am(33, 5 * P).rearrange("p (s n) -> p s n", s=5)
        out_tok = am(0, NCH * D).rearrange("p (c n) -> p c n", c=NCH)
        ada_acc = am(33, 4 * PC).rearrange("p (e g n) -> p e g n", e=2, g=2)
        ada_acc_ssm = ax(16.5, 4 * PC).rearrange("p (e g n) -> p e g n", e=2, g=2)
        gw_small = am(37, KT * 48).rearrange("p (k n) -> p k n", k=KT)
        gw_pad = am(0, KT * PC).rearrange("p (k n) -> p k n", k=KT)
        rows = [ax(1.5 * r, TOK) for r in range(13)]
        r_u, r_e, r_lw, r_d, r_q, r_sp, r_cs, r_Q, r_E, r_W, r_T4, r_li, r_t = rows
        r_P = ax(22.5, TOK)
        cols = am(15.25, 4 * NCH * P).rearrange("p (q c r) -> p q c r", q=4, c=NCH)
        C_Q, C_E, C_W, C_T = range(4)
        xs_tok = am(0, NCH * SSM_W).rearrange("p (c n) -> p c n", c=NCH)
        bm_tok = am(12, NCH * SSM_G * SSM_N).rearrange("p (c n) -> p c n", c=NCH)
        bcT = am(21.25, 4 * TOK).rearrange("p (s t) -> p s t", s=4)
        cv = am(27.25, 2 * TOK).rearrange("p (s t) -> p s t", s=2)
        cvs = am(30.25, 2 * TOK).rearrange("p (s t) -> p s t", s=2)
        ST = am(33.5, 2 * SSM_W).rearrange("p (d n) -> p d n", d=2)
        seg = ax(0, 8 * P).rearrange("p (h t) -> p h t", h=8)
        xdt = ax(4, GRP_W)
        xte = ax(6, GRP_W)
        cbs = ax(8, P)
        stt_ = ax(8.5, GRP_W)
        s_out = ax(10.5, GRP_W)
        s_raw = ax(12.5, 2 * 8 * P).rearrange("p (d j n) -> p d j n", d=2, j=8)
        ytmp = ax(20.5, GRP_W)
        yacc = y[:, 0:KT // 2, :].rearrange("p k t -> p (k t)").rearrange("p (c n) -> p c n", c=NCH)
        VW = DH + 1
        def head_set(v):
            a = v.rearrange("p n -> p n")
            qT = a[:, 0:2 * TOK].rearrange("p (s t) -> p s t", s=2)
            kT = a[:, 2 * TOK:4 * TOK].rearrange("p (s t) -> p s t", s=2)
            vT = a[:, 4 * TOK:6 * TOK].rearrange("p (s t) -> p s t", s=2)
            ktok = a[:, 6 * TOK:8 * TOK].rearrange("p (c n) -> p c n", c=NCH)
            va = a[:, 8 * TOK:8 * TOK + NCH * VW].rearrange("p (c n) -> p c n", c=NCH)
            return qT, kT, vT, ktok, va
        HS_N = 8 * TOK + NCH * VW
        hset = [head_set(am(0, HS_N)), head_set(ax(0, HS_N))]
        cst = [am(21.25 + 4.25 * s, 2 * 2 * VW).rearrange("p (d k n) -> p d k n", d=2, k=2) for s in range(2)]
        mrow = am(29.75, 2 * TOK).rearrange("p (d t) -> p d t", d=2)
        ex = am(32.75, P)
        sT = am(33.25, P)
        ti = am(33.75, VW)
        num = am(34.85, VW)
        wk = am(35.95, DH)
        hacc = am(37, NCH * DH).rearrange("p (c n) -> p c n", c=NCH)
        c_out = am(40, 2 * VW).rearrange("p (k n) -> p k n", k=2)
        sigo = [ax(15.2 + 3 * s, 2 * TOK).rearrange("p (k t) -> p k t", k=2) for s in range(2)]

        x_wait = nc.dram_tensor("x_wait", (P, KT * TOK), F32).ap()

        raw_loaded = [sem(f"raw_loaded{s}") for s in range(NR)]
        w_hi_ready, w_lo_dve, w_lo_pool, pe_piece = sem("w_hi_ready"), sem("w_lo_dve"), sem("w_lo_pool"), sem("pe_piece")
        ada_sum, ada_acc_ready, ada_row_ready = sem("ada_sum"), sem("ada_acc_ready"), sem("ada_row_ready")
        ada_cols, ada_done = sem("ada_cols"), sem("ada_done")
        const_ready, pool_step, dve_step = sem("const_ready"), sem("pool_step"), sem("dve_step")
        x_loaded, cond_loaded, vec_loaded, cols_loaded, gw_loaded = sem("x_loaded"), sem("cond_loaded"), sem("vec_loaded"), sem("cols_loaded"), sem("gw_loaded")
        vec_tr, vec_ready, c_ready = sem("vec_tr"), sem("vec_ready"), sem("c_ready")
        xt_tr, xT_ready = sem("xt_tr"), sem("xT_ready")
        sq_ready, ss_mm, std_ready, xt_done = sem("sq_ready"), sem("ss_mm"), sem("std_ready"), sem("xt_done")
        hn_ready, xn_hi_ready, xn_lo_ready = sem("hn_ready"), sem("xn_hi_ready"), sem("xn_lo_ready")
        silu_ready, hid_ready = sem("silu_ready"), sem("hid_ready")
        hid_hi_ready, hid_lo_ready = sem("hid_hi_ready"), sem("hid_lo_ready")
        y_zeroed, y_done, u_ready, x_updated = sem("y_zeroed"), sem("y_done"), sem("u_ready"), sem("x_updated")
        out_tr, out_ready_dve, out_ready_act, out_stored = sem("out_tr"), sem("out_ready_dve"), sem("out_ready_act"), sem("out_stored")
        x_spilled, x_back = sem("x_spilled"), sem("x_back")
        gw_ready, gate_read, dve_row, act_row, gates_done = sem("gw_ready"), sem("gate_read"), sem("dve_row"), sem("act_row"), sem("gates_done")
        cols_tr, cols_ready, dec_mm, dec_ready, m_stored = sem("cols_tr"), sem("cols_ready"), sem("dec_mm"), sem("dec_ready"), sem("m_stored")
        conv_done, conv_silu, conv_tr, tok_ready = sem("conv_done"), sem("conv_silu"), sem("conv_tr"), sem("tok_ready")
        sr_loaded, st_tr, st_ready = sem("sr_loaded"), sem("st_tr"), sem("st_ready")
        ss_bc, ss_cb, ss_seg, ss_exp, ss_x = sem("ss_bc"), sem("ss_cb"), sem("ss_seg"), sem("ss_exp"), sem("ss_x")
        ss_wd, ss_wp, ss_y, ss_int, ss_yacc = sem("ss_wd"), sem("ss_wp"), sem("ss_y"), sem("ss_int"), sem("ss_yacc")
        ss_tmp, ss_ypool, ss_stm, ss_state, s_stored = sem("ss_tmp"), sem("ss_ypool"), sem("ss_stm"), sem("ss_state"), sem("s_stored")
        yt_tr, yt_ready = sem("yt_tr"), sem("yt_ready")
        qkv_ready, og_ready, z_silu, z_done = sem("qkv_ready"), sem("og_ready"), sem("z_silu"), sem("z_done")
        kv_tr, kv_tok, row_ready, m_bc, v_ones = sem("kv_tr"), sem("kv_tok"), sem("row_ready"), sem("m_bc"), sem("v_ones")
        c_loaded = [sem(f"c_loaded{s}") for s in range(2)]
        m_seg, m_exp, m_qk, m_s, m_num, m_int = sem("m_seg"), sem("m_exp"), sem("m_qk"), sem("m_s"), sem("m_num"), sem("m_int")
        m_ti, m_h, m_wk, m_upd, m_c, m_cstored = sem("m_ti"), sem("m_h"), sem("m_wk"), sem("m_upd"), sem("m_c"), sem("m_cstored")
        h_var, h_std, h_norm, h_tr, mix_ready, ms_scaled = sem("h_var"), sem("h_std"), sem("h_norm"), sem("h_tr"), sem("mix_ready"), sem("ms_scaled")

        def wait_lo(eng, p, i=None, per=0):
            if pool_splits(p):
                eng.wait_ge(w_lo_pool, of_piece(N_POOL, p, i, per))
            else:
                eng.wait_ge(w_lo_dve, of_piece(N_DVE, p, i, per))

        def wait_pe(eng, p, i=None, per=0):
            eng.wait_ge(pe_piece, of_piece(N_PE, p, i, per))

        def wait_raw(eng, p, i=None, per=0):
            eng.wait_ge(raw_loaded[p % NR], at(16 * (p // NR + 1), i, 16 * per // NR))

        def slot(p):
            return M_OF[p] % NS

        def ahead(p):
            m = M_OF[p] + AHEAD
            return MAIN[m] if m < len(MAIN) else None

        def by_tile(w):
            return w.rearrange("(k p) n -> p k n", p=P)

        w_in = by_tile(A["w_in"][0])
        w_out = by_tile(A["w_out"][0])
        w_ada = by_tile(A["w_ada"][0])
        w_gate = [by_tile(A["ffn_w_gate"][0, n]) for n in range(2)]
        w_up = [by_tile(A["ffn_w_up"][0, n]) for n in range(2)]
        w_down = [by_tile(A["ffn_w_down"][0, n]) for n in range(2)]

        SQ, total = {}, 0
        for name, count in (("x0", KT), ("y1", KT), ("x1", KT), ("ssm", KT // 2), ("y2", KT), ("x2", KT), ("y3", KT)):
            SQ[name] = (total, count)
            total += count
        SQ_ORDER = list(SQ)
        SSM_STEPS = [(g, c, d, n) for g in range(SSM_G) for n, (c, d) in enumerate(STEPS)]

        def ssm_before(n):
            return (sum(1 for x in SSM_STEPS[:n] if x[1]), sum(1 for x in SSM_STEPS[:n] if x[3] < N_STATE))

        def step_of(n, i):
            base = ((FFN1, LOOP1), (FFN2, LOOP2))[n][i is not None]
            return 0 if i is None else FFN_PER[n], [
                (base + j, *piece) for j, piece in enumerate(ffn_pieces(n, "first" if i is None else "loop"))]

        def tail_of(n):
            return (TAIL1, TAIL2)[n]

        def ada_unit(k, i):
            return ADA_FIRST + k + (0 if i is None else ADA_STEP)

        UNIT_SSM = ADA_T // 2 - ADA_SSM

        SUM_BANK, ROOT_BANK = psum[0], psum[5]

        def ada_places(unit):
            return (ada_acc_ssm, psum[0], psum[1]) if unit >= UNIT_SSM else (ada_acc, psum[6], psum[7])

        with nc.Block() as block:

            @block.sync
            def _(sp):
                def load(p, src, i=None, per=0):
                    old = p - NR
                    if old >= 0 and KINDS[old] == "a":
                        sp.wait_ge(ada_sum, of_piece(N_ADA, old, i, per, 2 * PK))
                    elif old >= 0 and KINDS[old] == "p":
                        wait_pe(sp, old, i, per)
                    elif old >= 0:
                        wait_lo(sp, old, i, per)
                    dst = w_raw[:, p % NR, :].rearrange("p (k n) -> p k n", k=PK)
                    sp.dma_start(dst, src).then_inc(raw_loaded[p % NR], 16)

                def block_of(w, c0, q):
                    return w[:, PK * q:PK * q + PK, bass.ds(c0, PC)]

                def load_ada(p, unit, i=None, per=0):
                    for q in range(U):
                        load(p + q, block_of(w_ada, unit * PC, q), i, per)

                def ffn_step(n, i):
                    per, pieces = step_of(n, i)
                    f0 = 0 if i is None else i * 512 + 512
                    u0 = ada_unit(0, i) if i is None else i * ADA_STEP + ada_unit(0, i)
                    for p, kind, s, q in pieces:
                        if kind == "a":
                            src = block_of(w_ada, (u0 + s) * PC, q)
                        elif kind == "d":
                            src = w_down[n][:, bass.ds(i * PK, PK), PC * q:PC * q + PC]
                        else:
                            src = block_of(w_gate[n] if kind == "g" else w_up[n], f0 + PC * s, q)
                        load(p, src, i, per)

                def ffn(n):
                    ffn_step(n, None)
                    with sp.Fori(0, FFN_IT - 1) as i:
                        ffn_step(n, i)
                    for j in range(DOWN):
                        load(tail_of(n) + j, w_down[n][:, D_FF // P - PK:, PC * j:PC * j + PC])

                for v, unit in enumerate(ADA_START):
                    if v == 2:
                        sp.dma_start(x_tok[:, 0, :], A["x_prompt"][0]).then_inc(x_loaded, 16)
                        sp.dma_start(x_tok[:, 1:3, :], A["x_sample"][0].rearrange("(c p) n -> p c n", p=P)).then_inc(x_loaded, 16)
                    for q in range(U):
                        load(U * v + q, block_of(w_ada, unit * PC, q))
                ffn(0)
                sp.wait_ge(gw_ready, 1)
                for q in range(U):
                    load(P_GATES + q, gw_pad[:, PK * q:PK * q + PK, :])
                for n, t in enumerate(XBC_ORDER):
                    for q in range(U):
                        load(P_XBC + U * n + q, block_of(w_in, COL_XBC + PC * t, q))
                for n in range(ADA_SSM):
                    for q in range(U):
                        load(P_SSM + U * n + q, block_of(w_ada, (UNIT_SSM + n) * PC, q))
                for i in range(HEADS // 2):
                    for j, (col, hh, q) in enumerate(PAIR_ORDER):
                        load(P_HEADS + PAIR * i + j, block_of(w_in, col + DH * (2 * i + hh), q))
                for t in range(D // PC):
                    for q in range(U):
                        load(P_OUT + U * t + q, block_of(w_out, PC * t, q))
                ffn(1)
                for kk in range(KT // 4):
                    for c in range(NCH):
                        n = NCH * kk + c
                        sp.wait_ge(out_ready_act if n % 2 else out_ready_dve, n // 2 + 1)
                        dst = A["y_prompt"][0] if c == 0 else A["y_sample"][0, P * (c - 1):P * c]
                        sp.dma_start(dst[:, 512 * kk:512 * kk + 512], out_tok[:, c, 512 * kk:512 * kk + 512]).then_inc(out_stored, 16)
                sp.wait_ge(out_stored, 16 * NCH * (KT // 4))
                sp.wait_ge(s_stored, 16 * 2 * SSM_G)
                sp.wait_ge(m_cstored, 32 * 2 * HEADS)
                sp.wait_ge(m_stored, 32)

            @block.tensor
            def _(pe):
                def product(out, w, off, hi, lo, start, stop):
                    wh = w_hi[:, w, off:off + P]
                    pe.matmul(out, wh, hi, start=start, stop=False)
                    pe.matmul(out, wh, lo, start=False, stop=False)
                    return pe.matmul(out, w_lo[:, w, off:off + P], hi, start=False, stop=stop)

                def unit_piece(p, q, b0, i=None, per=0, fresh=None):
                    wait_lo(pe, p, i, per)
                    if fresh is not None:
                        pe.wait_ge(xn_lo_ready, fresh + PK * (q + 1))
                    for f in range(2):
                        for k in range(PK):
                            last = product(psum[b0 + f][:, 0:TOK], slot(p), k * PC + f * P, xn_hi[:, PK * q + k, :],
                                           xn_lo[:, PK * q + k, :], q == 0 and k == 0, q == U - 1 and k == PK - 1)
                    last.then_inc(pe_piece, 1)

                def ada_piece(p, q, unit):
                    acc, rows, columns = ada_places(unit)
                    wait_raw(pe, p)
                    if q == 0 and unit and unit != UNIT_SSM:
                        pe.wait_ge(ada_row_ready, rows_before(unit))
                    for k in range(PK):
                        last = pe.matmul(rows[0:2, 0:PC], cT[:, PK * q + k, :], w_raw[:, p % NR, k * PC:k * PC + PC],
                                         start=(q == 0 and k == 0), stop=(KINDS[p + 1] == "a" and k == PK - 1))
                    last.then_inc(pe_piece, 1)

                def rows_before(unit):
                    return unit if unit <= ADA_FIRST else ADA_FIRST + unit - UNIT_SSM

                def ada_columns(unit, i=None, shared=False):
                    acc, rows, columns = ada_places(unit)
                    pe.wait_ge(ada_acc_ready, at(unit + 1, i, ADA_STEP))
                    if shared:
                        pe.wait_ge(ada_row_ready, rows_before(unit) + 1)
                    if unit:
                        pe.wait_ge(ada_done, at(unit, i, ADA_STEP))
                    for f in range(2):
                        if shared:
                            pe.matmul(columns[:, 2 * f:2 * f + 2], ada_row[:, P * f:P * f + P], idn[:, 0:2], start=(f == 0), stop=False,
                                      skip_group_check=True)
                        for g in range(2):
                            last = pe.matmul(columns[:, 2 * f + g:2 * f + g + 1], acc[:, 0, g, P * f:P * f + P], ones[:, 0:1],
                                             start=(not shared and f == 0 and g == 0), stop=True, skip_group_check=True)
                    last.then_inc(ada_cols, 1)

                def square_sum(name, k):
                    base, count = SQ[name]
                    pe.wait_ge(sq_ready, base + k + 1)
                    if k == 0 and base:
                        pe.wait_ge(std_ready, SQ_ORDER.index(name))
                    pe.matmul(SUM_BANK[:, 0:TOK], ones[:, :], sq[:, (base + k) % 2, :], start=(k == 0),
                              stop=(k == count - 1)).then_inc(ss_mm, 1)

                pe.wait_ge(const_ready, 1)
                pe.wait_ge(cond_loaded, 32)
                for r in (4, 0, 1, 2, 3):
                    n, col = VEC_ROWS[r]
                    if r == 0:
                        pe.wait_ge(vec_loaded, 16 * N_VEC)
                        pe.wait_ge(vec_ready, 1)
                    last = pe.transpose(psum[4][:, col:col + n], vec_rows[0:n, r, :], idn[0:n, 0:n])
                    if r >= 3:
                        last.then_inc(vec_tr, 1)
                pe.wait_ge(c_ready, 2)
                for v in range(ADA_FIRST):
                    for q in range(U):
                        if not start_on_dve(v, q):
                            ada_piece(U * v + q, q, v)
                        if v and not start_on_dve(v, q) and start_on_dve(v, q + 1):
                            ada_columns(v - 1, shared=True)
                        summed = first_tile(v, q, 4)
                        if summed is not None:
                            square_sum("x0", summed)
                        t = first_tile(v, q)
                        if t is None:
                            continue
                        if t == 0:
                            pe.wait_ge(x_loaded, 32)
                        if t >= 2:
                            pe.wait_ge(xT_ready, t - 1)
                        for c in range(NCH):
                            last = pe.transpose(psum[2 + t % 2][:, P * c:P * c + P], x_tok[:, c, P * t:P * t + P], idn[:, :])
                        last.then_inc(xt_tr, 1)
                ada_columns(ADA_FIRST - 1, shared=True)

                def ffn(n):
                    tiles_before = KT * (FFN_IT * n) + (KT if n else 0)

                    def down_piece(p, j, it, i=None):
                        wait_lo(pe, p, i, FFN_PER[n])
                        if j == 0:
                            pe.wait_ge(hid_lo_ready, at(4 * (FFN_IT * n + it + 1), i, 4))
                        if j >= 2:
                            pe.wait_ge(y_done, at(tiles_before + KT * it + 2 * j - 2, i, KT))
                        for f in range(2):
                            bank = (4 if j % 2 else 2) + f
                            for k in range(PK):
                                last = product(psum[bank][:, 0:TOK], slot(p), k * PC + f * P, hid_hi[:, k, :],
                                               hid_lo[:, k, :], k == 0, k == PK - 1)
                        last.then_inc(pe_piece, 1)

                    def step(i):
                        per, pieces = step_of(n, i)
                        first = i is None
                        pending = None
                        for p, kind, s, q in pieces:
                            if kind == "a":
                                if q == U - 1:
                                    pending = ada_unit(s, i)
                                continue
                            read = 4 * (FFN_IT * n + (0 if first else 1)) + 2 * s
                            if kind == "g" and q == 0 and read:
                                pe.wait_ge(silu_ready, at(read, i, 4))
                            if kind == "u" and q == 0 and (s or first) and read:
                                pe.wait_ge(hid_ready, at(read, i, 4))
                            if kind == "u" and q == 0 and not first:
                                pe.wait_ge(y_done, at(tiles_before + (KT if s else KT - 2), i, KT))
                            if kind == "d":
                                down_piece(p, q, 0, i)
                            else:
                                fresh = KT * (3 if n else 0) if first and (kind, s) == ("g", 0) else None
                                unit_piece(p, q, 0 if kind == "g" else 2, i, per, fresh)
                            if pending is not None:
                                ada_columns(pending, i)
                                pending = None

                    step(None)
                    with pe.Fori(0, FFN_IT - 1) as i:
                        step(i)
                    name = "y3" if n else "y1"
                    for j in range(DOWN):
                        down_piece(tail_of(n) + j, j, FFN_IT - 1)
                        if j:
                            square_sum(name, 2 * j - 2)
                            square_sum(name, 2 * j - 1)
                    square_sum(name, KT - 2)
                    square_sum(name, KT - 1)

                ffn(0)
                for k in range(KT):
                    square_sum("x1", k)

                for q in range(U):
                    unit_piece(P_GATES + q, q, 0, fresh=KT)

                def conv_transposes(n):
                    for f in range(2):
                        m = 2 * TOK_UNITS.index(n) + f
                        pe.wait_ge(conv_silu, 2 * n + f + 1)
                        if m >= 2:
                            pe.wait_ge(tok_ready, m - 1)
                        src = bcT[:, f, :] if n == UNIT_B else cvs[:, f, :]
                        for c in range(NCH):
                            last = pe.transpose(psum[4 + f][:, P * c:P * c + P], src[:, P * c:P * c + P], idn[:, :])
                        last.then_inc(conv_tr, 1)

                for n in range(XBC_T // 2):
                    if n == 1:
                        pe.wait_ge(gate_read, 2)
                    elif n >= 2:
                        pe.wait_ge(conv_done, 2 * (n - 1))
                    for q in range(U):
                        unit_piece(P_XBC + U * n + q, q, 0 if n % 2 else 2)
                    if n - 1 in TOK_UNITS:
                        conv_transposes(n - 1)
                conv_transposes(XBC_T // 2 - 1)

                pe.wait_ge(gates_done, 1)
                pe.wait_ge(tok_ready, 2 * len(TOK_UNITS))
                pe.wait_ge(conv_done, XBC_T)
                for kind, src in enumerate((r_Q, r_E, r_W, r_T4)):
                    for c in range(NCH):
                        last = pe.transpose(psum[4 + kind][:, P * c:P * c + P], src[:, P * c:P * c + P], idn[:, :])
                    last.then_inc(cols_tr, 1)
                pe.matmul(psum[2][:, 0:P], ones[:, :], r_t[:, 0:P], start=True, stop=True).then_inc(dec_mm, 1)
                pe.wait_ge(sr_loaded, 32)
                for n in range(4):
                    d, half = divmod(n, 2)
                    if n >= 2:
                        pe.wait_ge(st_ready, n - 1)
                    for j in range(4):
                        last = pe.transpose(psum[half][:, P * j:P * j + P], s_raw[:, d, 4 * half + j, :], idn[:, :])
                    last.then_inc(st_tr, 1)

                pe.wait_ge(cols_ready, 4)
                pe.wait_ge(st_ready, 4)
                for n, (g, c, d, step) in enumerate(SSM_STEPS):
                    tok = slice(P * c, P * c + P)
                    carried, states = ssm_before(n)
                    if n:
                        pe.wait_ge(ss_seg, n)
                        if carried:
                            pe.wait_ge(ss_tmp, carried)
                        if states:
                            pe.wait_ge(ss_state, states)
                    for h in range(8):
                        r = ROW_SS[d] + 8 * g + h
                        pe.matmul(psum[4 + h // 4][:, P * (h % 4):P * (h % 4) + P], idn[:, r:r + 1].broadcast_to((P, P)),
                                  r_P[:, tok], start=True, stop=True)
                    pe.matmul(psum[6][:, 0:P], bcT[:, g, tok], bcT[:, 2 + g, tok], start=True, stop=True).then_inc(ss_bc, 1)
                    if n:
                        ada_columns(UNIT_SSM + n - 1, shared=True)
                    for q in range(U - 1):
                        ada_piece(P_SSM + U * n + q, q, UNIT_SSM + n)
                    pe.wait_ge(ss_wd, n + 1)
                    pe.wait_ge(ss_wp, n + 1)
                    pe.wait_ge(ss_x, n + 1)
                    if n:
                        pe.wait_ge(ss_yacc, n)
                    for h in range(8):
                        last = pe.matmul(psum[7][:, SSM_P * h:SSM_P * h + SSM_P], seg[:, h, :],
                                         xdt[:, SSM_P * h:SSM_P * h + SSM_P], start=True, stop=True)
                    last.then_inc(ss_y, 1)
                    pe.wait_ge(ss_cb, n + 1)
                    if c:
                        pe.matmul(psum[6][:, :], bcT[:, 2 + g, tok], ST[:, d, GRP_W * g:GRP_W * g + GRP_W],
                                  start=True, stop=True).then_inc(ss_int, 1)
                    if step < N_STATE:
                        if c:
                            pe.wait_ge(ss_tmp, carried + 1)
                            last = pe.matmul(psum[6][:, :], bm_tok[:, c, SSM_N * g:SSM_N * g + SSM_N], xte[:, :],
                                             start=True, stop=True)
                        else:
                            for j in range(4):
                                last = pe.matmul(psum[6][:, P * j:P * j + P], xte[:, P * j:P * j + P],
                                                 bm_tok[:, 0, SSM_N * g:SSM_N * g + SSM_N], start=True, stop=True)
                        last.then_inc(ss_stm, 1)

                ada_columns(ADA_T // 2 - 1, shared=True)
                pe.wait_ge(ss_yacc, len(SSM_STEPS))
                pe.wait_ge(ss_ypool, ssm_before(len(SSM_STEPS))[0])
                for t in range(KT // 2):
                    if t >= 2:
                        pe.wait_ge(yt_ready, t - 1)
                    for c in range(NCH):
                        last = pe.transpose(psum[4 + t % 2][:, P * c:P * c + P], yacc[:, c, P * t:P * t + P], idn[:, :])
                    last.then_inc(yt_tr, 1)
                pe.wait_ge(yt_ready, KT // 2)

                pe.wait_ge(dec_ready, 1)
                pe.wait_ge(v_ones, 1)
                with pe.Fori(0, HEADS // 2) as i:
                    def kv_transposes(hh):
                        qT, kT, vT, ktok, va = hset[hh]
                        if hh:
                            pe.wait_ge(m_seg, at(6, i, 12))
                        for n, src in enumerate((kT, vT)):
                            pe.wait_ge(qkv_ready, at(6 * hh + 4 + 2 * n, i, 12))
                            for f in range(2):
                                if n:
                                    pe.wait_ge(kv_tok, at(4 * hh + f + 1, i, 8))
                                for c in range(NCH):
                                    last = pe.transpose(psum[4 + f][:, P * c:P * c + P], src[:, f, P * c:P * c + P], idn[:, :])
                                last.then_inc(kv_tr, 1)

                    def core_start(hh):
                        pe.wait_ge(row_ready, at(2 * hh + 2, i, 4))
                        pe.wait_ge(kv_tok, at(4 * hh + 4, i, 8))
                        if hh:
                            pe.wait_ge(mix_ready, at(2, i, 4))
                        for d in range(2):
                            last = pe.matmul(psum[4 + d][:, 0:TOK], ones[:, :], mrow[:, d, :], start=True, stop=True)
                        last.then_inc(m_bc, 1)

                    def core_a(hh, n):
                        qT, kT, vT, ktok, va = hset[hh]
                        tok = slice(P * STEPS[n][0], P * STEPS[n][0] + P)
                        if n or hh:
                            pe.wait_ge(m_h, at(6 * hh + n, i, 12))
                            pe.wait_ge(m_c, at(N_STATE * hh + min(n, N_STATE), i, 8))
                        for k in range(2):
                            last = pe.matmul(psum[6][:, 0:P], kT[:, k, tok], qT[:, k, tok], start=(k == 0), stop=(k == 1))
                        last.then_inc(m_qk, 1)

                    def core_b(hh, n):
                        qT, kT, vT, ktok, va = hset[hh]
                        c, d = STEPS[n]
                        pe.wait_ge(m_s, at(6 * hh + n + 1, i, 12))
                        pe.matmul(psum[7][:, 0:VW], sT[:, :], va[:, c, :], start=True, stop=True).then_inc(m_num, 1)
                        if c:
                            if n == 2:
                                pe.wait_ge(c_loaded[hh], at(64, i, 64))
                            for k in range(2):
                                last = pe.matmul(psum[6][:, 0:VW], qT[:, k, P * c:P * c + P], cst[hh][:, d, k, :],
                                                 start=(k == 0), stop=(k == 1))
                            last.then_inc(m_int, 1)

                    def core_c(hh, n):
                        qT, kT, vT, ktok, va = hset[hh]
                        pe.wait_ge(m_wk, at(N_STATE * hh + n + 1, i, 8))
                        pe.wait_ge(m_h, at(6 * hh + n + 1, i, 12))
                        for k in range(2):
                            last = pe.matmul(psum[7 - k][:, 0:VW], wk[:, P * k:P * k + P], va[:, STEPS[n][0], :], start=True, stop=True)
                        last.then_inc(m_upd, 1)

                    def core_end(hh):
                        pe.wait_ge(h_norm, at(NCH * (hh + 1), i, 2 * NCH))
                        pe.wait_ge(kv_tok, at(8, i, 8))
                        for k in range(2):
                            for c in range(NCH):
                                last = pe.transpose(psum[4 + k][:, P * c:P * c + P], hacc[:, c, P * k:P * k + P], idn[:, :])
                        last.then_inc(h_tr, 1)

                    tasks = {"kv": kv_transposes, "start": core_start, "end": core_end, "a": core_a, "b": core_b, "c": core_c}
                    for j, (col, hh, q) in enumerate(PAIR_ORDER):
                        unit = j // U
                        if q == 0 and unit >= 2:
                            if unit < 8:
                                pe.wait_ge(qkv_ready, at(2 * (unit - 1), i, 12))
                            else:
                                pe.wait_ge(og_ready, at(2 * (unit - 7), i, 4))
                        unit_piece(P_HEADS + j, q, 2 * (unit % 2), i, PAIR)
                        for kind, thh, n in core_tasks(j):
                            tasks[kind](thh) if n is None else tasks[kind](thh, n)
                    pe.wait_ge(z_done, at(4, i, 4))
                    pe.wait_ge(mix_ready, at(4, i, 4))

                for k in range(KT // 2):
                    square_sum("ssm", k)
                for t in range(D // PC):
                    if t >= 2:
                        pe.wait_ge(y_done, KT * FFN_IT + 2 * (t - 1))
                    for q in range(U):
                        unit_piece(P_OUT + U * t + q, q, 4 if t % 2 else 2, fresh=None if t else 2 * KT)
                    if t:
                        square_sum("y2", 2 * t - 2)
                        square_sum("y2", 2 * t - 1)
                square_sum("y2", KT - 2)
                square_sum("y2", KT - 1)
                for k in range(KT):
                    square_sum("x2", k)
                ffn(1)
                for kk in range(KT // 4):
                    pe.wait_ge(x_updated, 2 * KT + 4 * kk + 4)
                    for c in range(NCH):
                        n = NCH * kk + c
                        if n >= 2:
                            pe.wait_ge(out_ready_act if n % 2 else out_ready_dve, n // 2)
                        for j in range(4):
                            last = pe.transpose(psum[2 + n % 2][:, P * j:P * j + P], xT[:, 4 * kk + j, P * c:P * c + P], idn[:, :])
                        last.then_inc(out_tr, 1)

            @block.scalar
            def _(act):
                def split(p, i=None, per=0):
                    p = ahead(p)
                    if p is not None:
                        make_hi(p, i, per)

                def make_hi(p, i=None, per=0):
                    wait_raw(act, p, i, per)
                    if M_OF[p] >= NS:
                        wait_pe(act, p - NS if per == PAIR else MAIN[M_OF[p] - NS], i, per)
                    act.activation(w_hi[:, slot(p), :], w_raw[:, p % NR, :], ACT.Copy).then_inc(w_hi_ready, 1)

                def square(name, k, src):
                    n = SQ[name][0] + k
                    if n >= 2:
                        act.wait_ge(ss_mm, n - 1)
                    act.activation(sq[:, n % 2, :], src, ACT.Square).then_inc(sq_ready, 1)

                def root(name, width):
                    base, count = SQ[name]
                    act.wait_ge(ss_mm, base + count)
                    act.activation(std[:, :], SUM_BANK[:, 0:TOK], ACT.Sqrt, bias=eps[:, 0:1], scale=1.0 / width).then_inc(std_ready, 1)

                def hi_of(stage, src, ready, first):
                    for k in range(KT):
                        act.wait_ge(ready, first + k + 1)
                        act.activation(xn_hi[:, k, :], src(k), ACT.Copy).then_inc(xn_hi_ready, 1)

                def ffn(n):
                    def posts(it, s, kind, p_end, i, per):
                        for f in range(2):
                            m = 4 * (FFN_IT * n + it) + 2 * s + f
                            if kind == "g":
                                if f == 0:
                                    wait_pe(act, p_end, i, per)
                                if m >= 2:
                                    act.wait_ge(hid_ready, at(m - 1, i, 4))
                                act.activation(sg[:, f, :], psum[f][:, 0:TOK], ACT.Silu).then_inc(silu_ready, 1)
                            else:
                                act.wait_ge(hid_ready, at(m + 1, i, 4))
                                act.activation(hid_hi[:, 2 * s + f, :], hidf[:, f, :], ACT.Copy).then_inc(hid_hi_ready, 1)

                    def step(i):
                        per, pieces = step_of(n, i)
                        for p, kind, s, q in pieces:
                            if kind != "a":
                                split(p, i, per)
                            if kind in "gu" and q == U - 1:
                                posts(0 if i is None else 1, s, kind, p, i, per)

                    step(None)
                    with act.Fori(0, FFN_IT - 1) as i:
                        step(i)
                    name = "y3" if n else "y1"
                    added = KT * (FFN_IT * (n + 1) - 1) + (KT if n else 0)
                    for j in range(DOWN):
                        split(tail_of(n) + j)
                        for k in (2 * j, 2 * j + 1):
                            act.wait_ge(y_done, added + k + 1)
                            square(name, k, y[:, k, :])
                    root(name, D)

                for n, src in enumerate((A["c_ctx"], A["c"][0])):
                    act.dma_start(vec_rows[KT * n:KT * n + KT, 4, :], src.rearrange("(k p) -> k p", p=P)).then_inc(cond_loaded, 16)
                for n, (rows, block_, src) in enumerate((
                        ((0, 96), 0, A["norm_g"][0].rearrange("j (k p) -> (j k) p", p=P)),
                        ((96, 108), 0, A["conv_b"][0].rearrange("(k p) -> k p", p=P)),
                        ((108, 116), 0, A["ml_norm_g"][0].rearrange("(k p) -> k p", p=P)),
                        ((116, 124), 0, A["ssm_norm_g"][0].rearrange("(k p) -> k p", p=P)),
                        ((0, 60), 1, A["conv_w"][0].rearrange("j (k p) -> (j k) p", p=P)),
                        ((0, 128), 2, A["b_ada"][0].rearrange("(k p) -> k p", p=P)[0:P]),
                        ((0, 16), 3, A["b_ada"][0].rearrange("(k p) -> k p", p=P)[P:ADA_T]))):
                    act.dma_start(vec_rows[rows[0]:rows[1], block_, :], src).then_inc(vec_loaded, 16)
                act.wait_ge(vec_ready, 1)
                act.activation(cT[:, :, 0], vecT[:, V_CCTX:V_CCTX + KT], ACT.Silu).then_inc(c_ready, 1)
                act.activation(cT[:, :, 1], vecT[:, V_C:V_C + KT], ACT.Silu).then_inc(c_ready, 1)
                act.wait_ge(const_ready, 1)
                for row, col, src in (
                        (0, 0, A["gate_bias"][0, 1, 0]), (64, 0, A["gate_bias"][0, 1, 1]),
                        (32, 0, A["dt_bias"][0, 0]), (96, 0, A["dt_bias"][0, 1]),
                        (0, 2, A["gate_bias"][0, 0, 0]), (64, 2, A["gate_bias"][0, 0, 1]),
                        (32, 3, A["a_log"][0, 0]), (96, 3, A["a_log"][0, 1]),
                        (0, 7, A["state_mlstm_m"][0, 0, 0]), (64, 8, A["state_mlstm_m"][0, 0, 1])):
                    act.dma_start(gcol[row:row + src.shape[0], col:col + 1], src.unsqueeze(1)).then_inc(cols_loaded, 16)
                act.dma_start(dsk[:, :], A["d_skip"][0].partition_broadcast(P)).then_inc(cols_loaded, 16)
                act.dma_start(gw_small[:, :, 0:16], w_in[:, :, COL_IG:COL_IG + 16]).then_inc(gw_loaded, 16)
                act.dma_start(gw_small[:, :, 16:48], w_in[:, :, COL_DT:COL_DT + 32]).then_inc(gw_loaded, 16)
                def first_tiles(pair):
                    for k in (2 * pair, 2 * pair + 1):
                        act.wait_ge(hn_ready, k + 1)
                        act.activation(xn_hi[:, k, :], hn[:, k % 2, :], ACT.Copy).then_inc(xn_hi_ready, 1)

                for v in range(ADA_FIRST):
                    for q in range(U):
                        t = first_tile(v, q)
                        if t is not None:
                            act.wait_ge(xT_ready, t + 1)
                            square("x0", t, xT[:, t, :])
                        if first_tile(v, q, 4) == KT - 1:
                            root("x0", D)
                    if v > PAIR_AT:
                        first_tiles(v - 1 - PAIR_AT)
                for p in MAIN[:AHEAD]:
                    make_hi(p)
                for pair in range(ADA_FIRST - 1 - PAIR_AT, KT // 2):
                    first_tiles(pair)
                ffn(0)
                for k in range(KT):
                    act.wait_ge(x_updated, k + 1)
                    square("x1", k, xT[:, k, :])
                root("x1", D)
                hi_of(1, lambda k: hn[:, k % 2, :], hn_ready, KT)
                act.dma_start(x_wait, AX).then_inc(x_spilled, 16)

                def gate_part(m):
                    if m == 0:
                        act.wait_ge(dve_row, 1)
                        act.activation(r_e, r_t, ACT.Exp, scale=-1.0).then_inc(act_row, 1)
                        act.wait_ge(cols_loaded, 16 * N_COLS)
                        act.activation(gcol[:, 4:5], gcol[:, 3:4], ACT.Exp).then_inc(act_row, 1)
                    if m == 1:
                        act.wait_ge(dve_row, 2)
                        act.activation(r_lw, r_d, ACT.Ln).then_inc(act_row, 1)
                    if m == 3:
                        act.wait_ge(dve_row, 3)
                        for c in range(NCH):
                            t = slice(P * c, P * c + P)
                            act.activation(r_E[:, t], r_P[:, t], ACT.Exp, bias=gcol[:, 6 + c:7 + c])
                            act.activation(r_W[:, t], r_Q[:, t], ACT.Exp, bias=gcol[:, 9 + c:10 + c])
                        act.activation(r_T4, r_li, ACT.Exp).then_inc(act_row, 1)

                for p in range(P_GATES, P_SSM):
                    if p < P_SSM - AHEAD:
                        split(p)
                    j = p - P_XBC
                    if j >= 0 and j % U == U - 1:
                        n = j // U
                        for f in range(2):
                            act.wait_ge(conv_done, 2 * n + f + 1)
                            if n in (UNIT_B, UNIT_C):
                                dst = bcT[:, 2 * n + f, :]
                            else:
                                dst = cvs[:, f, :]
                                if n > 2:
                                    act.wait_ge(conv_tr, 2 * TOK_UNITS.index(n) + f - 1)
                            act.activation(dst, cv[:, f, :], ACT.Silu).then_inc(conv_silu, 1)
                    if j in GATE_AT:
                        gate_part(GATE_AT[j])
                act.wait_ge(gates_done, 1)
                for d in range(2):
                    act.dma_start(A["new_m"][0, 0, d].unsqueeze(1), gcol[ROW_ML[d]:ROW_ML[d] + HEADS, 13:14]).then_inc(m_stored, 16)
                act.wait_ge(cols_tr, 4)
                act.wait_ge(dec_mm, 1)
                for d in range(2):
                    act.dma_start(s_raw[:, d, :, :], A["state_ssm"][0, 0, d].rearrange("(j a) q n -> (a q) j n", a=2)).then_inc(sr_loaded, 16)
                for n, (g, c, d, step) in enumerate(SSM_STEPS):
                    act.wait_ge(ss_bc, n + 1)
                    if n:
                        act.wait_ge(ss_wd, n)
                        act.wait_ge(ss_wp, n)
                    act.activation(cbs, psum[6][:, 0:P], ACT.Copy).then_inc(ss_cb, 1)
                    act.wait_ge(ss_seg, n + 1)
                    act.activation(seg[:, :, :], seg[:, :, :], ACT.Exp).then_inc(ss_exp, 1)
                    if c == 0:
                        act.wait_ge(ss_state, ssm_before(n)[1] + 1)
                        dst = A["new_ssm"][0, 0, d, 8 * g:8 * g + 8].rearrange("(j a) q n -> (a q) j n", a=2)
                        act.dma_start(dst, s_out.rearrange("p (j n) -> p j n", j=4)).then_inc(s_stored, 16)

                for p in range(P_SSM - AHEAD, P_SSM):
                    split(p)
                act.wait_ge(yt_ready, KT // 2)
                with act.Fori(0, HEADS // 2) as i:
                    def a(hh, n):
                        if n in (1, 2):
                            act.wait_ge(m_cstored, at(64 * hh + 32 * n, i, 128))
                        act.wait_ge(m_seg, at(6 * hh + n + 1, i, 12))
                        act.activation(ex, ex, ACT.Exp).then_inc(m_exp, 1)

                    def b(hh, n):
                        c, d = STEPS[n]
                        if c:
                            act.wait_ge(m_int, at(4 * hh + n - 1, i, 8))
                            act.wait_ge(m_h, at(6 * hh + n, i, 12))
                            row = i * 2 + (ROW_ML[d] + hh)
                            act.activation(ti, psum[6][:, 0:VW], ACT.Copy, scale=cols[:, C_E, c, bass.ds(row, 1)]).then_inc(m_ti, 1)

                    def c_(hh, n):
                        c, d = STEPS[n]
                        if c == 0:
                            act.wait_ge(m_c, at(N_STATE * hh + n + 1, i, 8))
                            h = i * 2 + hh
                            act.dma_start(A["new_C"][0, 0, d, bass.ds(h, 1)].rearrange("a (k p) v -> p (a k) v", p=P),
                                          c_out[:, :, 0:DH]).then_inc(m_cstored, 16)
                            act.dma_start(A["new_n"][0, 0, d, bass.ds(h, 1)].rearrange("a (k p) -> p (a k)", p=P),
                                          c_out[:, :, DH], allow_slow_non_contiguous=True).then_inc(m_cstored, 16)

                    def end(hh):
                        act.wait_ge(h_var, at(hh + 1, i, 2))
                        act.activation(small[:, 24:27], small[:, 20:23], ACT.Sqrt, bias=eps[:, 0:1]).then_inc(h_std, 1)

                    tasks = {"a": a, "b": b, "c": c_}
                    for j, (col, hh, q) in enumerate(PAIR_ORDER):
                        split(P_HEADS + j, i, PAIR)
                        if j == 0:
                            for s in range(2):
                                h = i * 2 + s
                                for d in range(2):
                                    act.dma_start(cst[s][:, d, :, 0:DH], A["state_mlstm_C"][0, 0, d, bass.ds(h, 1)].rearrange(
                                        "a (k p) v -> p (a k) v", p=P)).then_inc(c_loaded[s], 16)
                                    act.dma_start(cst[s][:, d, :, DH], A["state_mlstm_n"][0, 0, d, bass.ds(h, 1)].rearrange(
                                        "a (k p) -> p (a k)", p=P), allow_slow_non_contiguous=True).then_inc(c_loaded[s], 16)
                        if q == U - 1 and col in (COL_O, COL_Z):
                            b0 = 2 * ((j // U) % 2)
                            wait_pe(act, P_HEADS + j, i, PAIR)
                            for f in range(2):
                                if col == COL_O:
                                    act.activation(sigo[hh][:, f, :], psum[b0 + f][:, 0:TOK], ACT.Sigmoid).then_inc(og_ready, 1)
                                else:
                                    act.activation(psum[b0 + f][:, 0:TOK], psum[b0 + f][:, 0:TOK], ACT.Silu).then_inc(z_silu, 1)
                        for kind, thh, n in core_tasks(j):
                            if kind in tasks:
                                tasks[kind](thh, n)
                            elif kind == "end":
                                end(thh)

                act.wait_ge(mix_ready, 2 * HEADS)
                act.wait_ge(z_done, 2 * HEADS)
                for k in range(KT // 2):
                    square("ssm", k, y[:, KT // 2 + k, :])
                root("ssm", SSM_W)
                act.dma_start(AX, x_wait).then_inc(x_back, 16)
                for k in range(KT):
                    if k >= KT // 2:
                        act.wait_ge(ms_scaled, k - KT // 2 + 1)
                    act.activation(xn_hi[:, k, :], y[:, k, :], ACT.Copy).then_inc(xn_hi_ready, 1)
                for t in range(D // PC):
                    for q in range(U):
                        split(P_OUT + U * t + q)
                    for k in (2 * t, 2 * t + 1):
                        act.wait_ge(y_done, KT * FFN_IT + k + 1)
                        square("y2", k, y[:, k, :])
                root("y2", D)
                for k in range(KT):
                    act.wait_ge(x_updated, KT + k + 1)
                    square("x2", k, xT[:, k, :])
                root("x2", D)
                hi_of(3, lambda k: hn[:, k % 2, :], hn_ready, 2 * KT)
                ffn(1)
                for n in range(1, NCH * (KT // 4), 2):
                    kk, c = divmod(n, NCH)
                    act.wait_ge(out_tr, n + 1)
                    act.activation(out_tok[:, c, 512 * kk:512 * kk + 512], psum[2 + n % 2][:, :], ACT.Copy).then_inc(out_ready_act, 1)

            @block.vector
            def _(dve):
                own = Tally(dve, dve_step)
                link = own.link

                def split(p, i=None, per=0):
                    p = ahead(p)
                    if p is not None and not pool_splits(p):
                        make_lo(p, i, per)

                def make_lo(p, i=None, per=0):
                    dve.wait_ge(w_hi_ready, of_piece(N_HI, p, i, per))
                    dve.tensor_tensor(w_lo[:, slot(p), :], w_raw[:, p % NR, :], w_hi[:, slot(p), :].bitcast(F32),
                                      ALU.subtract).then_inc(w_lo_dve, 1)

                def norm_coefs(stage, k0=0, n=KT):
                    t = KT * (3 * stage + 1) + k0
                    g = vecT[:, V_NORM + 2 * stage * KT + k0:V_NORM + 2 * stage * KT + k0 + n].unsqueeze(2).broadcast_to((P, n, 2))
                    link(dve.scalar_tensor_tensor(out=coefA[:, k0:k0 + n, :], in0=modT[:, t:t + n, :], scalar=1.0, in1=g,
                                                  op0=ALU.add, op1=ALU.mult))

                def gate_coefs(stage):
                    gate = modT[:, KT * (3 * stage + 2):KT * (3 * stage + 3), :]
                    g = vecT[:, V_NORM + (2 * stage + 1) * KT:V_NORM + (2 * stage + 2) * KT].unsqueeze(2).broadcast_to((P, KT, 2))
                    link(dve.scalar_tensor_tensor(out=coefG[:, :, :], in0=gate, scalar=1.0 if stage == 1 else 0.5, in1=g,
                                                  op0=ALU.mult, op1=ALU.mult))

                def inverse_root(name):
                    dve.wait_ge(std_ready, SQ_ORDER.index(name) + 1)
                    link(dve.reciprocal(ROOT_BANK[:, 0:TOK], std[:, :]))

                def scaled(stage, k):
                    if k >= 2:
                        dve.wait_ge(hn_ready, KT * stage + k - 1)
                    dve.tensor_tensor(xt[:, k % 2, :], xT[:, k, :], ROOT_BANK[:, 0:TOK], ALU.mult).then_inc(xt_done, 1)

                def modulated(stage, k):
                    dve.wait_ge(xt_done, KT * stage + k + 1)
                    if k >= 2:
                        dve.wait_ge(xn_lo_ready, KT * (0, 1, 3)[stage] + k - 1)
                    for grp, (t0, t1) in enumerate(GROUPS):
                        last = dve.tensor_scalar(hn[:, k % 2, t0:t1], xt[:, k % 2, t0:t1], coefA[:, k, grp:grp + 1],
                                                 modT[:, 3 * stage * KT + k, grp:grp + 1], ALU.mult, ALU.add)
                    last.then_inc(hn_ready, 1)

                def pre_norm(stage, name):
                    norm_coefs(stage)
                    inverse_root(name)
                    scaled(stage, 0)
                    for k in range(KT):
                        if k + 1 < KT:
                            scaled(stage, k + 1)
                        modulated(stage, k)

                def post_norm(stage, name):
                    gate_coefs(stage)
                    inverse_root(name)
                    for k in range(KT):
                        for grp, (t0, t1) in enumerate(GROUPS):
                            last = dve.scalar_tensor_tensor(out=y[:, k, t0:t1], in0=y[:, k, t0:t1], scalar=coefG[:, k, grp:grp + 1],
                                                            in1=ROOT_BANK[:, t0:t1], op0=ALU.mult, op1=ALU.mult)
                        last.then_inc(u_ready, 1)

                def ada_piece(p, q, unit, i=None, per=0):
                    sums = ada_places(unit)[0]
                    wait_raw(dve, p, i, per)
                    first = not (q and KINDS[unit_piece_before(p)] == "a")
                    if first and unit:
                        dve.wait_ge(ada_cols, at(unit, i, ADA_STEP))
                    steps = 2 * PK * (N_ADA[p] - 1)
                    per_steps = 0 if i is None else 2 * PK * (N_ADA[p + per] - N_ADA[p])
                    for k in range(PK):
                        for g in range(2):
                            w, c = w_raw[:, p % NR, PC * k:PC * k + PC], cT[:, PK * q + k, g:g + 1]
                            acc = sums[:, k % 2, g, :]
                            if first and k < 2:
                                step = dve.tensor_scalar(acc, w, c, None, ALU.mult)
                            else:
                                dve.wait_ge(ada_sum, at(steps - 3, i, per_steps))
                                step = dve.scalar_tensor_tensor(out=acc, in0=w, scalar=c, in1=acc, op0=ALU.mult, op1=ALU.add)
                            step.then_inc(ada_sum, 1)
                            steps += 1
                    if q == U - 1:
                        dve.wait_ge(ada_sum, at(steps, i, per_steps))
                        dve.tensor_tensor(sums[:, 0, :, :], sums[:, 0, :, :], sums[:, 1, :, :], ALU.add).then_inc(ada_acc_ready, 1)

                def unit_piece_before(p):
                    return next(x for x in range(p - 1, -1, -1) if KINDS[x] in "ap")

                def ada_rows_out(unit):
                    dve.tensor_copy(ada_row[0:2, :], ada_places(unit)[1][0:2, 0:PC]).then_inc(ada_row_ready, 1)

                def ada_store(unit, i=None, t0=None):
                    dve.wait_ge(ada_cols, at(unit + 1, i, ADA_STEP))
                    if t0 is None:
                        t0 = 2 * unit if i is None else i * (2 * ADA_STEP) + 2 * unit
                    bias = vecT[:, bass.ds(t0 + V_BADA, 2)].unsqueeze(2).broadcast_to((P, 2, 2))
                    dve.tensor_tensor(modT[:, bass.ds(t0, 2), :], ada_places(unit)[2][:, 0:4].rearrange("p (f g) -> p f g", f=2),
                                      bias, ALU.add).then_inc(ada_done, 1)

                def ffn(n):
                    tiles_before = KT * (FFN_IT * n) + (KT if n else 0)

                    def add_down(p, j, it, i=None, per=0):
                        wait_pe(dve, p, i, per)
                        for f in range(2):
                            t = 2 * j + f
                            if it or i is not None:
                                before = tiles_before + KT * it + t + 1 - KT
                                if before > 0:
                                    dve.wait_ge(y_done, at(before, i, KT))
                            dve.tensor_tensor(y[:, t, :], y[:, t, :], psum[(4 if j % 2 else 2) + f][:, 0:TOK], ALU.add).then_inc(y_done, 1)

                    def hidden(p_end, it, s, i, per):
                        wait_pe(dve, p_end, i, per)
                        for f in range(2):
                            m = 4 * (FFN_IT * n + it) + 2 * s + f
                            dve.wait_ge(silu_ready, at(m + 1, i, 4))
                            if m >= 2:
                                dve.wait_ge(hid_lo_ready, at(m - 1, i, 4))
                            dve.tensor_tensor(hidf[:, f, :], sg[:, f, :], psum[2 + f][:, 0:TOK], ALU.mult).then_inc(hid_ready, 1)

                    def step(i):
                        per, pieces = step_of(n, i)
                        pending = None
                        for p, kind, s, q in pieces:
                            if kind == "a":
                                ada_piece(p, q, ada_unit(s, i), i, per)
                                if q == U - 1:
                                    pending = ada_unit(s, i)
                                continue
                            split(p, i, per)
                            if kind == "d":
                                add_down(p, q, 0, i, per)
                            if kind == "u" and q == U - 1:
                                hidden(p, 0 if i is None else 1, s, i, per)
                            if pending is not None:
                                ada_store(pending, i)
                                pending = None

                    dve.wait_ge(y_zeroed, n + 1)
                    step(None)
                    with dve.Fori(0, FFN_IT - 1) as i:
                        step(i)
                    for j in range(DOWN):
                        split(tail_of(n) + j)
                        add_down(tail_of(n) + j, j, FFN_IT - 1)

                dve.wait_ge(vec_tr, 1)
                dve.tensor_copy(vecT[:, V_CCTX:V_CCTX + 32], psum[4][:, V_CCTX:V_CCTX + 32]).then_inc(vec_ready, 1)
                dve.wait_ge(vec_tr, 2)
                for c0, c1 in ((0, 124), (128, 188)):
                    dve.tensor_copy(vecT[:, c0:c1], psum[4][:, c0:c1])
                dve.tensor_copy(vecT[:, V_BADA:V_CCTX], psum[4][:, V_BADA:V_CCTX]).then_inc(vec_ready, 1)
                dve.wait_ge(c_ready, 2)
                dve.wait_ge(vec_ready, 2)

                def first_tiles(pair):
                    dve.wait_ge(ada_done, 2 * pair + 2)
                    norm_coefs(0, 2 * pair, 2)
                    for k in (2 * pair, 2 * pair + 1):
                        scaled(0, k)
                    for k in (2 * pair, 2 * pair + 1):
                        modulated(0, k)

                for v in range(ADA_FIRST):
                    for q in range(U):
                        if start_on_dve(v, q):
                            ada_piece(U * v + q, q, v)
                        elif start_on_dve(v, q + 1):
                            if v:
                                ada_store(v - 1, t0=2 * ADA_START[v - 1])
                            wait_pe(dve, U * v + q)
                            ada_rows_out(v)
                        t = first_tile(v, q)
                        if t is not None:
                            dve.wait_ge(xt_tr, t + 1)
                            dve.tensor_copy(xT[:, t, :], psum[2 + t % 2][:, 0:TOK]).then_inc(xT_ready, 1)
                    if v == PAIR_AT:
                        dve.wait_ge(xT_ready, KT)
                        inverse_root("x0")
                    if v >= PAIR_AT:
                        first_tiles(v - PAIR_AT)
                ada_store(ADA_FIRST - 1, t0=2 * ADA_START[-1])
                first_tiles(KT // 2 - 1)
                ffn(0)
                dve.wait_ge(ada_done, UNIT_SSM)
                post_norm(0, "y1")
                pre_norm(1, "x1")

                def both(rows_of):
                    for d in range(2):
                        yield d, rows_of[d]

                def gate_part(m):
                    if m == 0:
                        wait_pe(dve, P_GATES + U - 1)
                        dve.wait_ge(cols_loaded, 16 * N_COLS)
                        dve.wait_ge(x_spilled, 16)
                        dve.tensor_scalar(r_u, psum[0][:, 0:TOK], gcol[:, 0:1], gcol[:, 1:2], ALU.add, ALU.mult).then_inc(gate_read, 1)
                        dve.tensor_scalar(r_li, psum[1][:, 0:TOK], gcol[:, 2:3], None, ALU.add).then_inc(gate_read, 1)
                        dve.wait_ge(gate_read, 2)
                        dve.scalar_tensor_tensor(out=r_t, in0=r_u, scalar=-1.0, in1=r_u, op0=ALU.mult, op1=ALU.max).then_inc(dve_row, 1)
                    if m == 1:
                        dve.wait_ge(act_row, 1)
                        dve.tensor_scalar(r_d, r_e, 1.0, None, ALU.add).then_inc(dve_row, 1)
                        dve.wait_ge(dve_row, 2)
                        link(dve.tensor_scalar(r_t, r_d, -1.0, None, ALU.add))
                        link(dve.tensor_scalar(r_q, r_t, 1e-30, None, ALU.max))
                        link(dve.reciprocal(r_cs, r_q))
                        link(dve.tensor_scalar(r_T4, r_t, 0.0, None, ALU.is_equal))
                    if m == 2:
                        dve.wait_ge(act_row, 3)
                        link(dve.tensor_tensor(r_q, r_lw, r_e, ALU.mult))
                        link(dve.tensor_tensor(r_t, r_q, r_cs, ALU.mult))
                        link(dve.tensor_tensor(r_q, r_T4, r_e, ALU.mult))
                        link(dve.tensor_tensor(r_lw, r_t, r_q, ALU.add))
                        link(dve.scalar_tensor_tensor(out=r_sp, in0=r_u, scalar=0.0, in1=r_lw, op0=ALU.max, op1=ALU.add))
                        link(dve.tensor_scalar(gcol[:, 4:5], gcol[:, 4:5], -1.0, None, ALU.mult))
                        link(dve.tensor_scalar(r_d, r_sp, gcol[:, 4:5], None, ALU.mult))
                        for d, (a, b) in both(SCAN):
                            for c in range(NCH):
                                t = run(d, c)
                                last = dve.tensor_tensor_scan(r_cs[a:b, t], ones[a:b, :], r_d[a:b, t], 0.0, ALU.mult, ALU.add)
                        link(last)
                        link(dve.tensor_tensor(r_Q, r_li, r_cs, ALU.subtract))
                        link(dve.tensor_copy(r_P, r_cs))
                    if m == 3:
                        for d in range(2):
                            a, b = (64 * d, 64 * d + 32)
                            for c in ((0, 1, 2), (0, 2, 1))[d]:
                                t = run(d, c)
                                init = 0.0 if c == 0 else gcol[a:b, 6 + c:7 + c]
                                link(dve.tensor_tensor_scan(r_t[a:b, t], r_Q[a:b, t], r_Q[a:b, t], init, ALU.max, ALU.max))
                                if c == (1, 2)[d]:
                                    e = last_of(d, c)
                                    link(dve.tensor_tensor(gcol[a:b, 9 - c:10 - c], r_cs[a:b, e:e + 1], r_t[a:b, e:e + 1], ALU.add))
                            link(dve.tensor_scalar(r_P[a:b, :], r_t[a:b, :], -1.0, None, ALU.mult))
                        for d, (a, b) in both(SCAN):
                            link(dve.tensor_copy(gcol[a:b, 9:12], r_P[a:b, last_of(d, 0):TOK:P]))
                        dve.tensor_tensor(r_li, r_P, r_cs, ALU.subtract).then_inc(dve_row, 1)
                    if m == 4:
                        dve.wait_ge(act_row, 4)
                        dve.wait_ge(dve_row, 3)
                        for d in range(2):
                            a, b = ROW_SS[d], ROW_SS[d] + 32
                            link(dve.tensor_tensor(r_W[a:b, :], r_W[a:b, :], r_sp[a:b, :], ALU.mult))
                            link(dve.tensor_copy(r_T4[a:b, :], r_sp[a:b, :]))
                        for d, (a, b) in both(SCAN):
                            e, e0 = last_of(d, (1, 2)[d]), last_of(d, 0)
                            link(dve.tensor_copy(gcol[a:b, 12:13], r_E[a:b, e:e + 1]))
                            link(dve.tensor_tensor(gcol[a:b, 13:14], r_cs[a:b, e0:e0 + 1], r_P[a:b, e0:e0 + 1], ALU.subtract))
                        dve.tensor_scalar(r_t[:, 0:P], idn[:, :], gcol[:, 12:13], None, ALU.mult).then_inc(gates_done, 1)

                def run(d, c):
                    if d == 0:
                        return slice(P * c, P * c + P)
                    return slice(P * c + P - 1, P * c - 1 if c else None, -1)

                def last_of(d, c):
                    return P * c + (0 if d else P - 1)

                def conv(n, f):
                    t = 2 * XBC_ORDER[n] + f
                    src, dst = psum[(0 if n % 2 else 2) + f], cv[:, f, :]

                    def tap(k):
                        return vecT[:, V_CONVW + k * XBC_T + t:V_CONVW + k * XBC_T + t + 1]

                    if n:
                        dve.wait_ge(conv_silu, 2 * n + f - 1)
                    link(dve.tensor_scalar(dst, src[:, 0:TOK], tap(CONV_K // 2), vecT[:, V_CONVB + t:V_CONVB + t + 1], ALU.mult, ALU.add))
                    for k in (0, 1, 3, 4):
                        s = k - CONV_K // 2
                        for t0, t1, width in ((0, TOK_P, TOK_P), (TOK_P, TOK, GRID_W)):
                            a, b = max(0, -s), width - max(0, s)
                            o = dst[:, t0:t1].rearrange("p (r w) -> p r w", w=width)[:, :, a:b]
                            x = src[:, t0:t1].rearrange("p (r w) -> p r w", w=width)[:, :, a + s:b + s]
                            last = dve.scalar_tensor_tensor(out=o, in0=x, scalar=tap(k), in1=o, op0=ALU.mult, op1=ALU.add)
                            if k == 4 and t0:
                                last.then_inc(conv_done, 1)
                            elif t0:
                                link(last)

                def to_tok(n):
                    for f in range(2):
                        m = 2 * TOK_UNITS.index(n) + f
                        dve.wait_ge(conv_tr, m + 1)
                        c0 = f * P if n == UNIT_B else 2 * P * XBC_ORDER[n] + f * P
                        dst = (bm_tok if n == UNIT_B else xs_tok)[:, :, c0:c0 + P]
                        dve.tensor_copy(dst, psum[4 + f][:, 0:TOK].rearrange("p (c n) -> p c n", c=NCH)).then_inc(tok_ready, 1)

                for p in range(P_GATES, P_SSM):
                    if p < P_SSM - AHEAD:
                        split(p)
                    j = p - P_XBC
                    if j >= 0 and j % U == U - 1:
                        n = j // U
                        wait_pe(dve, p)
                        for f in range(2):
                            conv(n, f)
                        if n - 1 in TOK_UNITS:
                            to_tok(n - 1)
                    if j in GATE_AT:
                        gate_part(GATE_AT[j])
                to_tok(XBC_T // 2 - 1)
                for kind in range(4):
                    dve.wait_ge(cols_tr, kind + 1)
                    dve.tensor_copy(cols[:, kind, :, :], psum[4 + kind][:, 0:TOK].rearrange("p (c r) -> p c r", c=NCH)).then_inc(cols_ready, 1)
                dve.wait_ge(dec_mm, 1)
                dve.tensor_copy(dbc[:, :], psum[2][:, 0:P]).then_inc(dec_ready, 1)
                for n in range(4):
                    d, half = divmod(n, 2)
                    dve.wait_ge(st_tr, n + 1)
                    dve.tensor_copy(ST[:, d, GRP_W * half:GRP_W * half + GRP_W], psum[half][:, :]).then_inc(st_ready, 1)

                dve.wait_ge(cols_ready, 4)
                dve.wait_ge(dec_ready, 1)
                dve.wait_ge(st_ready, 4)

                def by_head(v, n=8):
                    return v.unsqueeze(2).broadcast_to((P, n, SSM_P))

                def heads_of(v):
                    return v.rearrange("p (h q) -> p h q", q=SSM_P)

                for n, (g, c, d, step) in enumerate(SSM_STEPS):
                    carried, states = ssm_before(n)
                    r0 = ROW_SS[d] + 8 * g
                    mine = slice(GRP_W * g, GRP_W * g + GRP_W)
                    dve.wait_ge(ss_bc, n + 1)
                    if n:
                        dve.wait_ge(ss_y, n)
                    for h in range(8):
                        last = dve.scalar_tensor_tensor(out=seg[:, h, :], in0=psum[4 + h // 4][:, P * (h % 4):P * (h % 4) + P],
                                                        scalar=cols[:, C_Q, c, r0 + h:r0 + h + 1], in1=maskneg[:, d, :],
                                                        op0=ALU.add, op1=ALU.add)
                    last.then_inc(ss_seg, 1)
                    if n:
                        ada_store(UNIT_SSM + n - 1)
                    dve.wait_ge(ss_exp, n + 1)
                    dve.wait_ge(ss_cb, n + 1)
                    dve.tensor_tensor(seg[:, 0:4, :], seg[:, 0:4, :], cbs.unsqueeze(1).broadcast_to((P, 4, P)), ALU.mult).then_inc(ss_wd, 1)
                    ada_piece(P_SSM + U * n + U - 1, U - 1, UNIT_SSM + n)
                    dve.wait_ge(ss_y, n + 1)
                    dve.wait_ge(ss_x, n + 1)
                    if carried:
                        dve.wait_ge(ss_ypool, carried)
                    if n:
                        dve.wait_ge(ss_yacc, n)
                    dve.tensor_tensor(yacc[:, c, mine], yacc[:, c, mine], psum[7][:, :], ALU.add).then_inc(ss_yacc, 1)
                    ada_rows_out(UNIT_SSM + n)
                    if c:
                        dve.wait_ge(ss_int, carried + 1)
                        dve.tensor_tensor(heads_of(ytmp), heads_of(psum[6][:, :]), by_head(cols[:, C_E, c, r0:r0 + 8]),
                                          ALU.mult).then_inc(ss_tmp, 1)
                    if step < N_STATE:
                        if c:
                            link(dve.tensor_tensor(heads_of(stt_), heads_of(ST[:, d, mine]), by_head(dbc[:, r0:r0 + 8]), ALU.mult))
                            dve.wait_ge(ss_stm, states + 1)
                            dve.tensor_tensor(ST[:, d, mine], stt_, psum[6][:, :], ALU.add).then_inc(ss_state, 1)
                        else:
                            dve.wait_ge(ss_stm, states + 1)
                            stored = 2 * g + step
                            if stored:
                                dve.wait_ge(s_stored, 16 * stored)
                            dve.tensor_copy(s_out, psum[6][:, :]).then_inc(ss_state, 1)
                ada_store(ADA_T // 2 - 1)
                for p in range(P_SSM - AHEAD, P_SSM):
                    split(p)
                dve.wait_ge(ada_done, ADA_T // 2)
                for t in range(KT // 2):
                    dve.wait_ge(yt_tr, t + 1)
                    dve.tensor_copy(y[:, KT // 2 + t, :], psum[4 + t % 2][:, 0:TOK]).then_inc(yt_ready, 1)
                dve.wait_ge(yt_ready, KT // 2)

                with dve.Fori(0, HEADS // 2) as i:
                    own.enter(i, LINKS_PAIR)

                    def kv(hh):
                        ktok, va = hset[hh][3:5]
                        for n, dst in enumerate((ktok, va)):
                            for f in range(2):
                                dve.wait_ge(kv_tr, at(4 * hh + 2 * n + f + 1, i, 8))
                                dve.tensor_copy(dst[:, :, f * P:f * P + P], psum[4 + f][:, 0:TOK].rearrange("p (c n) -> p c n", c=NCH)).then_inc(kv_tok, 1)

                    def start(hh):
                        for d in range(2):
                            row = i * 2 + (ROW_ML[d] + hh)
                            dve.tensor_scalar(mrow[:, d, :], r_P, idn[:, bass.ds(row, 1)], None, ALU.mult).then_inc(row_ready, 1)

                    def a(hh, n):
                        c, d = STEPS[n]
                        row = i * 2 + (ROW_ML[d] + hh)
                        if n == 0:
                            dve.wait_ge(m_bc, at(hh + 1, i, 2))
                        else:
                            dve.wait_ge(m_s, at(6 * hh + n, i, 12))
                        dve.scalar_tensor_tensor(out=ex, in0=psum[4 + d][:, P * c:P * c + P], scalar=cols[:, C_Q, c, bass.ds(row, 1)],
                                                 in1=maskneg[:, d, :], op0=ALU.add, op1=ALU.add).then_inc(m_seg, 1)
                        dve.wait_ge(m_exp, at(6 * hh + n + 1, i, 12))
                        dve.wait_ge(m_qk, at(6 * hh + n + 1, i, 12))
                        dve.tensor_tensor(sT, ex, psum[6][:, 0:P], ALU.mult).then_inc(m_s, 1)

                    def b(hh, n):
                        c, d = STEPS[n]
                        row = i * 2 + (ROW_ML[d] + hh)
                        dve.wait_ge(m_num, at(6 * hh + n + 1, i, 12))
                        if c:
                            dve.wait_ge(m_ti, at(4 * hh + n - 1, i, 8))
                            link(dve.tensor_tensor(num, ti, psum[7][:, 0:VW], ALU.add))
                        else:
                            link(dve.tensor_copy(num, psum[7][:, 0:VW]))
                        link(dve.tensor_scalar(small[:, 2:3], num[:, DH:VW], -1.0, cols[:, C_T, c, bass.ds(row, 1)], ALU.mult, ALU.max))
                        link(dve.tensor_tensor(small[:, 0:1], num[:, DH:VW], small[:, 2:3], ALU.max))
                        link(dve.reciprocal(small[:, 1:2], small[:, 0:1]))
                        if n == 0 and hh:
                            dve.wait_ge(h_tr, at(1, i, 2))
                        if n in FIRST_VISIT:
                            dve.tensor_scalar(hacc[:, c, :], num[:, 0:DH], small[:, 1:2], None, ALU.mult).then_inc(m_h, 1)
                        else:
                            dve.scalar_tensor_tensor(out=hacc[:, c, :], in0=num[:, 0:DH], scalar=small[:, 1:2], in1=hacc[:, c, :],
                                                     op0=ALU.mult, op1=ALU.add).then_inc(m_h, 1)
                        dve.wait_ge(m_h, at(6 * hh + n + 1, i, 12))

                    def c_(hh, n):
                        c, d = STEPS[n]
                        row = i * 2 + (ROW_ML[d] + hh)
                        dve.wait_ge(m_upd, at(N_STATE * hh + n + 1, i, 8))
                        if n == 2:
                            dve.wait_ge(c_loaded[hh], at(64, i, 64))
                        for k in range(2):
                            if c:
                                last = dve.scalar_tensor_tensor(out=cst[hh][:, d, k, :], in0=cst[hh][:, d, k, :], scalar=dbc[:, bass.ds(row, 1)],
                                                                in1=psum[7 - k][:, 0:VW], op0=ALU.mult, op1=ALU.add)
                            else:
                                last = dve.tensor_copy(c_out[:, k, :], psum[7 - k][:, 0:VW])
                        last.then_inc(m_c, 1)

                    def end(hh):
                        for c in range(NCH):
                            last = dve.bn_stats(stats[:, c, :], hacc[:, c, :])
                        link(last)
                        dve.tensor_copy(small[:, 3:4], stats[:, 2, 0:1])
                        for c in range(NCH):
                            last = dve.bn_aggr(small[:, 12 + 2 * c:14 + 2 * c], stats[:, c, :])
                        link(last)
                        dve.tensor_copy(small[:, 20:23], small[:, 13:18:2]).then_inc(h_var, 1)
                        dve.wait_ge(h_std, at(hh + 1, i, 2))
                        link(dve.reciprocal(small[:, 28:31], small[:, 24:27]))
                        for c in range(NCH):
                            dve.tensor_scalar(hacc[:, c, :], hacc[:, c, :], small[:, 12 + 2 * c:13 + 2 * c], small[:, 28 + c:29 + c],
                                              ALU.subtract, ALU.mult).then_inc(h_norm, 1)
                        dve.wait_ge(h_tr, at(hh + 1, i, 2))
                        dve.wait_ge(og_ready, at(2 * hh + 2, i, 4))
                        for k in range(2):
                            t = i * 4 + (2 * hh + k)
                            dve.scalar_tensor_tensor(out=y[:, bass.ds(t, 1), :].rearrange("p a t -> p (a t)"), in0=psum[4 + k][:, 0:TOK],
                                                     scalar=vecT[:, bass.ds(t + V_MLG, 1)], in1=sigo[hh][:, k, :], op0=ALU.mult,
                                                     op1=ALU.mult).then_inc(mix_ready, 1)

                    tasks = {"kv": kv, "start": start, "end": end, "a": a, "b": b, "c": c_}
                    for j, (col, hh, q) in enumerate(PAIR_ORDER):
                        split(P_HEADS + j, i, PAIR)
                        if q == U - 1:
                            b0 = 2 * ((j // U) % 2)
                            if col in (COL_Q, COL_K, COL_V):
                                dst = hset[hh][(COL_Q, COL_K, COL_V).index(col)]
                                wait_pe(dve, P_HEADS + j, i, PAIR)
                                for f in range(2):
                                    if col == COL_K:
                                        dve.tensor_scalar(dst[:, f, :], psum[b0 + f][:, 0:TOK], DH ** -0.5, None, ALU.mult).then_inc(qkv_ready, 1)
                                    else:
                                        dve.tensor_copy(dst[:, f, :], psum[b0 + f][:, 0:TOK]).then_inc(qkv_ready, 1)
                            elif col == COL_Z:
                                for f in range(2):
                                    dve.wait_ge(z_silu, at(2 * hh + f + 1, i, 4))
                                    t = i * 4 + (KT // 2 + 2 * hh + f)
                                    tile = y[:, bass.ds(t, 1), :].rearrange("p a t -> p (a t)")
                                    dve.tensor_tensor(tile, tile, psum[b0 + f][:, 0:TOK], ALU.mult).then_inc(z_done, 1)
                        for kind, thh, n in core_tasks(j):
                            tasks[kind](thh) if n is None else tasks[kind](thh, n)
                own.leave(HEADS // 2)

                dve.wait_ge(z_done, 2 * HEADS)
                inverse_root("ssm")
                for k in range(KT // 2, KT):
                    g = vecT[:, V_SSG + k - KT // 2:V_SSG + k - KT // 2 + 1]
                    dve.scalar_tensor_tensor(out=y[:, k, :], in0=y[:, k, :], scalar=g, in1=ROOT_BANK[:, 0:TOK],
                                             op0=ALU.mult, op1=ALU.mult).then_inc(ms_scaled, 1)
                for t in range(D // PC):
                    for q in range(U):
                        split(P_OUT + U * t + q)
                    wait_pe(dve, P_OUT + U * t + U - 1)
                    for f in range(2):
                        dve.tensor_copy(y[:, 2 * t + f, :], psum[(4 if t % 2 else 2) + f][:, 0:TOK]).then_inc(y_done, 1)
                dve.wait_ge(y_done, KT * (FFN_IT + 1))
                post_norm(1, "y2")
                pre_norm(2, "x2")
                ffn(1)
                dve.wait_ge(y_done, KT * (2 * FFN_IT + 1))
                post_norm(2, "y3")
                for n in range(0, NCH * (KT // 4), 2):
                    kk, c = divmod(n, NCH)
                    dve.wait_ge(out_tr, n + 1)
                    dve.tensor_copy(out_tok[:, c, 512 * kk:512 * kk + 512], psum[2 + n % 2][:, :]).then_inc(out_ready_dve, 1)

            @block.gpsimd
            def _(pool):
                own = Tally(pool, pool_step)
                link = own.link

                def split(p, i=None, per=0):
                    p = ahead(p)
                    if p is not None and pool_splits(p):
                        make_lo(p, i, per)

                def make_lo(p, i=None, per=0):
                    pool.wait_ge(w_hi_ready, of_piece(N_HI, p, i, per))
                    pool.tensor_tensor(w_lo[:, slot(p), :], w_raw[:, p % NR, :], w_hi[:, slot(p), :].bitcast(F32),
                                       ALU.subtract).then_inc(w_lo_pool, 1)

                def lo_of(done, src, tiles=range(KT)):
                    for k in tiles:
                        pool.wait_ge(xn_hi_ready, done + k + 1)
                        pool.tensor_tensor(xn_lo[:, k, :], src(k), xn_hi[:, k, :].bitcast(F32), ALU.subtract).then_inc(xn_lo_ready, 1)

                def update(stage):
                    for k in range(KT):
                        pool.wait_ge(u_ready, KT * stage + k + 1)
                        pool.tensor_tensor(xT[:, k, :], xT[:, k, :], y[:, k, :], ALU.add).then_inc(x_updated, 1)

                def ffn(n):
                    def hid_lo_part(it, s, i):
                        for f in range(2):
                            m = 4 * (FFN_IT * n + it) + 2 * s + f
                            pool.wait_ge(hid_hi_ready, at(m + 1, i, 4))
                            pool.tensor_tensor(hid_lo[:, 2 * s + f, :], hidf[:, f, :], hid_hi[:, 2 * s + f, :].bitcast(F32),
                                               ALU.subtract).then_inc(hid_lo_ready, 1)

                    def step(i):
                        per, pieces = step_of(n, i)
                        for p, kind, s, q in pieces:
                            if kind != "a":
                                split(p, i, per)
                            if kind == "u" and q == U - 1:
                                hid_lo_part(0 if i is None else 1, s, i)

                    step(None)
                    with pool.Fori(0, FFN_IT - 1) as i:
                        step(i)
                    for j in range(DOWN):
                        split(tail_of(n) + j)

                def pad_gates():
                    pool.wait_ge(gw_loaded, 32)
                    link(pool.memset(gw_pad[:, :, :], 0.0))
                    for dst, src, n in ((ROW_ML[0], 2 * HEADS, HEADS), (ROW_ML[1], 3 * HEADS, HEADS),
                                        (ROW_SS[0], 4 * HEADS, SSM_H), (ROW_SS[1], 4 * HEADS + SSM_H, SSM_H),
                                        (P + ROW_ML[0], 0, HEADS), (P + ROW_ML[1], HEADS, HEADS)):
                        last = pool.tensor_copy(gw_pad[:, :, dst:dst + n], gw_small[:, :, src:src + n])
                    last.then_inc(gw_ready, 1)

                link(pool.memset(idn[:, :], 0.0))
                link(pool.affine_select(out=idn[:, :], in_=idn[:, :], compare_op=ALU.not_equal, fill=1.0, base=0,
                                        pattern=[[-1, P]], channel_multiplier=1))
                link(pool.memset(ada_row[:, :], 0.0))
                link(pool.memset(ones[:, :], 1.0))
                link(pool.memset(gcol[:, :], 0.0))
                link(pool.memset(gcol[:, 1:2], 1.0))
                link(pool.memset(gcol[0:32, 1:2], -1.0))
                link(pool.memset(gcol[64:96, 1:2], -1.0))
                link(pool.memset(maskneg[:, :, :], 0.0))
                for d in range(2):
                    sign = -1 if d else 1
                    link(pool.affine_select(out=maskneg[:, d, :], in_=maskneg[:, d, :], compare_op=ALU.is_ge, fill=MASKED, base=0,
                                            pattern=[[sign, P]], channel_multiplier=-sign))
                pool.memset(eps[:, :], EPS).then_inc(const_ready, 1)
                pad_gates()
                early = 2 * (ADA_FIRST - 1 - PAIR_AT)
                lo_of(0, lambda k: hn[:, k % 2, :], range(early))
                for p in MAIN[:AHEAD]:
                    make_lo(p)
                lo_of(0, lambda k: hn[:, k % 2, :], range(early, KT))
                pool.wait_ge(xt_tr, KT)
                pool.memset(y[:, :, :], 0.0).then_inc(y_zeroed, 1)
                ffn(0)
                update(0)
                lo_of(KT, lambda k: hn[:, k % 2, :])
                for p in range(P_GATES, P_SSM):
                    if p < P_SSM - AHEAD:
                        split(p)
                pool.wait_ge(cols_ready, 4)
                pool.wait_ge(tok_ready, 2 * len(TOK_UNITS))
                pool.wait_ge(cols_loaded, 16 * N_COLS)

                def by_head(v):
                    return v.unsqueeze(2).broadcast_to((P, 8, SSM_P))

                def heads_of(v):
                    return v.rearrange("p (h q) -> p h q", q=SSM_P)

                for n, (g, c, d, step) in enumerate(SSM_STEPS):
                    carried, states = ssm_before(n)
                    r0 = ROW_SS[d] + 8 * g
                    mine = slice(GRP_W * g, GRP_W * g + GRP_W)
                    x = heads_of(xs_tok[:, c, mine])
                    if n:
                        pool.wait_ge(ss_y, n)
                        if states:
                            pool.wait_ge(ss_stm, states)
                    last = pool.tensor_tensor(heads_of(xdt), x, by_head(cols[:, C_T, c, r0:r0 + 8]), ALU.mult)
                    if step < N_STATE:
                        last = pool.tensor_tensor(heads_of(xte), x, by_head(cols[:, C_W, c, r0:r0 + 8]), ALU.mult)
                    if step in FIRST_VISIT:
                        last = pool.tensor_tensor(heads_of(yacc[:, c, mine]), x, by_head(dsk[:, 8 * g:8 * g + 8]), ALU.mult)
                    last.then_inc(ss_x, 1)
                    pool.wait_ge(ss_exp, n + 1)
                    pool.wait_ge(ss_cb, n + 1)
                    pool.tensor_tensor(seg[:, 4:8, :], seg[:, 4:8, :], cbs.unsqueeze(1).broadcast_to((P, 4, P)), ALU.mult).then_inc(ss_wp, 1)
                    if c:
                        pool.wait_ge(ss_tmp, carried + 1)
                        pool.wait_ge(ss_yacc, n + 1)
                        pool.tensor_tensor(yacc[:, c, mine], yacc[:, c, mine], ytmp, ALU.add).then_inc(ss_ypool, 1)

                for p in range(P_SSM - AHEAD, P_SSM):
                    split(p)
                pool.wait_ge(ss_stm, ssm_before(len(SSM_STEPS))[1])
                for head in hset:
                    last = pool.memset(head[4][:, :, DH:VW], 1.0)
                last.then_inc(v_ones, 1)

                with pool.Fori(0, HEADS // 2) as i:
                    for j, (col, hh_, q) in enumerate(PAIR_ORDER):
                        split(P_HEADS + j, i, PAIR)
                        for kind, hh, n in core_tasks(j):
                            ktok, va = hset[hh][3:5]
                            if kind == "a" and n < N_STATE:
                                c, d = STEPS[n]
                                row = i * 2 + (ROW_ML[d] + hh)
                                if n == 0:
                                    pool.wait_ge(kv_tok, at(4 * hh + 4, i, 8))
                                if n or hh:
                                    pool.wait_ge(m_upd, at(N_STATE * hh + n, i, 8))
                                pool.tensor_tensor(wk, ktok[:, c, :], cols[:, C_W, c, bass.ds(row, 1)].broadcast_to((P, DH)),
                                                   ALU.mult).then_inc(m_wk, 1)
                lo_of(2 * KT, lambda k: y[:, k, :])
                for p in range(P_OUT, FFN2):
                    split(p)
                pool.wait_ge(x_back, 16)
                update(1)
                pool.wait_ge(x_updated, 2 * KT)
                pool.memset(y[:, :, :], 0.0).then_inc(y_zeroed, 1)
                lo_of(3 * KT, lambda k: hn[:, k % 2, :])
                ffn(1)
                update(2)


_INS = ['x_prompt', 'x_sample', 'state_mlstm_C', 'state_mlstm_n', 'state_mlstm_m', 'state_ssm', 'c', 'c_ctx', 'w_ada', 'b_ada',
        'norm_g', 'w_in', 'gate_bias', 'dt_bias', 'a_log', 'd_skip', 'conv_w', 'conv_b', 'ml_norm_g', 'ssm_norm_g', 'w_out',
        'ffn_w_gate', 'ffn_w_up', 'ffn_w_down']
_OUTS = [('y_prompt', (1, TOK_P, D)), ('y_sample', (1, TOK_S, D)), ('new_C', (1, 1, 2, HEADS, DH, DH)), ('new_n', (1, 1, 2, HEADS, DH)),
         ('new_m', (1, 1, 2, HEADS)), ('new_ssm', (1, 1, 2, SSM_H, SSM_P, SSM_N))]


def kernel(**inputs):
    import numpy as _np
    import concourse.bacc as _bacc
    from concourse.bass_utils import run_bass_kernel_spmd as _run

    nc = _bacc.Bacc("TRN2", target_bir_lowering=False, num_devices=1, dynamic_dma_scratch_size=1024)
    arrays, args = {}, {}
    for name in _INS:
        a = _np.ascontiguousarray(inputs[name])
        arrays[f"in_{name}_dram"] = a
        args[name] = nc.dram_tensor(f"in_{name}_dram", a.shape, mybir.dt.from_np(a.dtype), kind="ExternalInput").ap()
    for name, shape in _OUTS:
        args[name] = nc.dram_tensor(f"out_{name}_dram", shape, F32, kind="ExternalOutput").ap()
    hybrid_step(nc, args)
    r = _run(nc, [arrays], core_ids=[0])
    return tuple(r.results[0][f"out_{name}_dram"] for name, _ in _OUTS)
```
